# Optimizing a Trainium2 kernel written in Bass

```python
import math
import jax, jax.numpy as jnp
from jax import lax
import numpy as np

D_MODEL = 1024
BATCH = 1
SEQ = 128
DEPTH = 2
DEC_BATCH = 1
DEC_SEQ = 512
PAST_LEN = 128

GRID_W = 64
CHUNK = 128
N_MIXERS = 2
N_A = (DEPTH + 1) // 2
N_B = DEPTH // 2
A_HEADS = 4
A_DV = D_MODEL // A_HEADS
A_DK = A_DV // 2
A_IN = 2 * A_HEADS * A_DK + 2 * A_HEADS * A_DV + 4 * A_HEADS
A_FBIAS_LO = 3.0
A_FBIAS_HI = 6.0
B_HEADS = 8
B_DK = D_MODEL // B_HEADS
B_DV = 2 * D_MODEL // B_HEADS
B_IN = 2 * B_HEADS * B_DK + 2 * B_HEADS * B_DV
B_DECAY_BASE = 5.0
ROPE_BASE = 10000.0
D_FF = ((8 * D_MODEL // 3 + 127) // 128) * 128
CONV_W = 3
EPS = 1e-6

kernel_name = 'hybrid_mlstm_retention_diffusion_step'

F32 = jnp.float32

def rmsnorm(x, g):
    xf = x.astype(F32)
    y = xf * lax.rsqrt(jnp.mean(xf * xf, axis=-1, keepdims=True) + EPS)
    return (y * g.astype(F32)).astype(x.dtype)

def head_norm(h, g):
    mu = jnp.mean(h, axis=-1, keepdims=True)
    var = jnp.mean(jnp.square(h - mu), axis=-1, keepdims=True)
    return (h - mu) * lax.rsqrt(var + EPS) * g.astype(F32)

def modulation(cond, w, b):
    mod = jax.nn.silu(cond) @ w + b
    return [m[:, None, :] for m in jnp.split(mod, 6, axis=-1)]

def flip_t(a):
    return jnp.flip(a, axis=2)

def to_chunks(a):
    nc = a.shape[2] // CHUNK
    a = a.reshape(a.shape[:2] + (nc, CHUNK) + a.shape[3:])
    return jnp.moveaxis(a, 2, 0)

def from_chunks(a):
    a = jnp.moveaxis(a, 0, 2)
    return a.reshape(a.shape[:2] + (a.shape[2] * a.shape[3],) + a.shape[4:])

def mlstm_scan(q, k, v, ig, lf, C0, n0, m0):
    causal = jnp.tril(jnp.ones((CHUNK, CHUNK), bool))

    def step(carry, xs):
        C, n, m = carry
        qj, kj, vj, ij, fj = xs
        a = jnp.cumsum(fj, axis=-1)
        g = a[..., -1]
        dmat = jnp.where(causal, a[..., :, None] - a[..., None, :] + ij[..., None, :], -jnp.inf)
        inter = m[..., None] + a
        m_q = jnp.maximum(inter, jnp.max(dmat, axis=-1))
        w_intra = jnp.exp(dmat - m_q[..., None])
        w_inter = jnp.exp(inter - m_q)
        s = jnp.einsum('bhld,bhsd->bhls', qj, kj) * w_intra
        num = jnp.einsum('bhls,bhsv->bhlv', s, vj) + w_inter[..., None] * jnp.einsum('bhld,bhdv->bhlv', qj, C)
        den = jnp.sum(s, axis=-1) + w_inter * jnp.einsum('bhld,bhd->bhl', qj, n)
        h = num / jnp.maximum(jnp.abs(den), jnp.exp(-m_q))[..., None]
        w_s = g[..., None] - a + ij
        m_new = jnp.maximum(m + g, jnp.max(w_s, axis=-1))
        ws = jnp.exp(w_s - m_new[..., None])
        dec = jnp.exp(m + g - m_new)
        kw = kj * ws[..., None]
        C_new = dec[..., None, None] * C + jnp.einsum('bhsd,bhsv->bhdv', kw, vj)
        n_new = dec[..., None] * n + jnp.sum(kw, axis=2)
        return (C_new, n_new, m_new), h

    xs = (to_chunks(q), to_chunks(k), to_chunks(v), to_chunks(ig), to_chunks(lf))
    (C, n, m), hs = lax.scan(step, (C0, n0, m0), xs)
    return from_chunks(hs), C, n, m

def mlstm_mixer(u, w_in, b_gate, g_norm, w_out, C0, n0, m0):
    B, T, _ = u.shape
    z = jnp.einsum('btd,de->bte', u, w_in).astype(F32)
    hk, hv = A_HEADS * A_DK, A_HEADS * A_DV
    q, k, v, o, gates = jnp.split(z, [hk, 2 * hk, 2 * hk + hv, 2 * hk + 2 * hv], axis=-1)
    q = q.reshape(B, T, A_HEADS, A_DK).transpose(0, 2, 1, 3)
    k = (k * (A_DK ** -0.5)).reshape(B, T, A_HEADS, A_DK).transpose(0, 2, 1, 3)
    v = v.reshape(B, T, A_HEADS, A_DV).transpose(0, 2, 1, 3)
    gates = (gates.reshape(B, T, 4, A_HEADS) + b_gate.astype(F32)).transpose(2, 0, 3, 1)
    ig_f, lf_f = gates[0], jax.nn.log_sigmoid(gates[1])
    ig_b, lf_b = gates[2], jax.nn.log_sigmoid(gates[3])
    C0, n0, m0 = C0.astype(F32), n0.astype(F32), m0.astype(F32)
    h_f, Cf, nf, mf = mlstm_scan(q, k, v, ig_f, lf_f, C0[:, 0], n0[:, 0], m0[:, 0])
    h_b, Cb, nb, mb = mlstm_scan(flip_t(q), flip_t(k), flip_t(v), flip_t(ig_b), flip_t(lf_b),
                                 C0[:, 1], n0[:, 1], m0[:, 1])
    h = head_norm((h_f + flip_t(h_b)).transpose(0, 2, 1, 3), g_norm)
    h = h.reshape(B, T, hv) * jax.nn.sigmoid(o)
    y = h.astype(u.dtype) @ w_out
    return y, jnp.stack([Cf, Cb], 1), jnp.stack([nf, nb], 1), jnp.stack([mf, mb], 1)

def axial_rope(x, rows, cols):
    half = x.shape[-1] // 2
    quarter = half // 2
    inv = ROPE_BASE ** (-jnp.arange(quarter, dtype=F32) / quarter)

    def rot(xp, pos):
        ang = pos.astype(F32)[:, None] * inv
        cos, sin = jnp.cos(ang)[:, None, :], jnp.sin(ang)[:, None, :]
        x1, x2 = xp[..., :quarter], xp[..., quarter:]
        return jnp.concatenate([x1 * cos - x2 * sin, x1 * sin + x2 * cos], axis=-1)

    return jnp.concatenate([rot(x[..., :half], rows), rot(x[..., half:], cols)], axis=-1)

def retention_scan(q, k, v, log_gamma, S0):
    idx = jnp.arange(CHUNK, dtype=F32)
    lg = log_gamma[:, None]
    tri = jnp.tril(jnp.ones((CHUNK, CHUNK), bool))
    diff = jnp.where(tri, idx[:, None] - idx[None, :], 0.0)
    decay_mat = jnp.where(tri, jnp.exp(diff[None] * lg[..., None]), 0.0)
    xi = jnp.exp((idx + 1.0) * lg)
    zeta = jnp.exp((CHUNK - 1.0 - idx) * lg)
    chunk_decay = jnp.exp(CHUNK * log_gamma)

    def step(S, xs):
        qj, kj, vj = xs
        s = jnp.einsum('bhld,bhsd->bhls', qj, kj) * decay_mat
        o = jnp.einsum('bhls,bhsv->bhlv', s, vj) + xi[..., None] * jnp.einsum('bhld,bhdv->bhlv', qj, S)
        S_new = chunk_decay[:, None, None] * S + jnp.einsum('bhsd,bhsv->bhdv', kj * zeta[..., None], vj)
        return S_new, o

    S, hs = lax.scan(step, S0, (to_chunks(q), to_chunks(k), to_chunks(v)))
    return from_chunks(hs), S

def retention_mixer(u, w_in, decay_exp, g_norm, w_out, S0, grid):
    B, T, _ = u.shape
    z = jnp.einsum('btd,de->bte', u, w_in).astype(F32)
    hk, hv = B_HEADS * B_DK, B_HEADS * B_DV
    q, k, v, gate = jnp.split(z, [hk, 2 * hk, 2 * hk + hv], axis=-1)
    q = q.reshape(B, T, B_HEADS, B_DK)
    k = (k * (B_DK ** -0.5)).reshape(B, T, B_HEADS, B_DK)
    if grid is not None:
        q = axial_rope(q, grid[0], grid[1])
        k = axial_rope(k, grid[0], grid[1])
    q, k = q.transpose(0, 2, 1, 3), k.transpose(0, 2, 1, 3)
    v = v.reshape(B, T, B_HEADS, B_DV).transpose(0, 2, 1, 3)
    log_gamma = jnp.log1p(-jnp.exp2(-decay_exp.astype(F32)))
    S0 = S0.astype(F32)
    h_f, S_f = retention_scan(q, k, v, log_gamma[0], S0[:, 0])
    h_b, S_b = retention_scan(flip_t(q), flip_t(k), flip_t(v), log_gamma[1], S0[:, 1])
    h = head_norm((h_f + flip_t(h_b)).transpose(0, 2, 1, 3), g_norm).reshape(B, T, hv)
    h = h * jax.nn.silu(gate)
    return h.astype(u.dtype) @ w_out, jnp.stack([S_f, S_b], 1)

def dwconv3(h, w, b):
    L = h.shape[-2]
    hp = jnp.pad(h, [(0, 0)] * (h.ndim - 2) + [(1, 1), (0, 0)])
    return hp[..., 0:L, :] * w[0] + hp[..., 1:L + 1, :] * w[1] + hp[..., 2:L + 2, :] * w[2] + b

def conv_ffn(u, w_up, conv_w, conv_b, w_down, grid):
    B, T, _ = u.shape
    h = u @ w_up
    if grid is None:
        h = dwconv3(h, conv_w, conv_b)
    else:
        n_rows = grid[2]
        h = dwconv3(h.reshape(B, n_rows, GRID_W, 2 * D_FF), conv_w, conv_b).reshape(B, T, 2 * D_FF)
    g, up = jnp.split(h, 2, axis=-1)
    return (jax.nn.gelu(g, approximate=True) * up) @ w_down

def trunk(x, cond, grid, st_C, st_n, st_m, st_S, norm_gain, ada_w, ada_b,
          ml_w_in, ml_b_gate, ml_norm, ml_w_out, ret_w_in, ret_decay, ret_norm, ret_w_out,
          ffn_w_up, ffn_conv, ffn_conv_b, ffn_w_down):
    Cs, ns, ms, Ss = [], [], [], []
    for i in range(DEPTH):
        sh1, sc1, g1, sh2, sc2, g2 = modulation(cond, ada_w[i], ada_b[i])
        u = rmsnorm(x, norm_gain[i, 0]) * (1 + sc1) + sh1
        j = i // N_MIXERS
        if i % N_MIXERS == 0:
            y, C, n, m = mlstm_mixer(u, ml_w_in[j], ml_b_gate[j], ml_norm[j], ml_w_out[j],
                                     st_C[:, j], st_n[:, j], st_m[:, j])
            Cs.append(C)
            ns.append(n)
            ms.append(m)
        else:
            y, S = retention_mixer(u, ret_w_in[j], ret_decay[j], ret_norm[j], ret_w_out[j], st_S[:, j], grid)
            Ss.append(S)
        x = x + g1 * rmsnorm(y, norm_gain[i, 1])
        u = rmsnorm(x, norm_gain[i, 2]) * (1 + sc2) + sh2
        f = conv_ffn(u, ffn_w_up[i], ffn_conv[i], ffn_conv_b[i], ffn_w_down[i], grid)
        x = x + g2 * rmsnorm(f, norm_gain[i, 3])
    return x, Cs, ns, ms, Ss

def setup_inputs(seed: int = 0) -> dict:
    key = jax.random.key(seed)
    ks = jax.random.split(key, 32)
    nrm = lambda k, shape, s: jax.random.normal(k, shape, F32) * s
    f_bias = jnp.linspace(A_FBIAS_LO, A_FBIAS_HI, A_HEADS, dtype=F32)
    b_gate = nrm(ks[10], (N_A, 4, A_HEADS), 0.1)
    b_gate = b_gate.at[:, 1].add(f_bias).at[:, 3].add(f_bias)
    decay = B_DECAY_BASE + jnp.arange(B_HEADS, dtype=F32) + nrm(ks[14], (N_B, 2, B_HEADS), 0.1)
    return {
        'x_prompt': nrm(ks[0], (BATCH, SEQ, D_MODEL), 1.0),
        'x_sample': nrm(ks[1], (DEC_BATCH, DEC_SEQ, D_MODEL), 1.0),
        'state_mlstm_C': nrm(ks[2], (DEC_BATCH, N_A, 2, A_HEADS, A_DK, A_DV), 0.5),
        'state_mlstm_n': nrm(ks[3], (DEC_BATCH, N_A, 2, A_HEADS, A_DK), 0.5),
        'state_mlstm_m': nrm(ks[4], (DEC_BATCH, N_A, 2, A_HEADS), 1.0),
        'state_ret_S': nrm(ks[5], (DEC_BATCH, N_B, 2, B_HEADS, B_DK, B_DV), 1.0),
        'c': nrm(ks[6], (DEC_BATCH, D_MODEL), 1.0),
        'c_ctx': nrm(ks[7], (D_MODEL,), 1.0),
        'norm_gain': 1.0 + nrm(ks[8], (DEPTH, 4, D_MODEL), 0.02),
        'ada_w': nrm(ks[9], (DEPTH, D_MODEL, 6 * D_MODEL), 0.5 * D_MODEL ** -0.5),
        'ada_b': nrm(ks[11], (DEPTH, 6 * D_MODEL), 0.1),
        'ml_w_in': nrm(ks[12], (N_A, D_MODEL, A_IN), D_MODEL ** -0.5),
        'ml_b_gate': b_gate,
        'ml_norm': 1.0 + nrm(ks[13], (N_A, A_HEADS, A_DV), 0.02),
        'ml_w_out': nrm(ks[15], (N_A, A_HEADS * A_DV, D_MODEL), (A_HEADS * A_DV) ** -0.5),
        'ret_w_in': nrm(ks[16], (N_B, D_MODEL, B_IN), D_MODEL ** -0.5),
        'ret_decay': decay,
        'ret_norm': 1.0 + nrm(ks[17], (N_B, B_HEADS, B_DV), 0.02),
        'ret_w_out': nrm(ks[18], (N_B, B_HEADS * B_DV, D_MODEL), (B_HEADS * B_DV) ** -0.5),
        'ffn_w_up': nrm(ks[19], (DEPTH, D_MODEL, 2 * D_FF), D_MODEL ** -0.5),
        'ffn_conv': nrm(ks[20], (DEPTH, CONV_W, 2 * D_FF), 0.5),
        'ffn_conv_b': nrm(ks[21], (DEPTH, 2 * D_FF), 0.02),
        'ffn_w_down': nrm(ks[22], (DEPTH, D_FF, D_MODEL), D_FF ** -0.5),
    }

def reference(x_prompt, x_sample, state_mlstm_C, state_mlstm_n, state_mlstm_m, state_ret_S, c, c_ctx,
              norm_gain, ada_w, ada_b, ml_w_in, ml_b_gate, ml_norm, ml_w_out,
              ret_w_in, ret_decay, ret_norm, ret_w_out, ffn_w_up, ffn_conv, ffn_conv_b, ffn_w_down):
    weights = (norm_gain, ada_w, ada_b, ml_w_in, ml_b_gate, ml_norm, ml_w_out,
               ret_w_in, ret_decay, ret_norm, ret_w_out, ffn_w_up, ffn_conv, ffn_conv_b, ffn_w_down)
    Bp = x_prompt.shape[0]
    z_C = jnp.zeros((Bp, N_A, 2, A_HEADS, A_DK, A_DV), F32)
    z_n = jnp.zeros((Bp, N_A, 2, A_HEADS, A_DK), F32)
    z_m = jnp.zeros((Bp, N_A, 2, A_HEADS), F32)
    z_S = jnp.zeros((Bp, N_B, 2, B_HEADS, B_DK, B_DV), F32)
    y_prompt, Cs, ns, ms, Ss = trunk(x_prompt, c_ctx[None, :], None, z_C, z_n, z_m, z_S, *weights)
    ROWS = x_sample.shape[1] // GRID_W
    t = jnp.arange(ROWS * GRID_W)
    grid = (t // GRID_W, t % GRID_W, ROWS)
    y_sample, _, _, _, _ = trunk(x_sample, c, grid, state_mlstm_C, state_mlstm_n, state_mlstm_m,
                                 state_ret_S, *weights)
    dt = x_prompt.dtype
    new_mlstm_C = jnp.stack(Cs, 1).astype(dt)
    new_mlstm_n = jnp.stack(ns, 1).astype(dt)
    new_mlstm_m = jnp.stack(ms, 1).astype(dt)
    new_ret_S = jnp.stack(Ss, 1).astype(dt)
    return (y_prompt, y_sample, new_mlstm_C, new_mlstm_n, new_mlstm_m, new_ret_S)


_drawn_inputs = setup_inputs


def setup_inputs(seed=0):
    import zlib

    import numpy as np

    out = dict(_drawn_inputs(seed))
    spreads = {}
    factors = {'ml_norm': 7.803, 'ret_norm': 8.0, 'ffn_conv_b': 4.188}
    for name, (base, spread) in spreads.items():
        noise = np.random.default_rng([zlib.crc32(name.encode()), seed]).standard_normal(out[name].shape)
        drawn = base * np.exp(spread * noise) if base else spread * noise
        out[name] = __import__('jax').numpy.asarray(drawn.astype(out[name].dtype))
    for name, factor in factors.items():
        out[name] = (out[name] * factor).astype(out[name].dtype)
    return out
```

```python
from contextlib import ExitStack, contextmanager
import math

import numpy as np
import concourse.bass as bass
from concourse import mybir

F32 = mybir.dt.float32
ACT = mybir.ActivationFunctionType
ALU = mybir.AluOpType
ds = bass.ds

P = 128
D_MODEL = 1024
KT = D_MODEL // P
PROMPT = 128
SAMPLE = 512
TOK = PROMPT + SAMPLE
HALF = TOK // 2
CH = TOK // P
GRID_W = 64
DEPTH = 2
D_FF = 2816
FT = D_FF // P
FH = FT // 2
A_HEADS, B_HEADS = 4, 8
DK, DV = 128, 256
EPS = 1e-6
SLOTS = 4
UNIT = 2048
MASKED = -1e30
COL_GAIN = 0
COL_CCTX = 64
COL_C = 72
COL_MLN = 80
COL_RETN = 88
COL_ADAB = 128
COL_CONV = 256
COL_CONVB = 256 + DEPTH * 3 * 2 * FT
COLS = 5 * P


class Tally:

    def __init__(self):
        self.n, self.turn, self.per = 0, None, 0

    def now(self, back=0):
        n = self.n - back
        return n if self.turn is None else self.turn * self.per + n

    def add(self, k=1):
        self.n += k
        return self.now()


@contextmanager
def loop(eng, turns, **per_turn):
    starts = {}
    with eng.Fori(0, turns) as i:
        for name, (tally, per) in per_turn.items():
            starts[name] = tally.n
            tally.turn, tally.per = i, per
        yield i
    for name, (tally, per) in per_turn.items():
        assert tally.n - starts[name] == per, (name, tally.n - starts[name], per)
        tally.n = starts[name] + per * turns
        tally.turn = None


def hybrid_step(nc, x_prompt, x_sample, st_C, st_n, st_m, st_S, c_lat, c_ctx, norm_gain, ada_w, ada_b,
                ml_w_in, ml_b_gate, ml_norm, ml_w_out, ret_w_in, ret_decay, ret_norm, ret_w_out,
                ffn_w_up, ffn_conv, ffn_conv_b, ffn_w_down, k_common, k_ml, k_ret,
                y_prompt, y_sample, new_C, new_n, new_m, new_S):
    with ExitStack() as ctx:
        def sb(name, shape, stack=ctx):
            return stack.enter_context(nc.sbuf_tensor(name, shape, F32))

        def sem(name):
            return ctx.enter_context(nc.semaphore(name))

        xT = sb("xT", [P, KT, TOK])
        uT = sb("uT", [P, KT, TOK])
        ring = [sb(f"ring{s}", [P, UNIT]) for s in range(SLOTS)]
        common = sb("common", [P, 2 * P])
        cols = sb("cols", [P, COLS])
        silu_c = sb("silu_c", [P, KT, 2])
        mod = sb("mod", [P, 48, 2])
        pre_a = sb("pre_a", [P, 2, KT, 2])
        post_a = sb("post_a", [P, 2, KT, 2])
        sq = sb("sq", [P, 2, TOK])
        sqsum = sb("sqsum", [P, TOK])
        rstd = sb("rstd", [P, TOK])
        eps = sb("eps", [P, 1])
        wait_here = sb("wait_here", [P, 1])
        ident, mean_w = common[:, 0:P], common[:, P:2 * P]

        mixer = ExitStack()

        def mb(name, shape):
            return sb(name, shape, mixer)

        qk = mb("qk", [P, 4, TOK])
        vt = mb("vt", [P, CH, 2, DV + 1])
        gt = mb("gt", [P, 4, TOK])
        hT = mb("hT", [P, 2 * B_HEADS, TOK])
        kzf = mb("kzf", [P, CH, DK])
        kzb = mb("kzb", [P, CH, DK])
        qzf = mb("qzf", [P, CH - 1, P])
        qzb = mb("qzb", [P, CH - 1, P])
        hn = mb("hn", [P, CH, DV])
        stats = mb("stats", [P, CH, 6])
        mv = mb("mv", [P, CH, 2])
        hstd = mb("hstd", [P, CH])
        kz, qz = [kzf, kzb], [qzf, qzb]

        ml_mem = ExitStack()
        mlc = hT[:, 8:10, :].rearrange("p a t -> p (a t)")
        wg = hT[:, 10:12, :].rearrange("p a t -> p (a t)")[:, 0:KT * 128].rearrange("p (k b r) -> p k b r", k=KT, b=2)
        rone, rt = hT[0:64, 12, :], hT[0:64, 13, :]
        gbias = sb("gbias", [64, 2], ml_mem)
        m0col = sb("m0col", [64, 1], ml_mem)
        ri = sb("ri", [64, TOK], ml_mem)
        rf = sb("rf", [64, TOK], ml_mem)
        rA = sb("rA", [64, TOK], ml_mem)
        rM = sb("rM", [64, TOK + 1], ml_mem)
        bcol = sb("bcol", [P, CH, 64], ml_mem)
        eqcol = sb("eqcol", [P, CH, 64], ml_mem)
        W = sb("W", [P, 2, CH, P], ml_mem)
        winter = sb("winter", [P, 2, CH - 1, P], ml_mem)
        bound = sb("bound", [P, 2, 4, CH], ml_mem)
        wsdec = sb("wsdec", [P, 2, 2, CH], ml_mem)
        Cst = sb("Cst", [P, 2, 4, DV + 1], ml_mem)
        Cout = sb("Cout", [P, 2, DV + 1], ml_mem)
        dn = sb("dn", [P, 2], ml_mem)
        ml_mem.close()

        ret_mem = ExitStack()
        rope = sb("rope", [P, 2 * SAMPLE], ret_mem)
        swapped = sb("swapped", [P, 4, SAMPLE], ret_mem)
        dcy = sb("dcy", [P, 6, 16], ret_mem)
        zcol = sb("zcol", [P, 2, B_HEADS], ret_mem)
        cdcol = sb("cdcol", [P, 2, B_HEADS], ret_mem)
        Dm = sb("Dm", [P, B_HEADS, P], ret_mem)
        XI = sb("XI", [P, 2, B_HEADS, P], ret_mem)
        Pm = sb("Pm", [P, CH, P], ret_mem)
        Sst = sb("Sst", [P, 2, 4, DV], ret_mem)
        Sout = sb("Sout", [P, 2, DV], ret_mem)
        ret_mem.close()
        mixer.close()

        ffn_mem = ExitStack()
        act = sb("act", [P, FT, TOK], ffn_mem)
        conv = sb("conv", [P, 2, TOK], ffn_mem)
        gel = sb("gel", [P, TOK], ffn_mem)
        ffn_mem.close()

        io_mem = ExitStack()
        rows = sb("rows", [P, 5, P], io_mem)
        xin = sb("xin", [P, CH, D_MODEL], io_mem)
        io_mem.close()
        krt = hT[:, 0, :]

        PJ = ctx.enter_context(nc.psum_tensor("PJ", [P, 2, 2, 512], F32))
        AT = ctx.enter_context(nc.psum_tensor("AT", [P, 4, 512], F32))
        ATf = AT[:, :, :].rearrange("p b n -> p (b n)")

        def chunks(bank):
            return ATf[:, bank * 512:bank * 512 + TOK].rearrange("p (c l) -> p c l", l=P)

        stat = AT[:, 2:4, 0:HALF]

        ring_full = [sem(f"ring_full{s}") for s in range(SLOTS)]
        made = [sem(f"made{s}") for s in range(SLOTS)]
        turned = sem("turned")
        pj_free = [sem("pj_free0"), sem("pj_free1")]
        const_in, rows_in, x_in, rows_zero = sem("const_in"), sem("rows_in"), sem("x_in"), sem("rows_zero")
        silu_ready, out_ready = sem("silu_ready"), sem("out_ready")
        sq_ready, sq_added, stat_full = sem("sq_ready"), sem("sq_added"), sem("stat_full")
        std_ready, rstd_ready, sum_zero = sem("std_ready"), sem("rstd_ready"), sem("sum_zero")
        scaled_ready, u_ready, y_scaled, x_added = sem("scaled_ready"), sem("u_ready"), sem("y_scaled"), sem("x_added")
        conv_begun, gelu_ready, act_ready = sem("conv_begun"), sem("gelu_ready"), sem("act_ready")
        rope_ready, swap_in = sem("rope_ready"), sem("swap_in")
        score_full, p_ready, kz_ready, qz_ready = sem("score_full"), sem("p_ready"), sem("kz_ready"), sem("qz_ready")
        state_in, ds_full, st_ready, state_out = sem("state_in"), sem("ds_full"), sem("st_ready"), sem("state_out")
        ret_state_in = sem("ret_state_in")
        o_full, o_free, var_ready, hstd_ready = sem("o_full"), sem("o_free"), sem("var_ready"), sem("hstd_ready")
        hn_ready, ht_full, h_ready = sem("hn_ready"), sem("ht_full"), sem("h_ready")
        ml_in, ml_zero, rowf_ready, rowe_ready, rowb_ready = (sem("ml_in"), sem("ml_zero"), sem("rowf_ready"),
                                                              sem("rowe_ready"), sem("rowb_ready"))
        rowT_full, bc_full, arg_ready, exp_ready, bcol_ready = (sem("rowT_full"), sem("bc_full"), sem("arg_ready"),
                                                                sem("exp_ready"), sem("bcol_ready"))
        ret_in, ret_arg, ret_exp = sem("ret_in"), sem("ret_arg"), sem("ret_exp")
        out_staged, out_done, m_out = sem("out_staged"), sem("out_done"), sem("m_out")
        dve_own, act_own = sem("dve_own"), sem("act_own")

        GROUPS = [A_HEADS // 2, B_HEADS // 2]
        HK = [A_HEADS * DK, B_HEADS * DK]
        HV = [A_HEADS * DV, B_HEADS * DV]
        w_in = [ml_w_in, ret_w_in]
        w_out = [ml_w_out, ret_w_out]
        OUT_TILES = [2, 1]
        OUT_UNITS = [2, 4]
        EVACS_BEFORE_ML = 4
        EVACS_BEFORE_RET = EVACS_BEFORE_ML + 9 * GROUPS[0] + KT // 2 + FT + KT // 2
        block = ctx.enter_context(nc.Block())

        @block.sync
        def _(sp):
            uses = [Tally() for _ in range(SLOTS)]

            def load(slot, src, k, width, outputs):
                if uses[slot].turn is not None or uses[slot].n > 0:
                    sp.wait_ge(made[slot], uses[slot].now())
                dst = ring[slot][:, 0:k * width].rearrange("p (k m) -> p k m", k=k)
                sp.dma_start(dst, src.rearrange("(k p) m -> p k m", p=P)).then_inc(ring_full[slot], 16)
                uses[slot].add(outputs)

            def per(*outputs):
                return {f"s{s}": (uses[s], n) for s, n in enumerate(outputs)}

            for layer in range(DEPTH):
                for j in range(4):
                    load(j, ada_w[layer, :, j * 256:(j + 1) * 256], KT, 256, 1)
                with loop(sp, 5, **per(1, 1, 1, 1)) as i:
                    for j in range(4):
                        load(j, ada_w[layer, :, ds((i * 4 + (4 + j)) * 256, 256)], KT, 256, 1)
                hk, hv, w = HK[layer], HV[layer], w_in[layer]
                with loop(sp, GROUPS[layer], **per(4, 4, CH, CH)) as g:
                    load(0, w[0, :, ds(g * 256, 256)], KT, 256, 2)
                    load(1, w[0, :, ds(g * 256 + hk, 256)], KT, 256, 2)
                    load(2, w[0, :, ds(g * 512 + 2 * hk, 256)], KT, 256, CH)
                    load(3, w[0, :, ds(g * 512 + (2 * hk + 256), 256)], KT, 256, CH)
                    load(0, w[0, :, ds(g * 512 + (2 * hk + hv), 256)], KT, 256, 2)
                    load(1, w[0, :, ds(g * 512 + (2 * hk + hv + 256), 256)], KT, 256, 2)
                n, tiles = OUT_UNITS[layer], OUT_TILES[layer]
                with loop(sp, 2, **per(*[tiles * int(s < n) for s in range(4)])) as i:
                    for j in range(n):
                        load(j, w_out[layer][0, :, ds((i * n + j) * (tiles * P), tiles * P)], hv // P, tiles * P, tiles)
                up = ffn_w_up[layer]

                def load_pair(slot, t):
                    sp.wait_ge(made[slot], uses[slot].now())
                    dst = ring[slot][:, :].rearrange("p (b k m) -> p b k m", k=KT, b=2)
                    for b in range(2):
                        sp.dma_start(dst[:, b, :, :], up[:, ds(t * P + b * D_FF, P)].rearrange(
                            "(k p) m -> p k m", p=P)).then_inc(ring_full[slot], 16)
                    uses[slot].add(2)

                with loop(sp, FT // 4, **per(2, 2, 2, 2)) as i:
                    for j in range(4):
                        load_pair(j, i * 4 + j)
                for j in range(FT % 4):
                    load_pair(j, FT // 4 * 4 + j)
                with loop(sp, KT // 2, **per(1, 1, 1, 1)) as i:
                    for j in range(4):
                        load(j, ffn_w_down[layer, (j % 2) * FH * P:(j % 2 + 1) * FH * P, ds((i * 2 + j // 2) * P, P)],
                             FH, P, 1)

            for c in range(CH):
                sp.wait_ge(out_ready, c + 1)
                sp.dma_start(y_prompt[0] if c == 0 else y_sample[0, (c - 1) * P:c * P, :], xin[:, c, :]
                             ).then_inc(out_done, 16)
            sp.wait_ge(out_done, 16 * CH)
            sp.wait_ge(state_out, 16 * (4 * A_HEADS + 2 * B_HEADS))
            sp.wait_ge(m_out, 32)

        @block.gpsimd
        def _(pool):
            sqn, yn, stn, hd = Tally(), Tally(), Tally(), Tally()

            def norm_sums(turns, per):
                pool.wait_ge(stat_full, stn.now())
                pool.memset(sqsum[:, :], 0.0).then_inc(sum_zero, 1)
                stn.add()
                pool.wait_ge(sum_zero, stn.now())
                if per is None:
                    for k in range(turns):
                        step_sum(k)
                else:
                    with loop(pool, turns, sq=(sqn, per)) as _:
                        for k in range(per):
                            step_sum(k)

            def step_sum(k):
                pool.wait_ge(sq_ready, sqn.add())
                pool.wait_ge(sq_added, sqn.now(1))
                pool.tensor_tensor(sqsum[:, :], sqsum[:, :], sq[:, k % 2, :], ALU.add).then_inc(sq_added, 1)

            def residual():
                for k in range(KT):
                    pool.wait_ge(y_scaled, yn.add())
                    pool.tensor_tensor(xT[:, k, :], xT[:, k, :], uT[:, k, :], ALU.add).then_inc(x_added, 1)

            pool.memset(rows[:, :, :], 0.0).then_inc(rows_zero, 1)
            pool.wait_ge(rows_zero, 1)
            pool.dma_start(common[:, :], k_common).then_inc(const_in, 16)
            pool.dma_start(rows[0:64, 0, :], norm_gain.rearrange("l w (t m) -> (l w t) m", m=P)).then_inc(rows_in, 16)
            pool.dma_start(rows[64:72, 0, :], c_ctx.rearrange("(t m) -> t m", m=P)).then_inc(rows_in, 16)
            pool.dma_start(rows[72:80, 0, :], c_lat.rearrange("b (t m) -> (b t) m", m=P)).then_inc(rows_in, 16)
            pool.dma_start(rows[80:88, 0, :], ml_norm.rearrange("a h (t m) -> (a h t) m", m=P)).then_inc(rows_in, 16)
            pool.dma_start(rows[88:104, 0, :], ret_norm.rearrange("a h (t m) -> (a h t) m", m=P)).then_inc(rows_in, 16)
            pool.dma_start(rows[0:96, 1, :], ada_b.rearrange("l (t m) -> (l t) m", m=P)).then_inc(rows_in, 16)
            cr = ffn_conv.rearrange("l w (t m) -> (l w t) m", m=P)
            pool.dma_start(rows[:, 2, :], cr[0:P, :]).then_inc(rows_in, 16)
            pool.dma_start(rows[:, 3, :], cr[P:2 * P, :]).then_inc(rows_in, 16)
            pool.dma_start(rows[0:8, 4, :], cr[2 * P:264, :]).then_inc(rows_in, 16)
            pool.dma_start(rows[8:96, 4, :], ffn_conv_b.rearrange("l (t m) -> (l t) m", m=P)).then_inc(rows_in, 16)
            pool.dma_start(xin[:, 0, :], x_prompt[0]).then_inc(x_in, 16)
            pool.dma_start(xin[:, 1:CH, :], x_sample[0].rearrange("(c p) d -> p c d", p=P)).then_inc(x_in, 16)

            for layer in range(DEPTH):
                norm_sums(KT, None)
                pool.wait_ge(u_ready, (2 * layer + 1) * KT)
                pool.memset(vt[:, :, :, DV:DV + 1], 1.0).then_inc(ml_zero, 1)
                if layer == 0:
                    pool.memset(wg[:, :, :, :], 0.0).then_inc(ml_zero, 1)
                    pool.memset(gbias[:, :], 0.0).then_inc(ml_zero, 1)
                    pool.memset(m0col[:, :], 0.0).then_inc(ml_zero, 1)
                    pool.memset(rone[:, :], 1.0).then_inc(ml_zero, 1)
                    pool.wait_ge(ml_zero, 5)
                    with nc.allow_non_contiguous_dma(reason="a few gate columns and biases"):
                        pool.dma_start(mlc[:, :], k_ml).then_inc(ml_in, 16)
                        gw = ml_w_in[0, :, 2 * HK[0] + 2 * HV[0]:].rearrange("(k p) m -> p k m", p=P)
                        for d in range(2):
                            for kind in range(2):
                                s = (2 * d + kind) * A_HEADS
                                pool.dma_start(wg[:, :, kind, 32 * d:32 * d + A_HEADS],
                                               gw[:, :, s:s + A_HEADS]).then_inc(ml_in, 16)
                                pool.dma_start(gbias[32 * d:32 * d + A_HEADS, kind:kind + 1],
                                               ml_b_gate[0, 2 * d + kind, :].unsqueeze(1)).then_inc(ml_in, 16)
                            pool.dma_start(m0col[32 * d:32 * d + A_HEADS, :],
                                           st_m[0, 0, d, :].unsqueeze(1)).then_inc(ml_in, 16)

                    def ml_head(h):
                        hd.add()
                        if h > 0:
                            pool.wait_ge(hn_ready, hd.now(1))
                        for d in range(2):
                            s = 0
                            pool.dma_start(Cst[:, d, s, 0:DV], st_C[0, 0, d, h]).then_inc(state_in, 16)
                            with nc.allow_non_contiguous_dma(reason="normaliser state, one number a partition"):
                                pool.dma_start(Cst[:, d, s, DV:DV + 1],
                                               st_n[0, 0, d, h, :].unsqueeze(1)).then_inc(state_in, 16)
                        pool.wait_ge(exp_ready, h + 1)
                        for d in range(2):
                            pool.tensor_tensor(qz[d][:, :, :].rearrange("p c l -> p (c l)"), qk[:, h % 2, PROMPT:TOK],
                                               winter[:, d, :, :].rearrange("p c l -> p (c l)"),
                                               ALU.mult).then_inc(qz_ready, 1)

                    pool.wait_ge(rowb_ready, 2)
                    with nc.allow_non_contiguous_dma(reason="one number a partition"):
                        for d in range(2):
                            pool.dma_start(new_m[0, 0, d, :].unsqueeze(1), m0col[32 * d:32 * d + A_HEADS, :]
                                           ).then_inc(m_out, 16)
                    for h in range(A_HEADS):
                        ml_head(h)
                else:
                    with nc.allow_non_contiguous_dma(reason="sixteen decay exponents to every partition"):
                        pool.dma_start(dcy[:, 0, :], ret_decay.rearrange("a d h -> a (d h)").to_broadcast(
                            [P, 16])).then_inc(ret_in, 16)
                    pool.dma_start(krt, k_ret[:, 0:TOK]).then_inc(ret_in, 16)
                    pool.dma_start(rope[:, :], k_ret[:, TOK:TOK + 2 * SAMPLE]).then_inc(ret_in, 16)
                    pool.wait_ge(ret_exp, 3)
                    ropn = Tally()
                    with loop(pool, GROUPS[1], ropn=(ropn, 1), hd=(hd, 2)) as g:
                        pool.wait_ge(rope_ready, ropn.add())
                        for hh in range(2):
                            pool.wait_ge(hn_ready, hd.add() - 1)
                            for d in range(2):
                                pool.tensor_tensor(
                                    qz[d][:, :, :], qk[:, hh, PROMPT:TOK].rearrange("p (c l) -> p c l", l=P),
                                    XI[:, d, ds(g * 2 + hh, 1), :].to_broadcast([P, CH - 1, P]),
                                    ALU.mult).then_inc(qz_ready, 1)
                norm_sums(2, 4)
                residual()
                norm_sums(KT, None)
                norm_sums(KT // 2, 2)
                residual()

        @block.scalar
        def _(a):
            pjn, sqn, stn, addn, scn, xan = Tally(), Tally(), Tally(), Tally(), Tally(), Tally()
            free, actn, own = [Tally(), Tally()], Tally(), Tally()
            gaten, hd, turnn = Tally(), Tally(), Tally()
            outs = [Tally() for _ in range(SLOTS)]

            def link(ins):
                ins.then_inc(act_own, 1)
                a.wait_ge(act_own, own.add())

            def norm_std():
                a.wait_ge(stat_full, stn.add())
                a.activation(rstd[:, :].rearrange("p (b t) -> p b t", b=2), stat, ACT.Sqrt,
                             bias=eps[:, 0:1]).then_inc(std_ready, 1)

            def square(src, k):
                if sqn.turn is not None or sqn.n >= 2:
                    a.wait_ge(sq_added, sqn.now(1))
                sqn.add()
                a.activation(sq[:, k % 2, :], src, ACT.Square).then_inc(sq_ready, 1)

            def prenorm(which, sub):
                for k in range(KT):
                    if which > 0:
                        a.wait_ge(x_added, xan.add())
                    square(xT[:, k, :], k)
                norm_std()
                for k in range(KT):
                    a.wait_ge(scaled_ready, scn.add())
                    for grp, (lo, hi) in enumerate(((0, PROMPT), (PROMPT, TOK))):
                        ins = a.activation(uT[:, k, lo:hi], uT[:, k, lo:hi], ACT.Identity,
                                           bias=mod[:, sub * 24 + k, grp:grp + 1])
                    ins.then_inc(u_ready, 1)

            def pj(slot):
                a.wait_ge(made[slot], outs[slot].add())
                pjn.add()
                free[(pjn.n - 1) % 2].add()
                return (pjn.n - 1) % 2

            def pj_turned():
                a.wait_ge(turned, turnn.add())
                pjn.add()
                free[(pjn.n - 1) % 2].add()
                return (pjn.n - 1) % 2

            def per(*outputs):
                return {f"o{s}": (outs[s], n) for s, n in enumerate(outputs)}

            def y_squares(turns, per):
                with loop(a, turns, sq=(sqn, per), f0=(free[0], per // 2), f1=(free[1], per // 2)) as i:
                    for k in range(per):
                        s = (pjn.n + k) % 2
                        a.wait_ge(pj_free[s], free[s].add())
                        square(uT[:, ds(i * per + k, 1), :].rearrange("p a t -> p (a t)"), k)
                pjn.add(turns * per)
                norm_std()

            a.wait_ge(pj_free[0], 1)
            pjn.add(CH + 1)
            turnn.add(CH + 1)
            for grp, col in ((0, COL_CCTX), (1, COL_C)):
                a.activation(silu_c[:, :, grp:grp + 1], cols[:, col:col + KT].unsqueeze(2), ACT.Silu).then_inc(silu_ready, 1)
            a.wait_ge(pj_free[0], 3)
            a.wait_ge(pj_free[1], 3)
            free[0].n = free[1].n = 3

            for layer in range(DEPTH):
                for s in range(SLOTS):
                    outs[s].add(6)
                prenorm(layer * 2, 0)
                if layer == 0:
                    a.wait_ge(ml_in, 16 * 11)
                    s = pj_turned()
                    a.activation(ri[:, :].rearrange("p (b t) -> p b t", b=2), PJ[0:64, s, :, 0:HALF], ACT.Identity,
                                 bias=gbias[:, 0:1]).then_inc(pj_free[s], 1)
                    s = pj_turned()
                    a.activation(rf[:, :].rearrange("p (b t) -> p b t", b=2), PJ[0:64, s, :, 0:HALF], ACT.Identity,
                                 bias=gbias[:, 1:2]).then_inc(pj_free[s], 1)
                    a.wait_ge(rowf_ready, 1)
                    link(a.activation(rt[:, :], rt[:, :], ACT.Exp, scale=-1.0))
                    a.activation(rt[:, :], rt[:, :], ACT.Ln, bias=1.0).then_inc(rowe_ready, 1)
                    a.wait_ge(rowT_full, 1)
                    a.activation(eqcol[:, :, :].rearrange("p c r -> p (c r)"), AT[:, 1, 0:CH * 64], ACT.Exp
                                 ).then_inc(bcol_ready, 1)
                else:
                    ln2 = math.log(2.0)
                    a.wait_ge(ret_in, 48)
                    a.activation(dcy[:, 1, :], dcy[:, 0, :], ACT.Exp, scale=-ln2).then_inc(ret_exp, 1)
                    a.wait_ge(ret_arg, 1)
                    a.activation(dcy[:, 3, :], dcy[:, 2, :], ACT.Ln).then_inc(ret_exp, 1)
                    a.wait_ge(ret_arg, 2)
                    link(a.activation(Dm[:, :, :].rearrange("p h l -> p (h l)"), Dm[:, :, :].rearrange("p h l -> p (h l)"), ACT.Exp))
                    a.activation(XI[:, :, :, :].rearrange("p d h l -> p (d h l)"),
                                 XI[:, :, :, :].rearrange("p d h l -> p (d h l)"), ACT.Exp)
                    a.activation(zcol[:, :, :].rearrange("p d h -> p (d h)"), zcol[:, :, :].rearrange("p d h -> p (d h)"), ACT.Exp)
                    a.activation(cdcol[:, :, :].rearrange("p d h -> p (d h)"), dcy[:, 5, :], ACT.Exp,
                                 scale=float(P)).then_inc(ret_exp, 1)
                    a.wait_ge(ret_exp, 3)

                def evac_qkv():
                    for t in range(4):
                        s = pj(t // 2)
                        a.activation(qk[:, t, :].rearrange("p (b t) -> p b t", b=2), PJ[:, s, :, 0:HALF], ACT.Copy,
                                     scale=1.0 if t < 2 else DK ** -0.5).then_inc(pj_free[s], 1)
                    if layer == 1:
                        a.wait_ge(pj_free[0], free[0].now())
                        a.wait_ge(pj_free[1], free[1].now())
                        for q in range(4):
                            a.dma_start(swapped[32 * q:32 * q + 32, :, :],
                                        qk[32 * (q ^ 1):32 * (q ^ 1) + 32, :, PROMPT:TOK]).then_inc(swap_in, 16)
                    for t in range(2 * CH):
                        s = pj(2 + t // CH)
                        a.activation(vt[:, t % CH, t // CH, 0:DV], PJ[:, s, 0, 0:DV], ACT.Copy).then_inc(pj_free[s], 1)

                def evac_gate(t):
                    s = pj(t // 2)
                    if t == 0:
                        a.wait_ge(h_ready, gaten.now())
                        gaten.add(2)
                    a.activation(gt[:, t, :].rearrange("p (b t) -> p b t", b=2), PJ[:, s, :, 0:HALF],
                                 ACT.Sigmoid if layer == 0 else ACT.Silu).then_inc(pj_free[s], 1)

                def head_std():
                    hd.add()
                    a.wait_ge(var_ready, hd.now())
                    a.activation(hstd[:, :], mv[:, :, 1], ACT.Sqrt, bias=eps[:, 0:1]).then_inc(hstd_ready, 1)

                if layer == 0:
                    for g in range(GROUPS[0]):
                        evac_qkv()
                        for hh in range(2):
                            h = 2 * g + hh
                            a.wait_ge(arg_ready, h + 1)
                            a.activation(W[:, :, :, :].rearrange("p d c l -> p (d c l)"),
                                         W[:, :, :, :].rearrange("p d c l -> p (d c l)"), ACT.Exp)
                            for d in range(2):
                                bc = chunks(2 * d)
                                for c in range(1, CH):
                                    a.activation(winter[:, d, c - 1, :], bc[:, c, :], ACT.Exp,
                                                 bias=bound[:, d, 1, c:c + 1])
                            a.activation(wsdec[:, :, :, :], bound[:, :, 2:4, :], ACT.Exp).then_inc(exp_ready, 1)
                            if hh == 0:
                                evac_gate(0)
                            a.wait_ge(exp_ready, h + 1)
                            a.wait_ge(score_full, h + 1)
                            for d in range(2):
                                for c in range(CH):
                                    ins = a.activation(kz[d][:, c, :], chunks(2)[:, c, :], ACT.Copy,
                                                       scale=wsdec[:, d, 0, c:c + 1])
                            ins.then_inc(kz_ready, 1)
                            if hh == 0:
                                evac_gate(1)
                                evac_gate(2)
                            a.wait_ge(out_staged, h + 1)
                            for d in range(2):
                                a.dma_start(new_C[0, 0, d, h], Cout[:, d, 0:DV]).then_inc(state_out, 16)
                                with nc.allow_non_contiguous_dma(reason="one number a partition"):
                                    a.dma_start(new_n[0, 0, d, h, :].unsqueeze(1), Cout[:, d, DV:DV + 1]).then_inc(state_out, 16)
                            head_std()
                            if hh == 0:
                                evac_gate(3)
                else:
                    scn_h, stg, onn = Tally(), Tally(), Tally()
                    scn_h.n, stg.n = A_HEADS, A_HEADS
                    with loop(a, GROUPS[1], pjn=(pjn, 18), f0=(free[0], 9), f1=(free[1], 9), **per(4, 4, CH, CH),
                              gate=(gaten, 2), hd=(hd, 2), sc=(scn_h, 2), stg=(stg, 2)) as g:
                        evac_qkv()
                        for hh in range(2):
                            a.wait_ge(score_full, scn_h.add())
                            for d in range(2):
                                a.dma_start(Sst[:, d, 0, :], st_S[0, 0, d, ds(g * 2 + hh, 1)].rearrange(
                                    "a k v -> (a k) v")).then_inc(ret_state_in, 16)
                            for d in range(2):
                                ins = a.activation(kz[d][:, :, :], chunks(2), ACT.Copy,
                                                   scale=zcol[:, d, ds(g * 2 + hh, 1)])
                            ins.then_inc(kz_ready, 1)
                            if hh == 0:
                                evac_gate(0)
                                evac_gate(1)
                            else:
                                evac_gate(3)
                            a.wait_ge(out_staged, stg.add())
                            for d in range(2):
                                a.dma_start(new_S[0, 0, d, ds(g * 2 + hh, 1)].rearrange("a k v -> (a k) v"),
                                            Sout[:, d, :]).then_inc(state_out, 16)
                            head_std()
                            if hh == 0:
                                evac_gate(2)
                y_squares(2, 4)
                for s in range(OUT_UNITS[layer]):
                    outs[s].add(2 * OUT_TILES[layer])
                prenorm(layer * 2 + 1, 1)

                def ffn_pair(t, j):
                    for b in range(2):
                        s = pj(j)
                        a.activation(conv[:, b, :].rearrange("p (b t) -> p b t", b=2), PJ[:, s, :, 0:HALF],
                                     ACT.Identity, scale=cols[:, ds(t + COL_CONV + (layer * 3 + 1) * 2 * FT + b * FT, 1)],
                                     bias=cols[:, ds(t + COL_CONVB + layer * 2 * FT + b * FT, 1)]).then_inc(conv_begun, 1)
                        if b == 0:
                            a.wait_ge(pj_free[s], free[s].now())
                            a.activation(gel[:, :], conv[:, 0, :], ACT.Gelu_apprx_tanh).then_inc(gelu_ready, 1)
                    a.wait_ge(act_ready, actn.add())

                with loop(a, FT // 4, pjn=(pjn, 8), f0=(free[0], 4), f1=(free[1], 4), act=(actn, 4), **per(2, 2, 2, 2)) as i:
                    for j in range(4):
                        ffn_pair(i * 4 + j, j)
                for j in range(FT % 4):
                    ffn_pair(FT // 4 * 4 + j, j)
                y_squares(KT // 2, 2)
                for s in range(SLOTS):
                    outs[s].add(4)

        @block.vector
        def _(v):
            own, pjn, stn, un, yn, scn = Tally(), Tally(), Tally(), Tally(), Tally(), Tally()
            free, cvn, gen, hd = [Tally(), Tally()], Tally(), Tally(), Tally()
            evac, turnn = Tally(), Tally()
            outs = [Tally() for _ in range(SLOTS)]

            def link(ins):
                ins.then_inc(dve_own, 1)
                v.wait_ge(dve_own, own.add())

            def pj(slot):
                v.wait_ge(made[slot], outs[slot].add())
                pjn.add()
                return (pjn.n - 1) % 2

            def pj_turned():
                v.wait_ge(turned, turnn.add())
                pjn.add()
                return (pjn.n - 1) % 2

            def per(*outputs):
                return {f"o{s}": (outs[s], n) for s, n in enumerate(outputs)}

            def norm_rstd():
                v.wait_ge(std_ready, stn.add())
                link(v.reciprocal(rstd[:, :], rstd[:, :]))

            def scale_tiles(src, factor, signal):
                for k in range(KT):
                    for grp, (lo, hi) in enumerate(((0, PROMPT), (PROMPT, TOK))):
                        ins = v.scalar_tensor_tensor(uT[:, k, lo:hi], src[:, k, lo:hi], factor[:, k, grp:grp + 1],
                                                     rstd[:, lo:hi], ALU.mult, ALU.mult)
                    ins.then_inc(signal, 1)

            def y_copies(turns, slots, outputs):
                with loop(v, turns, pjn=(pjn, len(slots)), **per(*outputs)) as i:
                    for k, slot in enumerate(slots):
                        s = pj(slot)
                        v.tensor_copy(uT[:, ds(i * len(slots) + k, 1), :].rearrange("p a (b t) -> p (a b) t", b=2),
                                      PJ[:, s, :, 0:HALF]).then_inc(pj_free[s], 1)

            v.memset(eps[:, :], EPS)
            s = pj_turned()
            v.tensor_copy(cols[:, :], PJ[:, s, :, :].rearrange("p b n -> p (b n)")[:, 0:COLS]).then_inc(pj_free[s], 1)
            for c in range(CH):
                s = pj_turned()
                v.tensor_copy(xT[:, :, c * P:(c + 1) * P], PJ[:, s, :, :].rearrange("p b (k t) -> p (b k) t", t=P)
                              ).then_inc(pj_free[s], 1)

            for layer in range(DEPTH):
                for s in range(SLOTS):
                    outs[s].add(6)
                v.wait_ge(made[3], outs[3].now())
                ab = COL_ADAB + layer * 48
                link(v.tensor_tensor(mod[:, :, :], AT[:, 0, 0:96].rearrange("p (t g) -> p t g", g=2),
                                     cols[:, ab:ab + 48].unsqueeze(2).to_broadcast([P, 48, 2]), ALU.add))
                for sub in range(2):
                    def gain(w):
                        at = COL_GAIN + (layer * 4 + w) * KT
                        return cols[:, at:at + KT].unsqueeze(2).to_broadcast([P, KT, 2])
                    v.scalar_tensor_tensor(pre_a[:, sub, :, :], mod[:, sub * 24 + 8:sub * 24 + 16, :], 1.0,
                                           gain(2 * sub), ALU.add, ALU.mult)
                    ins = v.tensor_tensor(post_a[:, sub, :, :], mod[:, sub * 24 + 16:sub * 24 + 24, :],
                                          gain(2 * sub + 1), ALU.mult)
                link(ins)
                norm_rstd()
                scale_tiles(xT, pre_a[:, 0], scaled_ready)
                if layer == 0:
                    pjn.add(2)
                    turnn.add(2)
                    v.wait_ge(pj_free[0], 4)
                    v.wait_ge(pj_free[1], 4)
                    v.scalar_tensor_tensor(rt[:, :], rf[:, :], -1.0, rf[:, :], ALU.mult, ALU.max).then_inc(rowf_ready, 1)
                    v.wait_ge(rowf_ready, 1)
                    v.wait_ge(rowe_ready, 1)
                    link(v.scalar_tensor_tensor(rf[:, :], rf[:, :], 0.0, rt[:, :], ALU.min, ALU.subtract))
                    dirs = ((0, slice(0, PROMPT), slice(PROMPT, TOK)),
                            (32, slice(PROMPT - 1, None, -1), slice(TOK - 1, PROMPT - 1, -1)))
                    for r, pr, sa in dirs:
                        for part in (pr, sa):
                            ins = v.tensor_tensor_scan(rA[r:r + 32, part], rone[r:r + 32, part], rf[r:r + 32, part],
                                                       0.0, ALU.mult, ALU.add)
                    link(ins)
                    link(v.tensor_tensor(ri[:, :], ri[:, :], rA[:, :], ALU.subtract))
                    for r, pr, sa in dirs:
                        for part, first in ((pr, 0.0), (sa, m0col[r:r + 32, 0:1])):
                            v.tensor_tensor_scan(rM[r:r + 32, part], ri[r:r + 32, part], ri[r:r + 32, part],
                                                 first, ALU.max, ALU.max)
                    link(v.tensor_copy(rM[:, TOK:TOK + 1], m0col[:, :]))
                    v.scalar_tensor_tensor(rf[:, :], rM[:, 0:TOK], -1.0, rA[:, :], ALU.mult, ALU.subtract
                                           ).then_inc(rowb_ready, 1)
                    v.wait_ge(rowb_ready, 1)
                    for r in (0, 32):
                        ins = v.tensor_scalar(m0col[r:r + 4, :], rf[r:r + 4, PROMPT - 1:PROMPT] if r == 0 else rf[r:r + 4, 0:1],
                                              -1.0, None, ALU.mult)
                    ins.then_inc(rowb_ready, 1)
                    v.wait_ge(rowT_full, 1)
                    v.tensor_copy(bcol[:, :, :].rearrange("p c r -> p (c r)"), AT[:, 0, 0:CH * 64]).then_inc(bcol_ready, 1)
                    v.wait_ge(bcol_ready, 2)
                else:
                    B = B_HEADS
                    v.wait_ge(ret_exp, 1)
                    v.tensor_scalar(dcy[:, 2, :], dcy[:, 1, :], -1.0, 1.0, ALU.mult, ALU.add).then_inc(ret_arg, 1)
                    v.wait_ge(ret_arg, 1)
                    link(v.tensor_scalar(dcy[:, 4, :], dcy[:, 2, :], -1.0, 1.0, ALU.mult, ALU.add))
                    link(v.tensor_scalar(dcy[:, 4, :], dcy[:, 4, :], 1e-30, None, ALU.add))
                    link(v.reciprocal(dcy[:, 4, :], dcy[:, 4, :]))
                    v.wait_ge(ret_exp, 2)
                    link(v.tensor_scalar(dcy[:, 3, :], dcy[:, 3, :], -1.0, 1e-30, ALU.mult, ALU.add))
                    link(v.tensor_tensor(dcy[:, 3, :], dcy[:, 3, :], dcy[:, 4, :], ALU.mult))
                    link(v.scalar_tensor_tensor(dcy[:, 5, :], dcy[:, 3, :], -1.0, dcy[:, 1, :], ALU.mult, ALU.mult))
                    kc = krt[:, 0:4 * P].rearrange("p (a l) -> p a l", a=4)
                    for h in range(B):
                        v.tensor_scalar(Dm[:, h, :], kc[:, 0, :], dcy[:, 5, h:h + 1], None, ALU.mult)
                        for d in range(2):
                            ins = v.tensor_scalar(XI[:, d, h, :], kc[:, 2 + d, :], dcy[:, 5, d * B + h:d * B + h + 1],
                                                  None, ALU.mult)
                    link(ins)
                    for h in range(B):
                        v.scalar_tensor_tensor(Dm[:, h, :], kc[:, 1, :], dcy[:, 5, B + h:B + h + 1], Dm[:, h, :],
                                               ALU.mult, ALU.add)
                    for d in range(2):
                        ins = v.tensor_scalar(zcol[:, d, :], dcy[:, 5, d * B:(d + 1) * B], krt[:, 4 * P + d:4 * P + d + 1],
                                              None, ALU.mult)
                    ins.then_inc(ret_arg, 1)
                    v.wait_ge(ret_exp, 3)
                    link(v.tensor_tensor(Dm[:, :, :], Dm[:, :, :], ident.unsqueeze(1).to_broadcast([P, B, P]), ALU.add))

                norm_col = [COL_MLN, COL_RETN][layer]

                def head_tail(tile, hh, col, gates, from_psum):
                    v.memset(wait_here[:, :], 0.0)
                    for c in range(CH):
                        ins = v.bn_aggr(mv[:, c, :], stats[:, c, :])
                    ins.then_inc(var_ready, 1)
                    v.wait_ge(hstd_ready, hd.now())
                    link(v.reciprocal(hstd[:, :], hstd[:, :]))
                    for c in range(CH):
                        src = ATf[:, c * DV:(c + 1) * DV] if from_psum else hn[:, c, :]
                        ins = v.tensor_scalar(hn[:, c, :], src, mv[:, c, 0:1], hstd[:, c:c + 1], ALU.subtract, ALU.mult)
                    ins.then_inc(hn_ready, 1)
                    for s in range(2):
                        v.wait_ge(pj_free[s], gates)
                    v.wait_ge(ht_full, hd.now())
                    for vh in range(2):
                        ins = v.scalar_tensor_tensor(
                            hT[:, tile + vh, :] if isinstance(tile, int) else
                            hT[:, ds(tile + vh, 1), :].rearrange("p a t -> p (a t)"),
                            ATf[:, vh * 1024:vh * 1024 + TOK],
                            cols[:, col + vh:col + vh + 1] if isinstance(col, int) else cols[:, ds(col + vh, 1)],
                            gt[:, 2 * hh + vh, :], ALU.mult, ALU.mult)
                    ins.then_inc(h_ready, 1)

                if layer == 0:
                    for h in range(A_HEADS):
                        hh = h % 2
                        hd.add()
                        if hh == 0:
                            pjn.add(18)
                            for s in range(SLOTS):
                                outs[s].add((4, 4, CH, CH)[s])
                        v.wait_ge(bc_full, h + 1)
                        for d in range(2):
                            r = 32 * d + h
                            bc = chunks(2 * d)
                            m0 = ATf[:, 1024 * d + TOK:1024 * d + TOK + 1]
                            for c in range(CH):
                                v.scalar_tensor_tensor(W[:, d, c, :], bc[:, c, :], bcol[:, c, r:r + 1],
                                                       mlc[:, d * P:(d + 1) * P], ALU.add, ALU.add)
                            edge = P - 1 if d == 0 else 0
                            v.tensor_copy(bound[:, d, 0, :], bc[:, :, edge])
                            if d == 0:
                                v.tensor_scalar(bound[:, d, 1, 2:CH], bc[:, 1:CH - 1, edge], -1.0, None, ALU.mult)
                                v.tensor_scalar(bound[:, d, 1, 1:2], m0, -1.0, None, ALU.mult)
                                ins = v.memset(bound[:, d, 1, 0:1], 0.0)
                            else:
                                v.tensor_scalar(bound[:, d, 1, 1:CH - 1], bc[:, 2:CH, edge], -1.0, None, ALU.mult)
                                v.tensor_scalar(bound[:, d, 1, CH - 1:CH], m0, -1.0, None, ALU.mult)
                                ins = v.memset(bound[:, d, 1, 0:1], 0.0)
                        link(ins)
                        for d in range(2):
                            r = 32 * d + h
                            v.tensor_tensor(bound[:, d, 2, :], bcol[:, :, r], bound[:, d, 0, :], ALU.add)
                            ins = v.tensor_tensor(bound[:, d, 3, :], bound[:, d, 0, :], bound[:, d, 1, :], ALU.add)
                        ins.then_inc(arg_ready, 1)
                        v.wait_ge(exp_ready, h + 1)
                        v.wait_ge(score_full, h + 1)
                        for d in range(2):
                            ins = v.tensor_tensor(W[:, d, :, :], W[:, d, :, :], chunks(0), ALU.mult)
                        ins.then_inc(p_ready, 1)
                        v.wait_ge(state_in, 64 * (h + 1))
                        if h > 0:
                            v.wait_ge(state_out, 64 * h)
                        for d in range(2):
                            v.wait_ge(ds_full, 2 * h + d + 1)
                            ins = v.tensor_copy(Cout[:, d, :], AT[:, 0, 0:DV + 1])
                            if d == 1:
                                ins.then_inc(out_staged, 1)
                            for n in range(1, 4):
                                c = n if d == 0 else CH - n
                                ins = (v.scalar_tensor_tensor(Cst[:, d, n, :], Cst[:, d, n - 1, :],
                                                            wsdec[:, d, 1, c:c + 1], AT[:, n, 0:DV + 1],
                                                            ALU.mult, ALU.add))
                                if n < 3:
                                    link(ins)
                            ins.then_inc(st_ready, 1)
                        for c in range(CH):
                            b = 2 * (c % 2)
                            v.wait_ge(o_full, CH * h + c + 1)
                            den = AT[:, b:b + 2, DV]
                            link(v.scalar_tensor_tensor(dn[:, :], den, -1.0, eqcol[:, c, h:h + 33:32], ALU.mult, ALU.max))
                            link(v.tensor_tensor(dn[:, :], den, dn[:, :], ALU.max))
                            link(v.reciprocal(dn[:, :], dn[:, :]))
                            link(v.tensor_scalar(hn[:, c, :], AT[:, b, 0:DV], dn[:, 0:1], None, ALU.mult))
                            v.scalar_tensor_tensor(hn[:, c, :], AT[:, b + 1, 0:DV], dn[:, 1:2], hn[:, c, :],
                                                   ALU.mult, ALU.add).then_inc(o_free, 1)
                            v.wait_ge(o_free, CH * h + c + 1)
                            ins = v.bn_stats(stats[:, c, :], hn[:, c, :])
                        link(ins)
                        head_tail(2 * h, hh, norm_col + 2 * h, EVACS_BEFORE_ML + 9 * (h // 2) + 8 + hh, False)
                else:
                    ropn, scnt, dcnt, ocnt, scount, gcount, swn = (Tally() for _ in range(7))
                    scnt.n = ocnt.n = A_HEADS
                    dcnt.n = 2 * A_HEADS
                    ocnt.n = CH * A_HEADS
                    gcount.n = EVACS_BEFORE_RET
                    sin_n, sout_n = Tally(), Tally()
                    sout_n.n = 64 * A_HEADS
                    heads = Tally()
                    with loop(v, GROUPS[1], own=(own, 9), hd=(hd, 2), sc=(scnt, 2), dc=(dcnt, 2), oc=(ocnt, 2),
                              gc=(gcount, 9), sw=(swn, 64), si=(sin_n, 64), so=(sout_n, 64)) as g:
                        v.wait_ge(swap_in, swn.add(64))
                        cos = rope[:, 0:SAMPLE].unsqueeze(1).to_broadcast([P, 4, SAMPLE])
                        sin = rope[:, SAMPLE:].unsqueeze(1).to_broadcast([P, 4, SAMPLE])
                        v.tensor_tensor(swapped[:, :, :], swapped[:, :, :], sin, ALU.mult)
                        link(v.tensor_tensor(qk[:, :, PROMPT:TOK], qk[:, :, PROMPT:TOK], cos, ALU.mult))
                        v.tensor_tensor(qk[:, :, PROMPT:TOK], qk[:, :, PROMPT:TOK], swapped[:, :, :],
                                        ALU.add).then_inc(rope_ready, 1)
                        for hh in range(2):
                            head = g * 2 + hh
                            hd.add()
                            v.wait_ge(score_full, scnt.add())
                            v.tensor_tensor(Pm[:, :, :], chunks(0), Dm[:, ds(head, 1), :].to_broadcast([P, CH, P]),
                                            ALU.mult).then_inc(p_ready, 1)
                            v.wait_ge(ds_full, dcnt.add())
                            v.wait_ge(ret_state_in, sin_n.add(32))
                            v.wait_ge(state_out, sout_n.now())
                            sout_n.add(32)
                            for d in range(2):
                                ins = v.tensor_copy(Sout[:, d, :], ATf[:, d * 1024:d * 1024 + DV])
                            ins.then_inc(out_staged, 1)
                            for n in range(1, 4):
                                for d in range(2):
                                    at = d * 1024 + n * DV
                                    ins = v.scalar_tensor_tensor(Sst[:, d, n, :], Sst[:, d, n - 1, :],
                                                                 cdcol[:, d, ds(head, 1)],
                                                                 ATf[:, at:at + DV], ALU.mult, ALU.add)
                                if n < 3:
                                    link(ins)
                            ins.then_inc(st_ready, 1)
                            v.wait_ge(o_full, ocnt.add())
                            for c in range(CH):
                                ins = v.bn_stats(stats[:, c, :], ATf[:, c * DV:(c + 1) * DV])
                            link(ins)
                            gcount.add(8 if hh == 0 else 1)
                            head_tail(g * 4 + 2 * hh, hh, g * 4 + (norm_col + 2 * hh), gcount.now(), True)
                    pjn.add(18 * GROUPS[1])
                    for s in range(SLOTS):
                        outs[s].add(GROUPS[1] * (4, 4, CH, CH)[s])
                if layer == 0:
                    y_copies(2, [0, 0, 1, 1], (2, 2, 0, 0))
                else:
                    y_copies(2, [0, 1, 2, 3], (1, 1, 1, 1))
                norm_rstd()
                scale_tiles(uT, post_a[:, 0], y_scaled)
                norm_rstd()
                scale_tiles(xT, pre_a[:, 1], scaled_ready)

                def taps(t, b):
                    s = pjn.n % 2
                    pjn.add()
                    v.wait_ge(conv_begun, cvn.add())
                    pieces = ((0, 0, 1, PROMPT), (0, PROMPT, (HALF - PROMPT) // GRID_W, GRID_W),
                              (1, 0, HALF // GRID_W, GRID_W))
                    for tap in (0, 2):
                        scalar = cols[:, ds(t + COL_CONV + (layer * 3 + tap) * 2 * FT + b * FT, 1)]
                        for bank, lo, n, w in pieces:
                            z = PJ[:, s, bank, lo:lo + n * w].rearrange("p (r w) -> p r w", w=w)
                            o = conv[:, b, bank * HALF + lo:bank * HALF + lo + n * w].rearrange("p (r w) -> p r w", w=w)
                            o, z = (o[:, :, 1:w], z[:, :, 0:w - 1]) if tap == 0 else (o[:, :, 0:w - 1], z[:, :, 1:w])
                            ins = v.scalar_tensor_tensor(o, z, scalar, o, ALU.mult, ALU.add)
                        if tap == 0:
                            link(ins)
                    ins.then_inc(pj_free[s], 1)
                    free[s].add()
                    return s

                def ffn_pair(t):
                    taps(t, 0)
                    s = taps(t, 1)
                    v.wait_ge(pj_free[s], free[s].now())
                    v.wait_ge(gelu_ready, gen.add())
                    v.tensor_tensor(act[:, ds(t, 1), :].rearrange("p a t -> p (a t)"), gel[:, :], conv[:, 1, :],
                                    ALU.mult).then_inc(act_ready, 1)

                free[0].n = free[1].n = pjn.n // 2
                assert pjn.n % 2 == 0
                with loop(v, FT // 4, own=(own, 8), pjn=(pjn, 8), cv=(cvn, 8), ge=(gen, 4), f0=(free[0], 4),
                          f1=(free[1], 4)) as i:
                    for j in range(4):
                        ffn_pair(i * 4 + j)
                for j in range(FT % 4):
                    ffn_pair(FT // 4 * 4 + j)
                for s in range(SLOTS):
                    outs[s].add(2 * (FT // 4 + int(s < FT % 4)))
                for s in (0, 2):
                    outs[s].add(4)
                y_copies(KT // 2, [1, 3], (0, 1, 0, 1))
                norm_rstd()
                scale_tiles(uT, post_a[:, 1], y_scaled)

            for c in range(CH):
                s = pj_turned()
                v.tensor_copy(xin[:, c, :], PJ[:, s, :, :].rearrange("p b n -> p (b n)")).then_inc(out_ready, 1)

        @block.tensor
        def _(pe):
            full = [Tally() for _ in range(SLOTS)]
            pjn, free = Tally(), [Tally(), Tally()]
            stn, un, hrn = Tally(), Tally(), Tally()
            scn, stc, qzn, hnn, ron = (Tally() for _ in range(5))

            def per(*uses):
                return {f"s{s}": (full[s], n) for s, n in enumerate(uses)}

            def unit(slot, dmas=1):
                full[slot].add(dmas)
                pe.wait_ge(ring_full[slot], full[slot].now() * 16)

            def emptied():
                for s in range(2):
                    pe.wait_ge(pj_free[s], free[s].now())

            def pj_slot():
                s = pjn.n % 2
                pjn.add()
                pe.wait_ge(pj_free[s], free[s].now())
                free[s].add()
                return s

            def project(weights, source, kts, start=True, stop=True, s=None):
                for k in range(kts):
                    for b in range(2):
                        ins = pe.matmul(PJ[:, s, b, 0:HALF], weights(k), source(k)[:, b * HALF:(b + 1) * HALF],
                                        start=(start and k == 0), stop=(stop and k == kts - 1))
                return ins

            def norm_stat():
                pe.wait_ge(sq_added, 8 * stn.now() + 8)
                stn.add()
                for b in range(2):
                    ins = pe.matmul(AT[:, 2 + b, 0:HALF], mean_w, sqsum[:, b * HALF:(b + 1) * HALF], start=True, stop=True)
                ins.then_inc(stat_full, 1)

            pe.wait_ge(const_in, 16)
            pe.wait_ge(rows_in, 160)
            s = pj_slot()
            for n in range(5):
                ins = pe.transpose(PJ[:, s, n // 4, (n % 4) * P:(n % 4 + 1) * P], rows[:, n, :], ident)
            ins.then_inc(turned, 1)
            pe.wait_ge(x_in, 32)
            for c in range(CH):
                s = pj_slot()
                for k in range(KT):
                    ins = pe.transpose(PJ[:, s, k // 4, (k % 4) * P:(k % 4 + 1) * P], xin[:, c, k * P:(k + 1) * P], ident)
                ins.then_inc(turned, 1)

            for layer in range(DEPTH):
                pe.wait_ge(silu_ready, 2)
                with loop(pe, 6, **per(1, 1, 1, 1)) as i:
                    for j in range(4):
                        unit(j)
                        w = ring[j][:, :].rearrange("p (k m) -> p k m", k=KT)
                        for m in range(2):
                            for k in range(KT):
                                ins = pe.matmul(AT[:, 0, ds(i * 16 + (j * 4 + m * 2), 2)], w[:, k, m * P:(m + 1) * P],
                                                silu_c[:, k, :], start=(k == 0), stop=(k == KT - 1))
                        ins.then_inc(made[j], 1)
                norm_stat()
                un.add(KT)
                pe.wait_ge(u_ready, un.now())

                if layer == 0:
                    pe.wait_ge(ml_in, 16 * 11)
                    for kind in range(2):
                        s = pj_slot()
                        for k in range(KT):
                            for b in range(2):
                                ins = pe.matmul(PJ[0:64, s, b, 0:HALF], wg[:, k, kind, :],
                                                uT[:, k, b * HALF:(b + 1) * HALF], start=(k == 0), stop=(k == KT - 1))
                        ins.then_inc(turned, 1)
                    pe.wait_ge(rowb_ready, 1)
                    for n, row in enumerate((ri, rf)):
                        for c in range(CH):
                            ins = pe.transpose(AT[:, n, c * 64:(c + 1) * 64], row[:, c * P:(c + 1) * P], ident[0:64, 0:64])
                    ins.then_inc(rowT_full, 1)
                    pe.wait_ge(bcol_ready, 2)

                def wide(slot, m):
                    w = ring[slot][:, :].rearrange("p (k m) -> p k m", k=KT)
                    return lambda k: w[:, k, m * P:(m + 1) * P]

                def gate(t):
                    if t % 2 == 0:
                        unit(t // 2)
                    s = pj_slot()
                    ins = project(wide(t // 2, t % 2), lambda k: uT[:, k, :], KT, s=s)
                    ins.then_inc(made[t // 2], 1)

                def qkv():
                    for u in range(2):
                        unit(u)
                        for m in range(2):
                            s = pj_slot()
                            project(wide(u, m), lambda k: uT[:, k, :], KT, s=s).then_inc(made[u], 1)
                    for hh in range(2):
                        unit(2 + hh)
                        w = ring[2 + hh][:, :].rearrange("p (k m) -> p k m", k=KT)
                        for c in range(CH):
                            s = pj_slot()
                            for k in range(KT):
                                ins = pe.matmul(PJ[:, s, 0, 0:DV], uT[:, k, c * P:(c + 1) * P], w[:, k, :],
                                                start=(k == 0), stop=(k == KT - 1))
                            ins.then_inc(made[2 + hh], 1)
                    emptied()

                def scores(hh):
                    for c in range(CH):
                        pe.matmul(chunks(0)[:, c, :], qk[:, 2 + hh, c * P:(c + 1) * P], qk[:, hh, c * P:(c + 1) * P],
                                  start=True, stop=True)
                    for c in range(CH):
                        ins = pe.transpose(chunks(2)[:, c, :], qk[:, 2 + hh, c * P:(c + 1) * P], ident)
                    ins.then_inc(score_full, 1)

                def turn_back():
                    pe.wait_ge(hn_ready, hnn.add())
                    for vh in range(2):
                        for c in range(CH):
                            ins = pe.transpose(chunks(2 * vh)[:, c, :], hn[:, c, vh * P:(vh + 1) * P], ident)
                    ins.then_inc(ht_full, 1)

                if layer == 0:
                    for g in range(GROUPS[0]):
                        qkv()
                        for hh in range(2):
                            h = 2 * g + hh
                            pe.wait_ge(h_ready, h)
                            for d in range(2):
                                sel = mlc[0:64, (2 + 4 * d + h) * P:(3 + 4 * d + h) * P]
                                pe.matmul(ATf[:, 1024 * d:1024 * d + 512], sel, rM[:, 0:512], start=True, stop=True)
                                ins = pe.matmul(ATf[:, 1024 * d + 512:1024 * d + TOK + 1], sel, rM[:, 512:TOK + 1],
                                                start=True, stop=True)
                            ins.then_inc(bc_full, 1)
                            if hh == 0:
                                gate(0)
                            pe.wait_ge(exp_ready, h + 1)
                            scores(hh)
                            if hh == 0:
                                gate(1)
                            pe.wait_ge(p_ready, h + 1)
                            pe.wait_ge(kz_ready, h + 1)
                            pe.wait_ge(ml_zero, 5)
                            for d in range(2):
                                pe.wait_ge(st_ready, 2 * h + d)
                                for n in range(4):
                                    c = n if d == 0 or n == 0 else CH - n
                                    ins = pe.matmul(AT[:, n, 0:DV + 1], kz[d][:, c, :], vt[:, c, hh, :], start=True, stop=True)
                                ins.then_inc(ds_full, 1)
                            if hh == 0:
                                gate(2)
                            pe.wait_ge(st_ready, 2 * h + 2)
                            pe.wait_ge(qz_ready, 2 * h + 2)
                            for c in range(CH):
                                if c >= 2:
                                    pe.wait_ge(o_free, CH * h + c - 1)
                                for d in range(2):
                                    o = AT[:, 2 * (c % 2) + d, 0:DV + 1]
                                    ins = pe.matmul(o, W[:, d, c, :], vt[:, c, hh, :], start=True, stop=(c == 0))
                                    if c:
                                        ins = pe.matmul(o, qz[d][:, c - 1, :], Cst[:, d, c - 1 if d == 0 else CH - 1 - c, :],
                                                        start=False, stop=True)
                                ins.then_inc(o_full, 1)
                            if hh == 0:
                                gate(3)
                            turn_back()
                else:
                    hrn.n = scn.n = A_HEADS
                    stc.n, qzn.n = 2 * A_HEADS, 2 * A_HEADS
                    pe.wait_ge(ml_zero, 6)
                    with loop(pe, GROUPS[1], pjn=(pjn, 18), f0=(free[0], 9), f1=(free[1], 9), h=(hrn, 2), sc=(scn, 2),
                              st=(stc, 2), qz=(qzn, 4), hn=(hnn, 2), ro=(ron, 1), **per(2, 2, 1, 1)) as g:
                        qkv()
                        pe.wait_ge(rope_ready, ron.add())
                        for hh in range(2):
                            pe.wait_ge(h_ready, hrn.now())
                            hrn.add()
                            scores(hh)
                            gate(0 if hh == 0 else 3)
                            pe.wait_ge(p_ready, scn.add())
                            pe.wait_ge(kz_ready, scn.now())
                            for d in range(2):
                                for n in range(4):
                                    c = n if d == 0 or n == 0 else CH - n
                                    at = d * 1024 + n * DV
                                    ins = pe.matmul(ATf[:, at:at + DV], kz[d][:, c, :], vt[:, c, hh, 0:DV],
                                                    start=True, stop=True)
                            ins.then_inc(ds_full, 1)
                            if hh == 0:
                                gate(1)
                            pe.wait_ge(st_ready, stc.add())
                            pe.wait_ge(qz_ready, qzn.add(2))
                            for c in range(CH):
                                o = ATf[:, c * DV:(c + 1) * DV]
                                ins = pe.matmul(o, Pm[:, c, :], vt[:, c, hh, 0:DV], start=True, stop=(c == 0))
                                if c:
                                    for d in range(2):
                                        ins = pe.matmul(o, qz[d][:, c - 1, :], Sst[:, d, c - 1 if d == 0 else CH - 1 - c, :],
                                                        start=False, stop=(d == 1))
                            ins.then_inc(o_full, 1)
                            if hh == 0:
                                gate(2)
                            turn_back()
                pe.wait_ge(h_ready, [A_HEADS, A_HEADS + B_HEADS][layer])

                n, tiles, kts = OUT_UNITS[layer], OUT_TILES[layer], HV[layer] // P
                with loop(pe, 2, pjn=(pjn, 4), f0=(free[0], 2), f1=(free[1], 2), **per(*[int(s < n) for s in range(4)])):
                    for j in range(n):
                        unit(j)
                        w = ring[j][:, 0:kts * tiles * P].rearrange("p (k m) -> p k m", k=kts)
                        for m in range(tiles):
                            s = pj_slot()
                            project(lambda k: w[:, k, m * P:(m + 1) * P], lambda k: hT[:, k, :], kts, s=s
                                    ).then_inc(made[j], 1)
                norm_stat()
                norm_stat()
                un.add(KT)
                pe.wait_ge(u_ready, un.now())

                def up_pair(j):
                    unit(j, dmas=2)
                    w = ring[j][:, :].rearrange("p (b k m) -> p b k m", k=KT, b=2)
                    for b in range(2):
                        s = pj_slot()
                        project(lambda k: w[:, b, k, :], lambda k: uT[:, k, :], KT, s=s).then_inc(made[j], 1)

                with loop(pe, FT // 4, pjn=(pjn, 8), f0=(free[0], 4), f1=(free[1], 4), **per(2, 2, 2, 2)):
                    for j in range(4):
                        up_pair(j)
                for j in range(FT % 4):
                    up_pair(j)
                pe.wait_ge(act_ready, FT * (layer + 1))
                with loop(pe, KT // 2, pjn=(pjn, 2), f0=(free[0], 1), f1=(free[1], 1), **per(1, 1, 1, 1)):
                    for j in range(4):
                        unit(j)
                        w = ring[j][:, 0:FH * P].rearrange("p (k m) -> p k m", k=FH)
                        if j % 2 == 0:
                            s = pj_slot()
                        ins = project(lambda k: w[:, k, :], lambda k: act[:, (j % 2) * FH + k, :], FH,
                                      start=(j % 2 == 0), stop=(j % 2 == 1), s=s)
                        ins.then_inc(made[j], 1)
                norm_stat()

            pe.wait_ge(x_added, 4 * KT)
            emptied()
            for c in range(CH):
                s = c % 2
                if c >= 2:
                    pe.wait_ge(out_ready, c - 1)
                for k in range(KT):
                    ins = pe.transpose(PJ[:, s, k // 4, (k % 4) * P:(k % 4 + 1) * P], xT[:, k, c * P:(c + 1) * P], ident)
                ins.then_inc(turned, 1)


_INS = ['x_prompt', 'x_sample', 'state_mlstm_C', 'state_mlstm_n', 'state_mlstm_m', 'state_ret_S', 'c', 'c_ctx',
        'norm_gain', 'ada_w', 'ada_b', 'ml_w_in', 'ml_b_gate', 'ml_norm', 'ml_w_out', 'ret_w_in', 'ret_decay',
        'ret_norm', 'ret_w_out', 'ffn_w_up', 'ffn_conv', 'ffn_conv_b', 'ffn_w_down']
_OUTS = [(1, PROMPT, D_MODEL), (1, SAMPLE, D_MODEL), (1, 1, 2, A_HEADS, DK, DV), (1, 1, 2, A_HEADS, DK),
         (1, 1, 2, A_HEADS), (1, 1, 2, B_HEADS, DK, DV)]


def shape_constants():
    one = np.arange(P)
    common = np.concatenate([np.eye(P), np.full((P, P), 1.0 / D_MODEL)], axis=1)
    s, l = one[:, None], one[None, :]
    ml = np.zeros((P, 10 * P))
    ml[:, 0:P] = np.where(s <= l, 0.0, MASKED)
    ml[:, P:2 * P] = np.where(s >= l, 0.0, MASKED)
    for d in range(2):
        for h in range(A_HEADS):
            at = (2 + 4 * d + h) * P
            ml[32 * d + h, at:at + P] = -1.0
    ret = np.zeros((P, TOK + 2 * SAMPLE))
    ret[:, 0:P] = np.maximum(l - s, 0)
    ret[:, P:2 * P] = np.maximum(s - l, 0)
    ret[:, 2 * P:3 * P] = l + 1
    ret[:, 3 * P:4 * P] = P - l
    ret[:, 4 * P] = P - 1 - one
    ret[:, 4 * P + 1] = one
    quarter = DK // 4
    inv = (10000.0 ** (-np.arange(quarter, dtype=np.float32) / quarter)).astype(np.float32)
    t = np.arange(SAMPLE)
    for half, pos in enumerate((t // GRID_W, t % GRID_W)):
        ang = (pos.astype(np.float32)[None, :] * inv[:, None]).astype(np.float32).astype(np.float64)
        for part, sign in enumerate((-1.0, 1.0)):
            r = half * 2 * quarter + part * quarter
            ret[r:r + quarter, TOK:TOK + SAMPLE] = np.cos(ang)
            ret[r:r + quarter, TOK + SAMPLE:] = sign * np.sin(ang)
    return {n: a.astype(np.float32) for n, a in (("common", common), ("ml", ml), ("ret", ret))}


def kernel(**inputs):
    import concourse.bacc as bacc
    from concourse.bass_utils import run_bass_kernel_spmd

    nc = bacc.Bacc("TRN2", target_bir_lowering=False, num_devices=1)
    given = {name: np.ascontiguousarray(inputs[name]) for name in _INS}
    arrays, args = {}, []
    for name, a in {**given, **{"k_" + n: a for n, a in shape_constants().items()}}.items():
        arrays[f"in_{name}"] = a
        args.append(nc.dram_tensor(f"in_{name}", a.shape, mybir.dt.from_np(a.dtype), kind="ExternalInput").ap())
    for i, shape in enumerate(_OUTS):
        args.append(nc.dram_tensor(f"out_{i}", shape, F32, kind="ExternalOutput").ap())
    hybrid_step(nc, *args)
    r = run_bass_kernel_spmd(nc, [arrays], core_ids=[0])
    return tuple(r.results[0][f"out_{i}"] for i in range(len(_OUTS)))
```

```python
from contextlib import ExitStack, contextmanager
import math

import numpy as np
import concourse.bass as bass
from concourse import mybir

F32 = mybir.dt.float32
F32R = mybir.dt.float32r
ACT = mybir.ActivationFunctionType
ALU = mybir.AluOpType
ds = bass.ds

P = 128
D_MODEL = 1024
KT = D_MODEL // P
PROMPT = 128
SAMPLE = 512
TOK = PROMPT + SAMPLE
HALF = TOK // 2
CH = TOK // P
GRID_W = 64
DEPTH = 2
D_FF = 2816
FT = D_FF // P
HALVES = (FT // 2 + 1, FT // 2 - 1)
A_HEADS, B_HEADS = 4, 8
DK, DV = 128, 256
EPS = 1e-6
SLOTS = 4
UNIT = 2048
MASKED = -1e30
COL_GAIN = 0
COL_CCTX = 64
COL_C = 72
COL_MLN = 80
COL_RETN = 88
COL_ADAB = 128
COL_CONV = 256
COL_CONVB = 256 + DEPTH * 3 * 2 * FT
COLS = 5 * P


class Tally:

    def __init__(self):
        self.n, self.turn, self.per = 0, None, 0

    def now(self, back=0):
        n = self.n - back
        return n if self.turn is None else self.turn * self.per + n

    def add(self, k=1):
        self.n += k
        return self.now()


@contextmanager
def loop(eng, turns, **per_turn):
    starts = {}
    with eng.Fori(0, turns) as i:
        for name, (tally, per) in per_turn.items():
            starts[name] = tally.n
            tally.turn, tally.per = i, per
        yield i
    for name, (tally, per) in per_turn.items():
        assert tally.n - starts[name] == per, (name, tally.n - starts[name], per)
        tally.n = starts[name] + per * turns
        tally.turn = None


def hybrid_step(nc, x_prompt, x_sample, st_C, st_n, st_m, st_S, c_lat, c_ctx, norm_gain, ada_w, ada_b,
                ml_w_in, ml_b_gate, ml_norm, ml_w_out, ret_w_in, ret_decay, ret_norm, ret_w_out,
                ffn_w_up, ffn_conv, ffn_conv_b, ffn_w_down, k_common, k_ml, k_ret,
                y_prompt, y_sample, new_C, new_n, new_m, new_S, x_saved_dram):
    with ExitStack() as ctx:
        def sb(name, shape, stack=ctx, dt=F32):
            return stack.enter_context(nc.sbuf_tensor(name, shape, dt))

        def sem(name):
            return ctx.enter_context(nc.semaphore(name))

        xT = sb("xT", [P, KT, TOK])
        uT = sb("uT", [P, KT, TOK])
        common = sb("common", [P, 3 * P])
        cols = sb("cols", [P, COLS])
        silu_c = sb("silu_c", [P, KT, 2])
        mod = sb("mod", [P, DEPTH, 48, 2])
        pre_a = sb("pre_a", [P, 2, KT, 2])
        post_a = sb("post_a", [P, 2, KT, 2])
        sq = sb("sq", [P, 2, TOK])
        sqsum = sb("sqsum", [P, TOK])
        tok_rstd = sb("tok_rstd", [P, CH])
        diag = sb("diag", [P, CH, P])
        ada_mem = sb("ada_mem", [P, SLOTS, 256])
        ada_rows = ada_mem[0:2, :, :]
        eps = sb("eps", [P, 1])
        wait_here = sb("wait_here", [P, 1])
        ident, mean_w, ones = common[:, 0:P], common[:, P:P + 1], common[:, 2 * P:3 * P]

        u_high = sb("u_high", [P, KT, TOK], dt=F32R)
        u_low = sb("u_low", [P, KT, TOK], dt=F32R)
        w_high = [sb(f"w_high{s}", [P, UNIT], dt=F32R) for s in range(2)]
        ring, ring_low = [], []
        mixer = ExitStack()
        for pair, stack in (((0, 1), ctx), ((2, 3), mixer)):
            with ExitStack() as place:
                ring += [sb(f"ring{s}", [P, UNIT], place) for s in pair]
            ring_low += [sb(f"ring_low{s}", [P, UNIT], stack, F32R) for s in pair]

        def mb(name, shape):
            return sb(name, shape, mixer)

        qk, gt = uT[:, 0:4, :], uT[:, 4:8, :]
        hT = mb("hT", [P, 2 * B_HEADS, TOK])
        xflat = xT[:, :, :].rearrange("p k t -> p (k t)")
        vt_n, kz_n, qz_n = CH * 2 * (DV + 1), CH * DK, (CH - 1) * P
        vt = xflat[:, 0:vt_n].rearrange("p (c h v) -> p c h v", c=CH, h=2)
        kzf, kzb = (xflat[:, vt_n + d * kz_n:vt_n + (d + 1) * kz_n].rearrange("p (c k) -> p c k", k=DK) for d in range(2))
        qz_at = vt_n + 2 * kz_n
        qzf, qzb = (xflat[:, qz_at + d * qz_n:qz_at + (d + 1) * qz_n].rearrange("p (c l) -> p c l", l=P) for d in range(2))
        hn = sq[:, :, :].rearrange("p a t -> p (a t)").rearrange("p (c v) -> p c v", v=DV)
        stats = mb("stats", [P, CH, 6])
        mv = mb("mv", [P, CH, 2])
        hstd = mb("hstd", [P, CH])
        kz, qz = [kzf, kzb], [qzf, qzb]

        ml_mem = ExitStack()
        mlc = hT[:, 8:10, :].rearrange("p a t -> p (a t)")
        wg = hT[:, 10:12, :].rearrange("p a t -> p (a t)")[:, 0:KT * 128].rearrange("p (k b r) -> p k b r", k=KT, b=2)
        rone, rt = hT[0:64, 12, :], hT[0:64, 13, :]
        winter = hT[:, 10:12, :].rearrange("p a t -> p (a t)")[:, 0:2 * (CH - 1) * P].rearrange(
            "p (d c l) -> p d c l", d=2, l=P)
        Cout = hT[:, 12, 0:2 * (DV + 1)].rearrange("p (d v) -> p d v", d=2)
        W = hT[:, 14:16, :].rearrange("p d (c l) -> p d c l", l=P)
        rA = rt
        gbias = sb("gbias", [64, 2], ml_mem)
        m0col = sb("m0col", [64, 1], ml_mem)
        ri = sb("ri", [64, TOK], ml_mem)
        rf = sb("rf", [64, TOK], ml_mem)
        rM = sb("rM", [64, TOK + 1], ml_mem)
        bcol = sb("bcol", [P, CH, 64], ml_mem)
        eqcol = sb("eqcol", [P, CH, 64], ml_mem)
        bound = sb("bound", [P, 2, 4, CH], ml_mem)
        wsdec = sb("wsdec", [P, 2, 2, CH], ml_mem)
        Cst = sb("Cst", [P, 2, 4, DV + 1], ml_mem)
        dn = sb("dn", [P, 2], ml_mem)
        ml_mem.close()

        ret_mem = ExitStack()
        rope = hT[:, 14:16, :].rearrange("p a t -> p (a t)")[:, 0:2 * SAMPLE]
        Dm = ada_mem[:, :, :].rearrange("p s m -> p (s m)").rearrange("p (h l) -> p h l", l=P)
        Pm = diag
        Sout = sqsum[:, 0:2 * DV].rearrange("p (d v) -> p d v", d=2)
        dcy = sb("dcy", [P, 6, 16], ret_mem)
        zcol = sb("zcol", [P, 2, B_HEADS], ret_mem)
        cdcol = sb("cdcol", [P, 2, B_HEADS], ret_mem)
        XI = sb("XI", [P, 2, B_HEADS, P], ret_mem)
        Sst = sb("Sst", [P, 2, 4, DV], ret_mem)
        swapped = Sst[:, :, :, :].rearrange("p d s v -> p (d s v)").rearrange("p (q t) -> p q t", t=SAMPLE)
        ret_mem.close()
        mixer.close()

        ffn_mem = ExitStack()
        act_high = sb("act_high", [P, HALVES[0], TOK], ffn_mem, F32R)
        w_low = [sb(f"w_low{s}", [P, UNIT], ffn_mem, F32R) for s in range(2)]
        act_low = sb("act_low", [P, HALVES[0], TOK], ffn_mem, F32R)
        conv = sq
        ffn_mem.close()

        io_mem = ExitStack()
        for s in range(2, SLOTS):
            sb(f"ring_hole{s}", [P, UNIT], io_mem)
        rows = sb("rows", [P, 5, P], io_mem)
        xin = sb("xin", [P, CH, D_MODEL], io_mem)
        io_mem.close()
        krt = hT[:, 0, :]

        PJ = ctx.enter_context(nc.psum_tensor("PJ", [P, 2, 2, 512], F32))
        AT = ctx.enter_context(nc.psum_tensor("AT", [P, 4, 512], F32))
        ATf = AT[:, :, :].rearrange("p b n -> p (b n)")

        def chunks(bank):
            return ATf[:, bank * 512:bank * 512 + TOK].rearrange("p (c l) -> p c l", l=P)

        mean_sq = ATf[:, 1536 + 256:1536 + 256 + CH]
        rstd = ATf[:, 1024:1024 + TOK]

        ring_full = [sem(f"ring_full{s}") for s in range(SLOTS)]
        made = [sem(f"made{s}") for s in range(SLOTS)]
        turned = sem("turned")
        pj_free = [sem("pj_free0"), sem("pj_free1")]
        const_in, rows_in, x_in, rows_zero = sem("const_in"), sem("rows_in"), sem("x_in"), sem("rows_zero")
        h_split, l_split = [sem("h_split0"), sem("h_split1")], [sem("l_split0"), sem("l_split1")]
        uh_ready, ul_ready, acth_ready, ada_row = sem("uh_ready"), sem("ul_ready"), sem("acth_ready"), sem("ada_row")
        prod_ready, ada_done, mod_ready = sem("prod_ready"), sem("ada_done"), sem("mod_ready")
        diag_ready, rstd_full = sem("diag_ready"), sem("rstd_full")
        silu_ready, out_ready = sem("silu_ready"), sem("out_ready")
        sq_ready, sq_added, stat_full = sem("sq_ready"), sem("sq_added"), sem("stat_full")
        std_ready, rstd_ready, sum_zero = sem("std_ready"), sem("rstd_ready"), sem("sum_zero")
        scaled_ready, u_ready, y_scaled, x_added = sem("scaled_ready"), sem("u_ready"), sem("y_scaled"), sem("x_added")
        conv_begun, gelu_ready, act_ready = sem("conv_begun"), sem("gelu_ready"), sem("act_ready")
        rope_ready, swap_in = sem("rope_ready"), sem("swap_in")
        score_full, p_ready, kz_ready, qz_ready = sem("score_full"), sem("p_ready"), sem("kz_ready"), sem("qz_ready")
        state_in, ds_full, st_ready, state_out = sem("state_in"), sem("ds_full"), sem("st_ready"), sem("state_out")
        ret_state_in = sem("ret_state_in")
        o_full, o_free, var_ready, hstd_ready = sem("o_full"), sem("o_free"), sem("var_ready"), sem("hstd_ready")
        hn_ready, ht_full, h_ready = sem("hn_ready"), sem("ht_full"), sem("h_ready")
        ml_in, ml_zero, rowf_ready, rowe_ready, rowb_ready = (sem("ml_in"), sem("ml_zero"), sem("rowf_ready"),
                                                              sem("rowe_ready"), sem("rowb_ready"))
        rowT_full, bc_full, arg_ready, exp_ready, bcol_ready = (sem("rowT_full"), sem("bc_full"), sem("arg_ready"),
                                                                sem("exp_ready"), sem("bcol_ready"))
        ret_in, ret_arg, ret_exp = sem("ret_in"), sem("ret_arg"), sem("ret_exp")
        out_staged, out_done, m_out = sem("out_staged"), sem("out_done"), sem("m_out")
        x_saved, x_back = sem("x_saved"), sem("x_back")
        dve_own, act_own = sem("dve_own"), sem("act_own")

        GROUPS = [A_HEADS // 2, B_HEADS // 2]
        HK = [A_HEADS * DK, B_HEADS * DK]
        HV = [A_HEADS * DV, B_HEADS * DV]
        w_in = [ml_w_in, ret_w_in]
        w_out = [ml_w_out, ret_w_out]
        OUT_TILES = [2, 1]
        OUT_UNITS = [2, 4]
        EVACS_BEFORE_ML = 4
        EVACS_BEFORE_RET = EVACS_BEFORE_ML + 9 * GROUPS[0] + KT // 2 + FT + KT
        ADA_START, ADA_NORM, ADA_ROWS = (0, 0, (0, 1, 2, 3), 2), (0, 8, (0, 1, 2, 3), 2), (0, 16, (2, 3), 4)
        ADA_POST, ADA_PRE, ADA_NEXT = (1, 0, (2, 3), 4), (1, 8, (2, 3), 4), (1, 16, (2, 3), 4)
        FFN = (("up", HALVES[0] // 2, 0), ("down", KT // 2, 0), ("up", HALVES[1] // 2, HALVES[0]),
               ("down", KT // 2, HALVES[0]))
        block = ctx.enter_context(nc.Block())

        @block.sync
        def _(sp):
            uses = [Tally() for _ in range(SLOTS)]

            def load(slot, src, k, width, outputs):
                if uses[slot].turn is not None or uses[slot].n > 0:
                    sp.wait_ge(made[slot], uses[slot].now())
                dst = ring[slot][:, 0:k * width].rearrange("p (k m) -> p k m", k=k)
                sp.dma_start(dst, src.rearrange("(k p) m -> p k m", p=P)).then_inc(ring_full[slot], 16)
                uses[slot].add(outputs)

            def per(*outputs):
                return {f"s{s}": (uses[s], n) for s, n in enumerate(outputs)}

            splits = [Tally(), Tally()]

            def load_ffn(kind, layer, slot, n, first, up, down):
                if kind == "up":
                    dst = ring[slot][:, :].rearrange("p (b k m) -> p b k m", k=KT, b=2)
                    for b in range(2):
                        sp.dma_start(dst[:, b, :, :], up[:, ds(n * P + (first * P + b * D_FF), P)].rearrange(
                            "(k p) m -> p k m", p=P)).then_inc(ring_full[slot], 16)
                else:
                    half = HALVES[int(first > 0)] // 2
                    dst = ring[slot][:, 0:2 * half * P].rearrange("p (b k m) -> p b k m", k=half, b=2)
                    for b in range(2):
                        lo = (first + b * half) * P
                        sp.dma_start(dst[:, b, :, :], down[lo:lo + half * P, ds(n * P, P)].rearrange(
                            "(k p) m -> p k m", p=P)).then_inc(ring_full[slot], 16)

            def load_ada(part):
                layer, first, slots, turns = part
                n = len(slots)
                with loop(sp, turns, **per(*[int(s in slots) for s in range(SLOTS)])) as i:
                    for j, s in enumerate(slots):
                        load(s, ada_w[layer, :, ds((i * n + (first + j)) * 256, 256)], KT, 256, 1)

            for j in range(SLOTS):
                load(j, ada_w[0, :, j * 256:(j + 1) * 256], KT, 256, 1)
            load_ada((0, 4, (0, 1, 2, 3), 1))
            load_ada(ADA_NORM)
            for layer in range(DEPTH):
                hk, hv, w = HK[layer], HV[layer], w_in[layer]

                def load_qk(g):
                    load(0, w[0, :, ds(g * 256, 256)], KT, 256, 2)
                    load(1, w[0, :, ds(g * 256 + hk, 256)], KT, 256, 2)

                def load_v_gates(g):
                    load(2, w[0, :, ds(g * 512 + 2 * hk, 256)], KT, 256, CH)
                    load(3, w[0, :, ds(g * 512 + (2 * hk + 256), 256)], KT, 256, CH)
                    load(0, w[0, :, ds(g * 512 + (2 * hk + hv), 256)], KT, 256, 2)
                    load(1, w[0, :, ds(g * 512 + (2 * hk + hv + 256), 256)], KT, 256, 2)

                if layer == 0:
                    load_qk(0)
                    load_ada(ADA_ROWS)
                    load_v_gates(0)
                    load_qk(1)
                    load_v_gates(1)
                else:
                    with loop(sp, GROUPS[layer], **per(4, 4, CH, CH)) as g:
                        load_qk(g)
                        load_v_gates(g)
                for s in range(2):
                    splits[s].add(3 * GROUPS[layer])
                n, tiles = OUT_UNITS[layer], OUT_TILES[layer]
                with loop(sp, 2, **per(*[tiles * int(s < n) for s in range(4)])) as i:
                    for j in range(n):
                        load(j, w_out[layer][0, :, ds((i * n + j) * (tiles * P), tiles * P)], hv // P, tiles * P, tiles)
                up, down = ffn_w_up[layer], ffn_w_down[layer]
                for kind, turns, first in FFN:
                    start = kind == "up" and first == 0
                    if start:
                        for s in range(2):
                            sp.wait_ge(made[s], uses[s].now())
                            load_ffn(kind, layer, s, s, first, up, down)
                        if layer == 0:
                            load_ada(ADA_POST)
                            load_ada(ADA_PRE)
                    with loop(sp, turns - start, sp0=(splits[0], 1), sp1=(splits[1], 1)) as i:
                        for s in range(2):
                            sp.wait_ge(l_split[s], splits[s].add())
                            load_ffn(kind, layer, s, i * 2 + (s + 2 * start), first, up, down)
                for s in range(2):
                    splits[s].add()
                    uses[s].add(HALVES[0] + HALVES[1] + KT)
                    sp.wait_ge(made[s], uses[s].now())
                if layer == 0:
                    load_ada(ADA_NEXT)

            for c in range(CH):
                sp.wait_ge(out_ready, c + 1)
                sp.dma_start(y_prompt[0] if c == 0 else y_sample[0, (c - 1) * P:c * P, :], xin[:, c, :]
                             ).then_inc(out_done, 16)
            sp.wait_ge(out_done, 16 * CH)
            sp.wait_ge(state_out, 16 * (4 * A_HEADS + 2 * B_HEADS))
            sp.wait_ge(m_out, 32)

        @block.gpsimd
        def _(pool):
            sqn, stn, hd = Tally(), Tally(), Tally()

            def norm_sums(turns, per):
                pool.wait_ge(stat_full, stn.now())
                pool.memset(sqsum[:, :], 0.0).then_inc(sum_zero, 1)
                stn.add()
                pool.wait_ge(sum_zero, stn.now())
                if per is None:
                    for k in range(turns):
                        step_sum(k)
                else:
                    with loop(pool, turns, sq=(sqn, per)) as _:
                        for k in range(per):
                            step_sum(k)

            def step_sum(k):
                pool.wait_ge(sq_ready, sqn.add())
                pool.wait_ge(sq_added, sqn.now(1))
                pool.tensor_tensor(sqsum[:, :], sqsum[:, :], sq[:, k % 2, :], ALU.add).then_inc(sq_added, 1)

            pool.memset(rows[:, :, :], 0.0).then_inc(rows_zero, 1)
            pool.wait_ge(rows_zero, 1)
            pool.dma_start(common[:, :], k_common).then_inc(const_in, 16)
            pool.dma_start(rows[0:64, 0, :], norm_gain.rearrange("l w (t m) -> (l w t) m", m=P)).then_inc(rows_in, 16)
            pool.dma_start(rows[64:72, 0, :], c_ctx.rearrange("(t m) -> t m", m=P)).then_inc(rows_in, 16)
            pool.dma_start(rows[72:80, 0, :], c_lat.rearrange("b (t m) -> (b t) m", m=P)).then_inc(rows_in, 16)
            pool.dma_start(rows[80:88, 0, :], ml_norm.rearrange("a h (t m) -> (a h t) m", m=P)).then_inc(rows_in, 16)
            pool.dma_start(rows[88:104, 0, :], ret_norm.rearrange("a h (t m) -> (a h t) m", m=P)).then_inc(rows_in, 16)
            pool.dma_start(rows[0:96, 1, :], ada_b.rearrange("l (t m) -> (l t) m", m=P)).then_inc(rows_in, 16)
            cr = ffn_conv.rearrange("l w (t m) -> (l w t) m", m=P)
            pool.dma_start(rows[:, 2, :], cr[0:P, :]).then_inc(rows_in, 16)
            pool.dma_start(rows[:, 3, :], cr[P:2 * P, :]).then_inc(rows_in, 16)
            pool.dma_start(rows[0:8, 4, :], cr[2 * P:264, :]).then_inc(rows_in, 16)
            pool.dma_start(rows[8:96, 4, :], ffn_conv_b.rearrange("l (t m) -> (l t) m", m=P)).then_inc(rows_in, 16)
            pool.dma_start(xin[:, 0, :], x_prompt[0]).then_inc(x_in, 16)
            pool.dma_start(xin[:, 1:CH, :], x_sample[0].rearrange("(c p) d -> p c d", p=P)).then_inc(x_in, 16)

            def save_x():
                pool.wait_ge(u_ready, (2 * layer + 1) * KT)
                pool.dma_start(x_saved_dram, xT[:, :, :]).then_inc(x_saved, 16)
                pool.wait_ge(x_saved, 16 * (layer + 1))
                pool.memset(vt[:, :, :, DV:DV + 1], 1.0).then_inc(ml_zero, 1)

            for layer in range(DEPTH):
                if layer == 0:
                    pool.wait_ge(turned, CH + 1)
                    pool.memset(wg[:, :, :, :], 0.0).then_inc(ml_zero, 1)
                    pool.memset(gbias[:, :], 0.0).then_inc(ml_zero, 1)
                    pool.memset(m0col[:, :], 0.0).then_inc(ml_zero, 1)
                    pool.memset(rone[:, :], 1.0).then_inc(ml_zero, 1)
                    pool.wait_ge(ml_zero, 4)
                    with nc.allow_non_contiguous_dma(reason="a few gate columns and biases"):
                        pool.dma_start(mlc[:, :], k_ml).then_inc(ml_in, 16)
                        gw = ml_w_in[0, :, 2 * HK[0] + 2 * HV[0]:].rearrange("(k p) m -> p k m", p=P)
                        for d in range(2):
                            for kind in range(2):
                                s = (2 * d + kind) * A_HEADS
                                pool.dma_start(wg[:, :, kind, 32 * d:32 * d + A_HEADS],
                                               gw[:, :, s:s + A_HEADS]).then_inc(ml_in, 16)
                                pool.dma_start(gbias[32 * d:32 * d + A_HEADS, kind:kind + 1],
                                               ml_b_gate[0, 2 * d + kind, :].unsqueeze(1)).then_inc(ml_in, 16)
                            pool.dma_start(m0col[32 * d:32 * d + A_HEADS, :],
                                           st_m[0, 0, d, :].unsqueeze(1)).then_inc(ml_in, 16)
                    norm_sums(KT, None)
                    save_x()

                    def ml_head(h):
                        hd.add()
                        if h > 0:
                            pool.wait_ge(hn_ready, hd.now(1))
                        for d in range(2):
                            s = 0
                            pool.dma_start(Cst[:, d, s, 0:DV], st_C[0, 0, d, h]).then_inc(state_in, 16)
                            with nc.allow_non_contiguous_dma(reason="normaliser state, one number a partition"):
                                pool.dma_start(Cst[:, d, s, DV:DV + 1],
                                               st_n[0, 0, d, h, :].unsqueeze(1)).then_inc(state_in, 16)
                        pool.wait_ge(exp_ready, h + 1)
                        for d in range(2):
                            pool.tensor_tensor(qz[d][:, :, :].rearrange("p c l -> p (c l)"), qk[:, h % 2, PROMPT:TOK],
                                               winter[:, d, :, :].rearrange("p c l -> p (c l)"),
                                               ALU.mult).then_inc(qz_ready, 1)

                    pool.wait_ge(rowb_ready, 2)
                    with nc.allow_non_contiguous_dma(reason="one number a partition"):
                        for d in range(2):
                            pool.dma_start(new_m[0, 0, d, :].unsqueeze(1), m0col[32 * d:32 * d + A_HEADS, :]
                                           ).then_inc(m_out, 16)
                    for h in range(A_HEADS):
                        ml_head(h)
                else:
                    norm_sums(KT, None)
                    pool.wait_ge(u_ready, (2 * layer + 1) * KT)
                    with nc.allow_non_contiguous_dma(reason="sixteen decay exponents to every partition"):
                        pool.dma_start(dcy[:, 0, :], ret_decay.rearrange("a d h -> a (d h)").to_broadcast(
                            [P, 16])).then_inc(ret_in, 16)
                    pool.dma_start(krt, k_ret[:, 0:TOK]).then_inc(ret_in, 16)
                    pool.dma_start(rope[:, :], k_ret[:, TOK:TOK + 2 * SAMPLE]).then_inc(ret_in, 16)
                    save_x()
                    pool.wait_ge(ret_exp, 3)
                    ropn = Tally()
                    with loop(pool, GROUPS[1], ropn=(ropn, 1), hd=(hd, 2)) as g:
                        pool.wait_ge(rope_ready, ropn.add())
                        for hh in range(2):
                            pool.wait_ge(hn_ready, hd.add() - 1)
                            for d in range(2):
                                pool.tensor_tensor(
                                    qz[d][:, :, :], qk[:, hh, PROMPT:TOK].rearrange("p (c l) -> p c l", l=P),
                                    XI[:, d, ds(g * 2 + hh, 1), :].to_broadcast([P, CH - 1, P]),
                                    ALU.mult).then_inc(qz_ready, 1)
                if layer == 1:
                    pool.wait_ge(state_out, 64 * A_HEADS + 32 * B_HEADS)
                norm_sums(2, 4)
                norm_sums(KT, None)
                norm_sums(KT // 2, 2)

        @block.scalar
        def _(a):
            pjn, sqn, stn, addn, scn, xan = Tally(), Tally(), Tally(), Tally(), Tally(), Tally()
            free, actn, own = [Tally(), Tally()], Tally(), Tally()
            gaten, hd, turnn, prodn = Tally(), Tally(), Tally(), Tally()
            outs = [Tally() for _ in range(SLOTS)]
            landed = [Tally() for _ in range(SLOTS)]
            adan = Tally()

            def link(ins):
                ins.then_inc(act_own, 1)
                a.wait_ge(act_own, own.add())

            def norm_std():
                a.wait_ge(stat_full, stn.add())
                a.activation(tok_rstd[:, :], mean_sq, ACT.Sqrt, bias=eps[:, 0:1]).then_inc(std_ready, 1)

            def square(src, k):
                if sqn.turn is not None or sqn.n >= 2:
                    a.wait_ge(sq_added, sqn.now(1))
                sqn.add()
                a.activation(sq[:, k % 2, :], src, ACT.Square).then_inc(sq_ready, 1)

            def high_weights(s):
                a.wait_ge(ring_full[s], landed[s].add(2) * 16)
                a.wait_ge(made[s], outs[s].now())
                a.activation(w_high[s][:, :], ring[s][:, :], ACT.Copy).then_inc(h_split[s], 1)

            def high_unit(s, before):
                a.wait_ge(ring_full[s], landed[s].add() * 16)
                a.wait_ge(made[before], outs[before].now())
                a.activation(w_high[s % 2][:, :], ring[s][:, :], ACT.Copy).then_inc(h_split[s % 2], 1)

            def ada_row_out(part, n):
                j = n % len(part[2])
                a.wait_ge(made[part[2][j]], outs[part[2][j]].add())
                if n >= len(part[2]):
                    a.wait_ge(ada_done, adan.n + n // len(part[2]))
                a.activation(ada_rows[:, j, :], PJ[0:2, j // 2, j % 2, 0:256], ACT.Copy).then_inc(ada_row, 1)
                if n == len(part[2]) * part[3] - 1:
                    adan.add(part[3])

            def prenorm(which, sub, during_squares=None, during_scaling=None):
                for k in range(KT):
                    if which > 0:
                        a.wait_ge(x_added, xan.add())
                    square(xT[:, k, :], k)
                    if during_squares:
                        ada_row_out(during_squares, k)
                norm_std()
                for k in range(KT):
                    if during_scaling and k:
                        ada_row_out(during_scaling, k - 1)
                    a.wait_ge(scaled_ready, scn.add())
                    for grp, (lo, hi) in enumerate(((0, PROMPT), (PROMPT, TOK))):
                        ins = a.activation(uT[:, k, lo:hi], uT[:, k, lo:hi], ACT.Identity,
                                           bias=mod[:, which // 2, sub * 24 + k, grp:grp + 1])
                    ins.then_inc(u_ready, 1)
                    a.wait_ge(u_ready, which * KT + k + 1)
                    a.activation(u_high[:, k, :], uT[:, k, :], ACT.Copy).then_inc(uh_ready, 1)
                    if k < 2 and sub == 1:
                        high_weights(k)
                    elif k < 2 and which == 2:
                        high_unit(k, k)
                if during_scaling:
                    ada_row_out(during_scaling, KT - 1)

            def pj(slot):
                a.wait_ge(made[slot], outs[slot].add())
                pjn.add()
                free[(pjn.n - 1) % 2].add()
                return (pjn.n - 1) % 2

            def pj_turned():
                a.wait_ge(turned, turnn.add())
                pjn.add()
                free[(pjn.n - 1) % 2].add()
                return (pjn.n - 1) % 2

            def per(*outputs):
                return {f"o{s}": (outs[s], n) for s, n in enumerate(outputs)}

            def y_squares(turns, per):
                with loop(a, turns, sq=(sqn, per), f0=(free[0], per // 2), f1=(free[1], per // 2)) as i:
                    for k in range(per):
                        s = (pjn.n + k) % 2
                        a.wait_ge(pj_free[s], free[s].add())
                        square(uT[:, ds(i * per + k, 1), :].rearrange("p a t -> p (a t)"), k)
                pjn.add(turns * per)
                norm_std()

            a.wait_ge(pj_free[0], 1)
            pjn.add(CH + 1)
            turnn.add(CH + 1)
            for grp, col in ((0, COL_CCTX), (1, COL_C)):
                a.activation(silu_c[:, :, grp:grp + 1], cols[:, col:col + KT].unsqueeze(2), ACT.Silu).then_inc(silu_ready, 1)
            a.wait_ge(pj_free[0], 3)
            a.wait_ge(pj_free[1], 3)
            free[0].n = free[1].n = 3

            for layer in range(DEPTH):
                if layer == 0:
                    for n in range(8):
                        ada_row_out(ADA_START, n)
                    prenorm(0, 0, during_scaling=ADA_NORM)
                else:
                    prenorm(2, 0, during_squares=ADA_NEXT)
                if layer == 0:
                    a.wait_ge(ml_in, 16 * 11)
                    s = pj_turned()
                    a.activation(ri[:, :].rearrange("p (b t) -> p b t", b=2), PJ[0:64, s, :, 0:HALF], ACT.Identity,
                                 bias=gbias[:, 0:1]).then_inc(pj_free[s], 1)
                    s = pj_turned()
                    a.activation(rf[:, :].rearrange("p (b t) -> p b t", b=2), PJ[0:64, s, :, 0:HALF], ACT.Identity,
                                 bias=gbias[:, 1:2]).then_inc(pj_free[s], 1)
                    for s in range(SLOTS):
                        landed[s].add((4, 4, 8, 8)[s])
                    for s in range(2):
                        high_unit(s, s)
                    a.wait_ge(rowf_ready, 1)
                    link(a.activation(rt[:, :], rt[:, :], ACT.Exp, scale=-1.0))
                    a.activation(rt[:, :], rt[:, :], ACT.Ln, bias=1.0).then_inc(rowe_ready, 1)
                    for n in range(8):
                        ada_row_out(ADA_ROWS, n)
                    a.wait_ge(x_saved, 16)
                else:
                    a.wait_ge(x_saved, 32)
                    ln2 = math.log(2.0)
                    a.wait_ge(ret_in, 48)
                    a.activation(dcy[:, 1, :], dcy[:, 0, :], ACT.Exp, scale=-ln2).then_inc(ret_exp, 1)
                    a.wait_ge(ret_arg, 1)
                    a.activation(dcy[:, 3, :], dcy[:, 2, :], ACT.Ln).then_inc(ret_exp, 1)
                    a.wait_ge(ret_arg, 2)
                    link(a.activation(Dm[:, :, :].rearrange("p h l -> p (h l)"), Dm[:, :, :].rearrange("p h l -> p (h l)"), ACT.Exp))
                    a.activation(XI[:, :, :, :].rearrange("p d h l -> p (d h l)"),
                                 XI[:, :, :, :].rearrange("p d h l -> p (d h l)"), ACT.Exp)
                    a.activation(zcol[:, :, :].rearrange("p d h -> p (d h)"), zcol[:, :, :].rearrange("p d h -> p (d h)"), ACT.Exp)
                    a.activation(cdcol[:, :, :].rearrange("p d h -> p (d h)"), dcy[:, 5, :], ACT.Exp,
                                 scale=float(P)).then_inc(ret_exp, 1)
                    a.wait_ge(ret_exp, 3)

                def evac_qkv():
                    for t in range(4):
                        s = pj(t // 2)
                        a.activation(qk[:, t, :].rearrange("p (b t) -> p b t", b=2), PJ[:, s, :, 0:HALF], ACT.Copy,
                                     scale=1.0 if t < 2 else DK ** -0.5).then_inc(pj_free[s], 1)
                        if t == 1:
                            high_unit(2, 0)
                    if layer == 1:
                        a.wait_ge(pj_free[0], free[0].now())
                        a.wait_ge(pj_free[1], free[1].now())
                        for q in range(4):
                            a.dma_start(swapped[32 * q:32 * q + 32, :, :],
                                        qk[32 * (q ^ 1):32 * (q ^ 1) + 32, :, PROMPT:TOK]).then_inc(swap_in, 16)
                    high_unit(3, 1)
                    for t in range(2 * CH):
                        s = pj(2 + t // CH)
                        a.activation(vt[:, t % CH, t // CH, 0:DV], PJ[:, s, 0, 0:DV], ACT.Copy).then_inc(pj_free[s], 1)
                        if t == CH - 1:
                            high_unit(0, 2)

                def evac_gate(t):
                    s = pj(t // 2)
                    if t == 0:
                        a.wait_ge(h_ready, gaten.now())
                        gaten.add(2)
                    a.activation(gt[:, t, :].rearrange("p (b t) -> p b t", b=2), PJ[:, s, :, 0:HALF],
                                 ACT.Sigmoid if layer == 0 else ACT.Silu).then_inc(pj_free[s], 1)

                def head_std():
                    hd.add()
                    a.wait_ge(var_ready, hd.now())
                    a.activation(hstd[:, :], mv[:, :, 1], ACT.Sqrt, bias=eps[:, 0:1]).then_inc(hstd_ready, 1)

                if layer == 0:
                    for g in range(GROUPS[0]):
                        evac_qkv()
                        if g == 0:
                            a.wait_ge(rowT_full, 1)
                            a.activation(eqcol[:, :, :].rearrange("p c r -> p (c r)"), AT[:, 1, 0:CH * 64], ACT.Exp
                                         ).then_inc(bcol_ready, 1)
                        for hh in range(2):
                            h = 2 * g + hh
                            a.wait_ge(arg_ready, h + 1)
                            a.activation(W[:, :, :, :].rearrange("p d c l -> p (d c l)"),
                                         W[:, :, :, :].rearrange("p d c l -> p (d c l)"), ACT.Exp)
                            for d in range(2):
                                bc = chunks(2 * d)
                                for c in range(1, CH):
                                    a.activation(winter[:, d, c - 1, :], bc[:, c, :], ACT.Exp,
                                                 bias=bound[:, d, 1, c:c + 1])
                            a.activation(wsdec[:, :, :, :], bound[:, :, 2:4, :], ACT.Exp).then_inc(exp_ready, 1)
                            if hh == 0:
                                evac_gate(0)
                            a.wait_ge(exp_ready, h + 1)
                            a.wait_ge(score_full, h + 1)
                            for d in range(2):
                                for c in range(CH):
                                    ins = a.activation(kz[d][:, c, :], chunks(2)[:, c, :], ACT.Copy,
                                                       scale=wsdec[:, d, 0, c:c + 1])
                            ins.then_inc(kz_ready, 1)
                            if hh == 0:
                                high_unit(1, 3)
                                evac_gate(1)
                                evac_gate(2)
                            a.wait_ge(out_staged, h + 1)
                            for d in range(2):
                                a.dma_start(new_C[0, 0, d, h], Cout[:, d, 0:DV]).then_inc(state_out, 16)
                                with nc.allow_non_contiguous_dma(reason="one number a partition"):
                                    a.dma_start(new_n[0, 0, d, h, :].unsqueeze(1), Cout[:, d, DV:DV + 1]).then_inc(state_out, 16)
                            head_std()
                            if hh == 0:
                                evac_gate(3)
                            if g + 1 < GROUPS[0]:
                                high_unit(hh, hh)
                else:
                    scn_h, stg, onn = Tally(), Tally(), Tally()
                    scn_h.n, stg.n = A_HEADS, A_HEADS

                    def ret_group(g, last):
                        evac_qkv()
                        for hh in range(2):
                            a.wait_ge(score_full, scn_h.add())
                            for d in range(2):
                                a.dma_start(Sst[:, d, 0, :], st_S[0, 0, d, ds(g * 2 + hh, 1)].rearrange(
                                    "a k v -> (a k) v")).then_inc(ret_state_in, 16)
                            for d in range(2):
                                ins = a.activation(kz[d][:, :, :], chunks(2), ACT.Copy,
                                                   scale=zcol[:, d, ds(g * 2 + hh, 1)])
                            ins.then_inc(kz_ready, 1)
                            if hh == 0:
                                high_unit(1, 3)
                                evac_gate(0)
                                evac_gate(1)
                            else:
                                evac_gate(3)
                            a.wait_ge(out_staged, stg.add())
                            for d in range(2):
                                a.dma_start(new_S[0, 0, d, ds(g * 2 + hh, 1)].rearrange("a k v -> (a k) v"),
                                            Sout[:, d, :]).then_inc(state_out, 16)
                            head_std()
                            if hh == 0:
                                evac_gate(2)
                            if not last:
                                high_unit(hh, hh)

                    with loop(a, GROUPS[1] - 1, pjn=(pjn, 18), f0=(free[0], 9), f1=(free[1], 9), **per(4, 4, CH, CH),
                              gate=(gaten, 2), hd=(hd, 2), sc=(scn_h, 2), stg=(stg, 2),
                              **{f"l{s}": (landed[s], (2, 2, 1, 1)[s]) for s in range(SLOTS)}) as g:
                        ret_group(g, False)
                    ret_group(GROUPS[1] - 1, True)
                a.wait_ge(h_ready, A_HEADS + layer * B_HEADS)
                a.dma_start(xT[:, :, :], x_saved_dram).then_inc(x_back, 16)
                y_squares(2, 4)
                for s in range(OUT_UNITS[layer]):
                    outs[s].add(2 * OUT_TILES[layer])
                for s in range(OUT_UNITS[layer]):
                    landed[s].add(2)
                if layer == 0:
                    prenorm(1, 1, during_squares=ADA_POST, during_scaling=ADA_PRE)
                    for s in (2, 3):
                        landed[s].add(3 * ADA_NEXT[3])
                else:
                    prenorm(3, 1)

                def up_pair(t, tile, s_in):
                    for b in range(2):
                        s = pj(s_in)
                        a.activation(conv[:, b, :].rearrange("p (b t) -> p b t", b=2), PJ[:, s, :, 0:HALF],
                                     ACT.Identity, scale=cols[:, ds(t + (COL_CONV + (layer * 3 + 1) * 2 * FT + b * FT), 1)],
                                     bias=cols[:, ds(t + (COL_CONVB + layer * 2 * FT + b * FT), 1)]).then_inc(conv_begun, 1)
                        if b == 0:
                            a.wait_ge(pj_free[s], free[s].now())
                            a.activation(conv[:, 0, :], conv[:, 0, :], ACT.Gelu_apprx_tanh).then_inc(gelu_ready, 1)
                        else:
                            high_weights(s_in)
                    a.wait_ge(prod_ready, prodn.add())
                    a.activation(act_high[:, ds(tile, 1), :].rearrange("p a t -> p (a t)"), conv[:, 1, :], ACT.Copy
                                 ).then_inc(acth_ready, 1)
                    a.wait_ge(act_ready, actn.add())

                def down_tile(m, s_in, k, half):
                    s = pjn.n % 2
                    pjn.add()
                    outs[s_in].add()
                    free[s].add()
                    if half:
                        a.wait_ge(pj_free[s], free[s].now())
                        square(uT[:, ds(m, 1), :].rearrange("p a t -> p (a t)"), k)

                for kind, turns, first in FFN:
                    out_per = 2 if kind == "up" else 1
                    tallies = dict(pjn=(pjn, 2 * out_per), f0=(free[0], out_per), f1=(free[1], out_per),
                                   o0=(outs[0], out_per), o1=(outs[1], out_per), l0=(landed[0], 2), l1=(landed[1], 2))
                    if kind == "up":
                        with loop(a, turns, **tallies, act=(actn, 2), prod=(prodn, 2)) as i:
                            for j in range(2):
                                up_pair(i * 2 + (first + j), i * 2 + j, j)
                    elif first == 0:
                        with loop(a, turns, **tallies) as i:
                            for j in range(2):
                                down_tile(i * 2 + j, j, j, 0)
                                high_weights(j)
                    else:
                        with loop(a, turns - 1, **tallies, sq=(sqn, 2)) as i:
                            for j in range(2):
                                down_tile(i * 2 + j, j, j, 1)
                                high_weights(j)
                        for j in range(2):
                            down_tile(KT - 2 + j, j, j, 1)
                norm_std()

        @block.vector
        def _(v):
            own, pjn, stn, un, yn, scn = Tally(), Tally(), Tally(), Tally(), Tally(), Tally()
            free, cvn, gen, hd = [Tally(), Tally()], Tally(), Tally(), Tally()
            evac, turnn = Tally(), Tally()
            outs = [Tally() for _ in range(SLOTS)]

            def link(ins):
                ins.then_inc(dve_own, 1)
                v.wait_ge(dve_own, own.add())

            def pj(slot):
                v.wait_ge(made[slot], outs[slot].add())
                pjn.add()
                return (pjn.n - 1) % 2

            def pj_turned():
                v.wait_ge(turned, turnn.add())
                pjn.add()
                return (pjn.n - 1) % 2

            def per(*outputs):
                return {f"o{s}": (outs[s], n) for s, n in enumerate(outputs)}

            def norm_rstd():
                v.wait_ge(std_ready, stn.add())
                link(v.reciprocal(tok_rstd[:, :], tok_rstd[:, :]))
                v.tensor_tensor(diag[:, :, :], ident.unsqueeze(1).to_broadcast([P, CH, P]),
                                tok_rstd[:, :].unsqueeze(2).to_broadcast([P, CH, P]), ALU.mult).then_inc(diag_ready, 1)
                v.wait_ge(rstd_full, stn.now())

            highs = [Tally(), Tally()]

            def low_weights(s):
                v.wait_ge(h_split[s], highs[s].add())
                v.tensor_tensor(w_low[s][:, :], ring[s][:, :], w_high[s][:, :].bitcast(F32), ALU.subtract
                                ).then_inc(l_split[s], 1)

            def low_unit(s):
                v.wait_ge(h_split[s % 2], highs[s % 2].add())
                v.tensor_tensor(ring_low[s][:, :], ring[s][:, :], w_high[s % 2][:, :].bitcast(F32), ALU.subtract
                                ).then_inc(l_split[s % 2], 1)

            def split_input(which, weights):
                for k in range(KT):
                    v.wait_ge(uh_ready, which * KT + k + 1)
                    v.tensor_tensor(u_low[:, k, :], uT[:, k, :], u_high[:, k, :].bitcast(F32), ALU.subtract
                                    ).then_inc(ul_ready, 1)
                    if k < 2 and weights:
                        weights(k)

            def scale_tiles(src, factor, signal):
                for k in range(KT):
                    for grp, (lo, hi) in enumerate(((0, PROMPT), (PROMPT, TOK))):
                        ins = v.scalar_tensor_tensor(uT[:, k, lo:hi], src[:, k, lo:hi], factor[:, k, grp:grp + 1],
                                                     rstd[:, lo:hi], ALU.mult, ALU.mult)
                    ins.then_inc(signal, 1)
                    if signal is y_scaled and k:
                        add_residual(k - 1)
                if signal is y_scaled:
                    add_residual(KT - 1)

            def add_residual(k):
                v.wait_ge(y_scaled, yn.add())
                v.tensor_tensor(xT[:, k, :], xT[:, k, :], uT[:, k, :], ALU.add).then_inc(x_added, 1)

            def modulate(part, tiles):
                layer = part[0]
                v.wait_ge(ada_done, done_after[part])
                ab = COL_ADAB + layer * 48
                lo, hi = tiles
                ins = v.tensor_tensor(mod[:, layer, lo:hi, :], AT[:, 0, 2 * lo:2 * hi].rearrange("p (t g) -> p t g", g=2),
                                      cols[:, ab + lo:ab + hi].unsqueeze(2).to_broadcast([P, hi - lo, 2]), ALU.add)
                ins.then_inc(mod_ready, 1)
                v.wait_ge(mod_ready, modn.add())

            def gain(layer, w):
                at = COL_GAIN + (layer * 4 + w) * KT
                return cols[:, at:at + KT].unsqueeze(2).to_broadcast([P, KT, 2])

            def pre_factor(layer, sub):
                link(v.scalar_tensor_tensor(pre_a[:, sub, :, :], mod[:, layer, sub * 24 + 8:sub * 24 + 16, :], 1.0,
                                            gain(layer, 2 * sub), ALU.add, ALU.mult))

            def post_factor(layer, sub):
                link(v.tensor_tensor(post_a[:, sub, :, :], mod[:, layer, sub * 24 + 16:sub * 24 + 24, :],
                                     gain(layer, 2 * sub + 1), ALU.mult))

            modn = Tally()
            done_after, total = {}, 0
            for part in (ADA_START, ADA_NORM, ADA_ROWS, ADA_POST, ADA_PRE, ADA_NEXT):
                total += part[3]
                done_after[part] = total

            def y_copies(turns, slots, outputs):
                with loop(v, turns, pjn=(pjn, len(slots)), **per(*outputs)) as i:
                    for k, slot in enumerate(slots):
                        s = pj(slot)
                        v.tensor_copy(uT[:, ds(i * len(slots) + k, 1), :].rearrange("p a (b t) -> p (a b) t", b=2),
                                      PJ[:, s, :, 0:HALF]).then_inc(pj_free[s], 1)

            v.memset(eps[:, :], EPS)
            s = pj_turned()
            v.tensor_copy(cols[:, :], PJ[:, s, :, :].rearrange("p b n -> p (b n)")[:, 0:COLS]).then_inc(pj_free[s], 1)
            for c in range(CH):
                s = pj_turned()
                v.tensor_copy(xT[:, :, c * P:(c + 1) * P], PJ[:, s, :, :].rearrange("p b (k t) -> p (b k) t", t=P)
                              ).then_inc(pj_free[s], 1)

            for layer in range(DEPTH):
                if layer == 0:
                    for s in range(SLOTS):
                        outs[s].add((4, 4, 8, 8)[s])
                    modulate(ADA_START, (0, 16))
                pre_factor(layer, 0)
                norm_rstd()
                scale_tiles(xT, pre_a[:, 0], scaled_ready)
                split_input(2 * layer, low_unit if layer == 1 else None)
                if layer == 0:
                    pjn.add(2)
                    turnn.add(2)
                    v.wait_ge(pj_free[0], 4)
                    v.wait_ge(pj_free[1], 4)
                    v.scalar_tensor_tensor(rt[:, :], rf[:, :], -1.0, rf[:, :], ALU.mult, ALU.max).then_inc(rowf_ready, 1)
                    for s in range(2):
                        low_unit(s)
                    v.wait_ge(rowf_ready, 1)
                    v.wait_ge(rowe_ready, 1)
                    link(v.scalar_tensor_tensor(rf[:, :], rf[:, :], 0.0, rt[:, :], ALU.min, ALU.subtract))
                    dirs = ((0, slice(0, PROMPT), slice(PROMPT, TOK)),
                            (32, slice(PROMPT - 1, None, -1), slice(TOK - 1, PROMPT - 1, -1)))
                    for r, pr, sa in dirs:
                        for part in (pr, sa):
                            ins = v.tensor_tensor_scan(rA[r:r + 32, part], rone[r:r + 32, part], rf[r:r + 32, part],
                                                       0.0, ALU.mult, ALU.add)
                    link(ins)
                    link(v.tensor_tensor(ri[:, :], ri[:, :], rA[:, :], ALU.subtract))
                    for r, pr, sa in dirs:
                        for part, first in ((pr, 0.0), (sa, m0col[r:r + 32, 0:1])):
                            v.tensor_tensor_scan(rM[r:r + 32, part], ri[r:r + 32, part], ri[r:r + 32, part],
                                                 first, ALU.max, ALU.max)
                    link(v.tensor_copy(rM[:, TOK:TOK + 1], m0col[:, :]))
                    v.scalar_tensor_tensor(rf[:, :], rM[:, 0:TOK], -1.0, rA[:, :], ALU.mult, ALU.subtract
                                           ).then_inc(rowb_ready, 1)
                    v.wait_ge(rowb_ready, 1)
                    for r in (0, 32):
                        ins = v.tensor_scalar(m0col[r:r + 4, :], rf[r:r + 4, PROMPT - 1:PROMPT] if r == 0 else rf[r:r + 4, 0:1],
                                              -1.0, None, ALU.mult)
                    ins.then_inc(rowb_ready, 1)
                    modulate(ADA_ROWS, (16, 48))
                    pre_factor(0, 1)
                    post_factor(0, 0)
                    post_factor(0, 1)
                    for s in (2, 3, 0):
                        low_unit(s)
                    v.wait_ge(rowT_full, 1)
                    v.tensor_copy(bcol[:, :, :].rearrange("p c r -> p (c r)"), AT[:, 0, 0:CH * 64]).then_inc(bcol_ready, 1)
                    v.wait_ge(bcol_ready, 2)
                else:
                    B = B_HEADS
                    v.wait_ge(ret_exp, 1)
                    v.tensor_scalar(dcy[:, 2, :], dcy[:, 1, :], -1.0, 1.0, ALU.mult, ALU.add).then_inc(ret_arg, 1)
                    v.wait_ge(ret_arg, 1)
                    link(v.tensor_scalar(dcy[:, 4, :], dcy[:, 2, :], -1.0, 1.0, ALU.mult, ALU.add))
                    link(v.tensor_scalar(dcy[:, 4, :], dcy[:, 4, :], 1e-30, None, ALU.add))
                    link(v.reciprocal(dcy[:, 4, :], dcy[:, 4, :]))
                    v.wait_ge(ret_exp, 2)
                    link(v.tensor_scalar(dcy[:, 3, :], dcy[:, 3, :], -1.0, 1e-30, ALU.mult, ALU.add))
                    link(v.tensor_tensor(dcy[:, 3, :], dcy[:, 3, :], dcy[:, 4, :], ALU.mult))
                    link(v.scalar_tensor_tensor(dcy[:, 5, :], dcy[:, 3, :], -1.0, dcy[:, 1, :], ALU.mult, ALU.mult))
                    kc = krt[:, 0:4 * P].rearrange("p (a l) -> p a l", a=4)
                    for h in range(B):
                        v.tensor_scalar(Dm[:, h, :], kc[:, 0, :], dcy[:, 5, h:h + 1], None, ALU.mult)
                        for d in range(2):
                            ins = v.tensor_scalar(XI[:, d, h, :], kc[:, 2 + d, :], dcy[:, 5, d * B + h:d * B + h + 1],
                                                  None, ALU.mult)
                    link(ins)
                    for h in range(B):
                        v.scalar_tensor_tensor(Dm[:, h, :], kc[:, 1, :], dcy[:, 5, B + h:B + h + 1], Dm[:, h, :],
                                               ALU.mult, ALU.add)
                    for d in range(2):
                        ins = v.tensor_scalar(zcol[:, d, :], dcy[:, 5, d * B:(d + 1) * B], krt[:, 4 * P + d:4 * P + d + 1],
                                              None, ALU.mult)
                    ins.then_inc(ret_arg, 1)
                    v.wait_ge(ret_exp, 3)
                    link(v.tensor_tensor(Dm[:, :, :], Dm[:, :, :], ident.unsqueeze(1).to_broadcast([P, B, P]), ALU.add))

                norm_col = [COL_MLN, COL_RETN][layer]

                def head_tail(tile, hh, col, gates, from_psum):
                    v.memset(wait_here[:, :], 0.0)
                    for c in range(CH):
                        ins = v.bn_aggr(mv[:, c, :], stats[:, c, :])
                    ins.then_inc(var_ready, 1)
                    v.wait_ge(hstd_ready, hd.now())
                    link(v.reciprocal(hstd[:, :], hstd[:, :]))
                    for c in range(CH):
                        src = ATf[:, c * DV:(c + 1) * DV] if from_psum else hn[:, c, :]
                        ins = v.tensor_scalar(hn[:, c, :], src, mv[:, c, 0:1], hstd[:, c:c + 1], ALU.subtract, ALU.mult)
                    ins.then_inc(hn_ready, 1)
                    for s in range(2):
                        v.wait_ge(pj_free[s], gates)
                    v.wait_ge(ht_full, hd.now())
                    for vh in range(2):
                        ins = v.scalar_tensor_tensor(
                            hT[:, tile + vh, :] if isinstance(tile, int) else
                            hT[:, ds(tile + vh, 1), :].rearrange("p a t -> p (a t)"),
                            ATf[:, vh * 1024:vh * 1024 + TOK],
                            cols[:, col + vh:col + vh + 1] if isinstance(col, int) else cols[:, ds(col + vh, 1)],
                            gt[:, 2 * hh + vh, :], ALU.mult, ALU.mult)
                    ins.then_inc(h_ready, 1)

                if layer == 0:
                    for h in range(A_HEADS):
                        hh = h % 2
                        hd.add()
                        if hh == 0:
                            pjn.add(18)
                            for s in range(SLOTS):
                                outs[s].add((4, 4, CH, CH)[s])
                            if h > 0:
                                for s in (2, 3, 0):
                                    low_unit(s)
                        v.wait_ge(bc_full, h + 1)
                        for d in range(2):
                            r = 32 * d + h
                            bc = chunks(2 * d)
                            m0 = ATf[:, 1024 * d + TOK:1024 * d + TOK + 1]
                            for c in range(CH):
                                v.scalar_tensor_tensor(W[:, d, c, :], bc[:, c, :], bcol[:, c, r:r + 1],
                                                       mlc[:, d * P:(d + 1) * P], ALU.add, ALU.add)
                            edge = P - 1 if d == 0 else 0
                            v.tensor_copy(bound[:, d, 0, :], bc[:, :, edge])
                            if d == 0:
                                v.tensor_scalar(bound[:, d, 1, 2:CH], bc[:, 1:CH - 1, edge], -1.0, None, ALU.mult)
                                v.tensor_scalar(bound[:, d, 1, 1:2], m0, -1.0, None, ALU.mult)
                                ins = v.memset(bound[:, d, 1, 0:1], 0.0)
                            else:
                                v.tensor_scalar(bound[:, d, 1, 1:CH - 1], bc[:, 2:CH, edge], -1.0, None, ALU.mult)
                                v.tensor_scalar(bound[:, d, 1, CH - 1:CH], m0, -1.0, None, ALU.mult)
                                ins = v.memset(bound[:, d, 1, 0:1], 0.0)
                        link(ins)
                        for d in range(2):
                            r = 32 * d + h
                            v.tensor_tensor(bound[:, d, 2, :], bcol[:, :, r], bound[:, d, 0, :], ALU.add)
                            ins = v.tensor_tensor(bound[:, d, 3, :], bound[:, d, 0, :], bound[:, d, 1, :], ALU.add)
                        ins.then_inc(arg_ready, 1)
                        v.wait_ge(exp_ready, h + 1)
                        v.wait_ge(score_full, h + 1)
                        for d in range(2):
                            ins = v.tensor_tensor(W[:, d, :, :], W[:, d, :, :], chunks(0), ALU.mult)
                        ins.then_inc(p_ready, 1)
                        v.wait_ge(state_in, 64 * (h + 1))
                        if h > 0:
                            v.wait_ge(state_out, 64 * h)
                        for d in range(2):
                            v.wait_ge(ds_full, 2 * h + d + 1)
                            ins = v.tensor_copy(Cout[:, d, :], AT[:, 0, 0:DV + 1])
                            if d == 1:
                                ins.then_inc(out_staged, 1)
                            for n in range(1, 4):
                                c = n if d == 0 else CH - n
                                ins = (v.scalar_tensor_tensor(Cst[:, d, n, :], Cst[:, d, n - 1, :],
                                                            wsdec[:, d, 1, c:c + 1], AT[:, n, 0:DV + 1],
                                                            ALU.mult, ALU.add))
                                if n < 3:
                                    link(ins)
                            ins.then_inc(st_ready, 1)
                        if hh == 0:
                            low_unit(1)
                        for c in range(CH):
                            b = 2 * (c % 2)
                            v.wait_ge(o_full, CH * h + c + 1)
                            den = AT[:, b:b + 2, DV]
                            link(v.scalar_tensor_tensor(dn[:, :], den, -1.0, eqcol[:, c, h:h + 33:32], ALU.mult, ALU.max))
                            link(v.tensor_tensor(dn[:, :], den, dn[:, :], ALU.max))
                            link(v.reciprocal(dn[:, :], dn[:, :]))
                            link(v.tensor_scalar(hn[:, c, :], AT[:, b, 0:DV], dn[:, 0:1], None, ALU.mult))
                            v.scalar_tensor_tensor(hn[:, c, :], AT[:, b + 1, 0:DV], dn[:, 1:2], hn[:, c, :],
                                                   ALU.mult, ALU.add).then_inc(o_free, 1)
                            v.wait_ge(o_free, CH * h + c + 1)
                            ins = v.bn_stats(stats[:, c, :], hn[:, c, :])
                        link(ins)
                        head_tail(2 * h, hh, norm_col + 2 * h, EVACS_BEFORE_ML + 9 * (h // 2) + 8 + hh, False)
                        if h < A_HEADS - 2:
                            low_unit(hh)
                else:
                    ropn, scnt, dcnt, ocnt, scount, gcount, swn = (Tally() for _ in range(7))
                    scnt.n = ocnt.n = A_HEADS
                    dcnt.n = 2 * A_HEADS
                    ocnt.n = CH * A_HEADS
                    gcount.n = EVACS_BEFORE_RET
                    sin_n, sout_n = Tally(), Tally()
                    sout_n.n = 64 * A_HEADS
                    heads = Tally()

                    def ret_group(g, last):
                        for s in (2, 3):
                            low_unit(s)
                        v.wait_ge(swap_in, swn.add(64))
                        cos = rope[:, 0:SAMPLE].unsqueeze(1).to_broadcast([P, 4, SAMPLE])
                        sin = rope[:, SAMPLE:].unsqueeze(1).to_broadcast([P, 4, SAMPLE])
                        v.tensor_tensor(swapped[:, :, :], swapped[:, :, :], sin, ALU.mult)
                        link(v.tensor_tensor(qk[:, :, PROMPT:TOK], qk[:, :, PROMPT:TOK], cos, ALU.mult))
                        v.tensor_tensor(qk[:, :, PROMPT:TOK], qk[:, :, PROMPT:TOK], swapped[:, :, :],
                                        ALU.add).then_inc(rope_ready, 1)
                        low_unit(0)
                        for hh in range(2):
                            head = g * 2 + hh
                            hd.add()
                            v.wait_ge(score_full, scnt.add())
                            v.tensor_tensor(Pm[:, :, :], chunks(0), Dm[:, ds(head, 1), :].to_broadcast([P, CH, P]),
                                            ALU.mult).then_inc(p_ready, 1)
                            v.wait_ge(ds_full, dcnt.add())
                            v.wait_ge(ret_state_in, sin_n.add(32))
                            v.wait_ge(state_out, sout_n.now())
                            sout_n.add(32)
                            for d in range(2):
                                ins = v.tensor_copy(Sout[:, d, :], ATf[:, d * 1024:d * 1024 + DV])
                            ins.then_inc(out_staged, 1)
                            for n in range(1, 4):
                                for d in range(2):
                                    at = d * 1024 + n * DV
                                    ins = v.scalar_tensor_tensor(Sst[:, d, n, :], Sst[:, d, n - 1, :],
                                                                 cdcol[:, d, ds(head, 1)],
                                                                 ATf[:, at:at + DV], ALU.mult, ALU.add)
                                if n < 3:
                                    link(ins)
                            ins.then_inc(st_ready, 1)
                            if hh == 0:
                                low_unit(1)
                            v.wait_ge(o_full, ocnt.add())
                            for c in range(CH):
                                ins = v.bn_stats(stats[:, c, :], ATf[:, c * DV:(c + 1) * DV])
                            link(ins)
                            gcount.add(8 if hh == 0 else 1)
                            head_tail(g * 4 + 2 * hh, hh, g * 4 + (norm_col + 2 * hh), gcount.now(), True)
                            if not last:
                                low_unit(hh)

                    with loop(v, GROUPS[1] - 1, own=(own, 9), hd=(hd, 2), sc=(scnt, 2), dc=(dcnt, 2), oc=(ocnt, 2),
                              gc=(gcount, 9), sw=(swn, 64), si=(sin_n, 64), so=(sout_n, 64), h0=(highs[0], 3),
                              h1=(highs[1], 3)) as g:
                        ret_group(g, False)
                    ret_group(GROUPS[1] - 1, True)
                    pjn.add(18 * GROUPS[1])
                    for s in range(SLOTS):
                        outs[s].add(GROUPS[1] * (4, 4, CH, CH)[s])
                if layer == 0:
                    y_copies(2, [0, 0, 1, 1], (2, 2, 0, 0))
                else:
                    y_copies(2, [0, 1, 2, 3], (1, 1, 1, 1))
                norm_rstd()
                v.wait_ge(x_back, 16 * (layer + 1))
                scale_tiles(uT, post_a[:, 0], y_scaled)
                norm_rstd()
                scale_tiles(xT, pre_a[:, 1], scaled_ready)
                split_input(2 * layer + 1, low_weights)

                def taps(t, b):
                    s = pjn.n % 2
                    pjn.add()
                    v.wait_ge(conv_begun, cvn.add())
                    pieces = ((0, 0, 1, PROMPT), (0, PROMPT, (HALF - PROMPT) // GRID_W, GRID_W),
                              (1, 0, HALF // GRID_W, GRID_W))
                    for tap in (0, 2):
                        scalar = cols[:, ds(t + (COL_CONV + (layer * 3 + tap) * 2 * FT + b * FT), 1)]
                        for bank, lo, n, w in pieces:
                            z = PJ[:, s, bank, lo:lo + n * w].rearrange("p (r w) -> p r w", w=w)
                            o = conv[:, b, bank * HALF + lo:bank * HALF + lo + n * w].rearrange("p (r w) -> p r w", w=w)
                            o, z = (o[:, :, 1:w], z[:, :, 0:w - 1]) if tap == 0 else (o[:, :, 0:w - 1], z[:, :, 1:w])
                            ins = v.scalar_tensor_tensor(o, z, scalar, o, ALU.mult, ALU.add)
                        if tap == 0:
                            link(ins)
                    ins.then_inc(pj_free[s], 1)
                    free[s].add()
                    return s

                def up_pair(t, tile, slot):
                    taps(t, 0)
                    s = taps(t, 1)
                    v.wait_ge(pj_free[s], free[s].now())
                    v.wait_ge(gelu_ready, gen.add())
                    v.tensor_tensor(conv[:, 1, :], conv[:, 0, :], conv[:, 1, :], ALU.mult).then_inc(prod_ready, 1)
                    low_weights(slot)
                    v.wait_ge(acth_ready, gen.now())
                    at = ds(tile, 1)
                    v.tensor_tensor(act_low[:, at, :], conv[:, 1:2, :], act_high[:, at, :].bitcast(F32), ALU.subtract
                                    ).then_inc(act_ready, 1)

                def down_tile(m, slot, half):
                    s = pj(slot)
                    y = uT[:, ds(m, 1), :].rearrange("p a (b t) -> p (a b) t", b=2)
                    if half == 0:
                        v.tensor_copy(y, PJ[:, s, :, 0:HALF]).then_inc(pj_free[s], 1)
                    else:
                        v.tensor_tensor(y, PJ[:, s, :, 0:HALF], y, ALU.add).then_inc(pj_free[s], 1)

                free[0].n = free[1].n = pjn.n // 2
                assert pjn.n % 2 == 0
                v.wait_ge(state_out, 64 * A_HEADS + layer * 32 * B_HEADS)
                for kind, turns, first in FFN:
                    if kind == "up":
                        for s in range(2):
                            outs[s].add(2 * turns)
                        with loop(v, turns, own=(own, 4), pjn=(pjn, 4), cv=(cvn, 4), ge=(gen, 2), f0=(free[0], 2),
                                  f1=(free[1], 2), h0=(highs[0], 1), h1=(highs[1], 1)) as i:
                            for j in range(2):
                                up_pair(i * 2 + (first + j), i * 2 + j, j)
                    else:
                        last = first > 0
                        with loop(v, turns - last, pjn=(pjn, 2), o0=(outs[0], 1), o1=(outs[1], 1), h0=(highs[0], 1),
                                  h1=(highs[1], 1)) as i:
                            for j in range(2):
                                down_tile(i * 2 + j, j, last)
                                low_weights(j)
                        if last:
                            for j in range(2):
                                down_tile(KT - 2 + j, j, last)
                        for s in range(2):
                            free[s].n = pjn.n // 2
                if layer == 0:
                    modulate(ADA_PRE, (0, 32))
                norm_rstd()
                scale_tiles(uT, post_a[:, 1], y_scaled)
                if layer == 0:
                    modulate(ADA_NEXT, (32, 48))
                    for s in ADA_NEXT[2]:
                        outs[s].add(ADA_POST[3] + ADA_PRE[3] + ADA_NEXT[3])
                    pre_factor(1, 1)
                    post_factor(1, 0)
                    post_factor(1, 1)

            for c in range(CH):
                s = pj_turned()
                v.tensor_copy(xin[:, c, :], PJ[:, s, :, :].rearrange("p b n -> p (b n)")).then_inc(out_ready, 1)

        @block.tensor
        def _(pe):
            full = [Tally() for _ in range(SLOTS)]
            pjn, free = Tally(), [Tally(), Tally()]
            stn, un, hrn, rown, splits = Tally(), Tally(), Tally(), Tally(), [Tally(), Tally()]
            scn, stc, qzn, hnn, ron = (Tally() for _ in range(5))

            def per(*uses):
                return {f"s{s}": (full[s], n) for s, n in enumerate(uses)}

            def unit(slot, dmas=1):
                full[slot].add(dmas)
                pe.wait_ge(ring_full[slot], full[slot].now() * 16)

            def emptied():
                for s in range(2):
                    pe.wait_ge(pj_free[s], free[s].now())

            def pj_slot():
                s = pjn.n % 2
                pjn.add()
                pe.wait_ge(pj_free[s], free[s].now())
                free[s].add()
                return s

            def project(weights, source, kts, start=True, stop=True, s=None):
                for k in range(kts):
                    for b in range(2):
                        ins = pe.matmul(PJ[:, s, b, 0:HALF], weights(k), source(k)[:, b * HALF:(b + 1) * HALF],
                                        start=(start and k == 0), stop=(stop and k == kts - 1))
                return ins

            def norm_stat():
                pe.wait_ge(sq_added, 8 * stn.now() + 8)
                stn.add()
                for c in range(CH):
                    ins = pe.matmul(mean_sq[:, c:c + 1], sqsum[:, c * P:(c + 1) * P], mean_w, start=True, stop=True)
                ins.then_inc(stat_full, 1)

            def norm_rstd():
                pe.wait_ge(diag_ready, stn.now())
                d = diag[:, :, :].rearrange("p c t -> p (c t)")
                pe.matmul(rstd[:, 0:512], ones, d[:, 0:512], start=True, stop=True)
                pe.matmul(rstd[:, 512:TOK], ones, d[:, 512:TOK], start=True, stop=True).then_inc(rstd_full, 1)

            pe.wait_ge(const_in, 16)
            pe.wait_ge(rows_in, 160)
            s = pj_slot()
            for n in range(5):
                ins = pe.transpose(PJ[:, s, n // 4, (n % 4) * P:(n % 4 + 1) * P], rows[:, n, :], ident)
            ins.then_inc(turned, 1)
            pe.wait_ge(x_in, 32)
            for c in range(CH):
                s = pj_slot()
                for k in range(KT):
                    ins = pe.transpose(PJ[:, s, k // 4, (k % 4) * P:(k % 4 + 1) * P], xin[:, c, k * P:(k + 1) * P], ident)
                ins.then_inc(turned, 1)

            def ada(part):
                layer, first, slots, turns = part
                n = len(slots)
                with loop(pe, turns, **per(*[int(s in slots) for s in range(SLOTS)]), row=(rown, n)) as i:
                    for j, slot in enumerate(slots):
                        unit(slot)
                        w = ring[slot][:, :].rearrange("p (k m) -> p k m", k=KT)
                        for k in range(KT):
                            ins = pe.matmul(PJ[0:2, j // 2, j % 2, 0:256], silu_c[:, k, :], w[:, k, :],
                                            start=(k == 0), stop=(k == KT - 1))
                        ins.then_inc(made[slot], 1)
                    pe.wait_ge(ada_row, rown.add(n))
                    for m in range(2 * n):
                        ins = pe.matmul(AT[:, 0, ds(i * (4 * n) + (4 * first + 2 * m), 2)],
                                        ada_rows[:, m // 2, (m % 2) * P:(m % 2 + 1) * P],
                                        ident[0:2, 0:2], start=True, stop=True)
                    ins.then_inc(ada_done, 1)

            def project_split(weights_high, weights_low, kts, at, step, high, low, s, source_ready=None):
                for k in range(kts):
                    if source_ready:
                        split, before = source_ready
                        pe.wait_ge(split, before + k + 1)
                    for n, (w, x) in enumerate(((weights_high, high), (weights_high, low), (weights_low, high))):
                        for b in range(2):
                            ins = pe.matmul(PJ[:, s, b, 0:HALF], w[:, at + k * step:at + k * step + P],
                                            x[:, k, b * HALF:(b + 1) * HALF],
                                            start=(k == 0 and n == 0), stop=(k == kts - 1 and n == 2))
                return ins

            for layer in range(DEPTH):
                if layer == 0:
                    pe.wait_ge(silu_ready, 2)
                    emptied()
                    ada(ADA_START)
                norm_stat()
                norm_rstd()
                if layer == 0:
                    pe.wait_ge(mod_ready, 1)
                    ada(ADA_NORM)
                un.add(KT)
                pe.wait_ge(u_ready, un.now())

                if layer == 0:
                    pe.wait_ge(ml_in, 16 * 11)
                    for kind in range(2):
                        s = pj_slot()
                        for k in range(KT):
                            for b in range(2):
                                ins = pe.matmul(PJ[0:64, s, b, 0:HALF], wg[:, k, kind, :],
                                                uT[:, k, b * HALF:(b + 1) * HALF], start=(k == 0), stop=(k == KT - 1))
                        ins.then_inc(turned, 1)
                    emptied()
                    ada(ADA_ROWS)
                pe.wait_ge(ul_ready, 2 * layer * KT + KT)

                def turn_gate_rows():
                    pe.wait_ge(rowb_ready, 1)
                    pe.wait_ge(mod_ready, 2)
                    for n, row in enumerate((ri, rf)):
                        for c in range(CH):
                            ins = pe.transpose(AT[:, n, c * 64:(c + 1) * 64], row[:, c * P:(c + 1) * P], ident[0:64, 0:64])
                    ins.then_inc(rowT_full, 1)
                    pe.wait_ge(bcol_ready, 2)

                def split_unit(slot):
                    full[slot].add()
                    pe.wait_ge(l_split[slot % 2], splits[slot % 2].add())

                def project_unit(slot, m):
                    s = pj_slot()
                    project_split(w_high[slot % 2], ring_low[slot], KT, m * P, 256, u_high, u_low, s
                                  ).then_inc(made[slot], 1)

                def gate(t):
                    if t % 2 == 0:
                        split_unit(t // 2)
                    project_unit(t // 2, t % 2)

                def qkv():
                    for u in range(2):
                        split_unit(u)
                        for m in range(2):
                            project_unit(u, m)
                    for hh in range(2):
                        split_unit(2 + hh)
                        for c in range(CH):
                            s = pj_slot()
                            for k in range(KT):
                                for n, (x, w) in enumerate(((u_high, w_high[hh]), (u_high, ring_low[2 + hh]),
                                                            (u_low, w_high[hh]))):
                                    ins = pe.matmul(PJ[:, s, 0, 0:DV], x[:, k, c * P:(c + 1) * P],
                                                    w[:, k * DV:(k + 1) * DV], start=(k == 0 and n == 0),
                                                    stop=(k == KT - 1 and n == 2))
                            ins.then_inc(made[2 + hh], 1)
                    emptied()

                def scores(hh):
                    for c in range(CH):
                        pe.matmul(chunks(0)[:, c, :], qk[:, 2 + hh, c * P:(c + 1) * P], qk[:, hh, c * P:(c + 1) * P],
                                  start=True, stop=True)
                    for c in range(CH):
                        ins = pe.transpose(chunks(2)[:, c, :], qk[:, 2 + hh, c * P:(c + 1) * P], ident)
                    ins.then_inc(score_full, 1)

                def turn_back():
                    pe.wait_ge(hn_ready, hnn.add())
                    for vh in range(2):
                        for c in range(CH):
                            ins = pe.transpose(chunks(2 * vh)[:, c, :], hn[:, c, vh * P:(vh + 1) * P], ident)
                    ins.then_inc(ht_full, 1)

                if layer == 0:
                    for g in range(GROUPS[0]):
                        qkv()
                        if g == 0:
                            turn_gate_rows()
                        for hh in range(2):
                            h = 2 * g + hh
                            pe.wait_ge(h_ready, h)
                            for d in range(2):
                                sel = mlc[0:64, (2 + 4 * d + h) * P:(3 + 4 * d + h) * P]
                                pe.matmul(ATf[:, 1024 * d:1024 * d + 512], sel, rM[:, 0:512], start=True, stop=True)
                                ins = pe.matmul(ATf[:, 1024 * d + 512:1024 * d + TOK + 1], sel, rM[:, 512:TOK + 1],
                                                start=True, stop=True)
                            ins.then_inc(bc_full, 1)
                            if hh == 0:
                                gate(0)
                            pe.wait_ge(exp_ready, h + 1)
                            scores(hh)
                            if hh == 0:
                                gate(1)
                            pe.wait_ge(p_ready, h + 1)
                            pe.wait_ge(kz_ready, h + 1)
                            pe.wait_ge(ml_zero, 5)
                            for d in range(2):
                                pe.wait_ge(st_ready, 2 * h + d)
                                for n in range(4):
                                    c = n if d == 0 or n == 0 else CH - n
                                    ins = pe.matmul(AT[:, n, 0:DV + 1], kz[d][:, c, :], vt[:, c, hh, :], start=True, stop=True)
                                ins.then_inc(ds_full, 1)
                            if hh == 0:
                                gate(2)
                            pe.wait_ge(st_ready, 2 * h + 2)
                            pe.wait_ge(qz_ready, 2 * h + 2)
                            for c in range(CH):
                                if c >= 2:
                                    pe.wait_ge(o_free, CH * h + c - 1)
                                for d in range(2):
                                    o = AT[:, 2 * (c % 2) + d, 0:DV + 1]
                                    ins = pe.matmul(o, W[:, d, c, :], vt[:, c, hh, :], start=True, stop=(c == 0))
                                    if c:
                                        ins = pe.matmul(o, qz[d][:, c - 1, :], Cst[:, d, c - 1 if d == 0 else CH - 1 - c, :],
                                                        start=False, stop=True)
                                ins.then_inc(o_full, 1)
                            if hh == 0:
                                gate(3)
                            turn_back()
                else:
                    hrn.n = scn.n = A_HEADS
                    stc.n, qzn.n = 2 * A_HEADS, 2 * A_HEADS
                    pe.wait_ge(ml_zero, 6)
                    with loop(pe, GROUPS[1], pjn=(pjn, 18), f0=(free[0], 9), f1=(free[1], 9), h=(hrn, 2), sc=(scn, 2),
                              st=(stc, 2), qz=(qzn, 4), hn=(hnn, 2), ro=(ron, 1), sp0=(splits[0], 3), sp1=(splits[1], 3),
                              **per(2, 2, 1, 1)) as g:
                        qkv()
                        pe.wait_ge(rope_ready, ron.add())
                        for hh in range(2):
                            pe.wait_ge(h_ready, hrn.now())
                            hrn.add()
                            scores(hh)
                            gate(0 if hh == 0 else 3)
                            pe.wait_ge(p_ready, scn.add())
                            pe.wait_ge(kz_ready, scn.now())
                            for d in range(2):
                                for n in range(4):
                                    c = n if d == 0 or n == 0 else CH - n
                                    at = d * 1024 + n * DV
                                    ins = pe.matmul(ATf[:, at:at + DV], kz[d][:, c, :], vt[:, c, hh, 0:DV],
                                                    start=True, stop=True)
                            ins.then_inc(ds_full, 1)
                            if hh == 0:
                                gate(1)
                            pe.wait_ge(st_ready, stc.add())
                            pe.wait_ge(qz_ready, qzn.add(2))
                            for c in range(CH):
                                o = ATf[:, c * DV:(c + 1) * DV]
                                ins = pe.matmul(o, Pm[:, c, :], vt[:, c, hh, 0:DV], start=True, stop=(c == 0))
                                if c:
                                    for d in range(2):
                                        ins = pe.matmul(o, qz[d][:, c - 1, :], Sst[:, d, c - 1 if d == 0 else CH - 1 - c, :],
                                                        start=False, stop=(d == 1))
                            ins.then_inc(o_full, 1)
                            if hh == 0:
                                gate(2)
                            turn_back()
                pe.wait_ge(h_ready, [A_HEADS, A_HEADS + B_HEADS][layer])

                n, tiles, kts = OUT_UNITS[layer], OUT_TILES[layer], HV[layer] // P
                with loop(pe, 2, pjn=(pjn, 4), f0=(free[0], 2), f1=(free[1], 2), **per(*[int(s < n) for s in range(4)])):
                    for j in range(n):
                        unit(j)
                        w = ring[j][:, 0:kts * tiles * P].rearrange("p (k m) -> p k m", k=kts)
                        for m in range(tiles):
                            s = pj_slot()
                            project(lambda k: w[:, k, m * P:(m + 1) * P], lambda k: hT[:, k, :], kts, s=s
                                    ).then_inc(made[j], 1)
                norm_stat()
                norm_rstd()
                if layer == 0:
                    ada(ADA_POST)
                norm_stat()
                norm_rstd()
                if layer == 0:
                    ada(ADA_PRE)
                un.add(KT)

                for kind, turns, first in FFN:
                    out_per = 2 if kind == "up" else 1

                    def ffn_turn(source_ready=None):
                        for j in range(2):
                            pe.wait_ge(l_split[j], splits[j].add())
                            for b in range(out_per):
                                s = pj_slot()
                                if kind == "up":
                                    ins = project_split(w_high[j], w_low[j], KT, b * KT * P, P, u_high, u_low, s, source_ready)
                                else:
                                    ins = project_split(w_high[j], w_low[j], HALVES[int(first > 0)], 0, P, act_high, act_low, s,
                                                        source_ready)
                                source_ready = None
                                ins.then_inc(made[j], 1)

                    if kind == "down":
                        ffn_turn((act_ready, FT * layer + first))
                    elif first == 0:
                        ffn_turn((ul_ready, KT * (2 * layer + 1)))
                    with loop(pe, turns - (kind == "down" or first == 0), pjn=(pjn, 2 * out_per), f0=(free[0], out_per),
                              f1=(free[1], out_per), sp0=(splits[0], 1), sp1=(splits[1], 1)):
                        ffn_turn()
                for s in range(2):
                    full[s].add(2 * (FT + KT * 2) // 2)
                norm_stat()
                norm_rstd()
                if layer == 0:
                    pe.wait_ge(mod_ready, 3)
                    ada(ADA_NEXT)

            pe.wait_ge(x_added, 4 * KT)
            emptied()
            for c in range(CH):
                s = c % 2
                if c >= 2:
                    pe.wait_ge(out_ready, c - 1)
                for k in range(KT):
                    ins = pe.transpose(PJ[:, s, k // 4, (k % 4) * P:(k % 4 + 1) * P], xT[:, k, c * P:(c + 1) * P], ident)
                ins.then_inc(turned, 1)


_INS = ['x_prompt', 'x_sample', 'state_mlstm_C', 'state_mlstm_n', 'state_mlstm_m', 'state_ret_S', 'c', 'c_ctx',
        'norm_gain', 'ada_w', 'ada_b', 'ml_w_in', 'ml_b_gate', 'ml_norm', 'ml_w_out', 'ret_w_in', 'ret_decay',
        'ret_norm', 'ret_w_out', 'ffn_w_up', 'ffn_conv', 'ffn_conv_b', 'ffn_w_down']
_OUTS = [(1, PROMPT, D_MODEL), (1, SAMPLE, D_MODEL), (1, 1, 2, A_HEADS, DK, DV), (1, 1, 2, A_HEADS, DK),
         (1, 1, 2, A_HEADS), (1, 1, 2, B_HEADS, DK, DV)]


def shape_constants():
    one = np.arange(P)
    common = np.concatenate([np.eye(P), np.full((P, P), 1.0 / D_MODEL), np.ones((P, P))], axis=1)
    s, l = one[:, None], one[None, :]
    ml = np.zeros((P, 10 * P))
    ml[:, 0:P] = np.where(s <= l, 0.0, MASKED)
    ml[:, P:2 * P] = np.where(s >= l, 0.0, MASKED)
    for d in range(2):
        for h in range(A_HEADS):
            at = (2 + 4 * d + h) * P
            ml[32 * d + h, at:at + P] = -1.0
    ret = np.zeros((P, TOK + 2 * SAMPLE))
    ret[:, 0:P] = np.maximum(l - s, 0)
    ret[:, P:2 * P] = np.maximum(s - l, 0)
    ret[:, 2 * P:3 * P] = l + 1
    ret[:, 3 * P:4 * P] = P - l
    ret[:, 4 * P] = P - 1 - one
    ret[:, 4 * P + 1] = one
    quarter = DK // 4
    inv = (10000.0 ** (-np.arange(quarter, dtype=np.float32) / quarter)).astype(np.float32)
    t = np.arange(SAMPLE)
    for half, pos in enumerate((t // GRID_W, t % GRID_W)):
        ang = (pos.astype(np.float32)[None, :] * inv[:, None]).astype(np.float32).astype(np.float64)
        for part, sign in enumerate((-1.0, 1.0)):
            r = half * 2 * quarter + part * quarter
            ret[r:r + quarter, TOK:TOK + SAMPLE] = np.cos(ang)
            ret[r:r + quarter, TOK + SAMPLE:] = sign * np.sin(ang)
    return {n: a.astype(np.float32) for n, a in (("common", common), ("ml", ml), ("ret", ret))}


def kernel(**inputs):
    import concourse.bacc as bacc
    from concourse.bass_utils import run_bass_kernel_spmd

    nc = bacc.Bacc("TRN2", target_bir_lowering=False, num_devices=1)
    given = {name: np.ascontiguousarray(inputs[name]) for name in _INS}
    arrays, args = {}, []
    for name, a in {**given, **{"k_" + n: a for n, a in shape_constants().items()}}.items():
        arrays[f"in_{name}"] = a
        args.append(nc.dram_tensor(f"in_{name}", a.shape, mybir.dt.from_np(a.dtype), kind="ExternalInput").ap())
    for i, shape in enumerate(_OUTS):
        args.append(nc.dram_tensor(f"out_{i}", shape, F32, kind="ExternalOutput").ap())
    args.append(nc.dram_tensor("x_saved_dram", (P, KT, TOK), F32, kind="Internal").ap())
    hybrid_step(nc, *args)
    r = run_bass_kernel_spmd(nc, [arrays], core_ids=[0])
    return tuple(r.results[0][f"out_{i}"] for i in range(len(_OUTS)))
```

```python
from contextlib import ExitStack, contextmanager
import math

import numpy as np
import concourse.bass as bass
from concourse import mybir

F32 = mybir.dt.float32
F32R = mybir.dt.float32r
ACT = mybir.ActivationFunctionType
ALU = mybir.AluOpType
ds = bass.ds

P = 128
D_MODEL = 1024
KT = D_MODEL // P
PROMPT = 128
SAMPLE = 512
TOK = PROMPT + SAMPLE
HALF = TOK // 2
CH = TOK // P
GRID_W = 64
DEPTH = 2
D_FF = 2816
FT = D_FF // P
HALVES = (FT // 2 + 1, FT // 2 - 1)
A_HEADS, B_HEADS = 4, 8
DK, DV = 128, 256
EPS = 1e-6
SLOTS = 4
UNIT = 2048
MASKED = -1e30
COL_GAIN = 0
COL_CCTX = 64
COL_C = 72
COL_MLN = 80
COL_RETN = 88
COL_ADAB = 128
COL_CONV = 256
COL_CONVB = 256 + DEPTH * 3 * 2 * FT
COLS = 5 * P


class Tally:

    def __init__(self):
        self.n, self.turn, self.per = 0, None, 0

    def now(self, back=0):
        n = self.n - back
        return n if self.turn is None else self.turn * self.per + n

    def add(self, k=1):
        self.n += k
        return self.now()


@contextmanager
def loop(eng, turns, **per_turn):
    starts = {}
    with eng.Fori(0, turns) as i:
        for name, (tally, per) in per_turn.items():
            starts[name] = tally.n
            tally.turn, tally.per = i, per
        yield i
    for name, (tally, per) in per_turn.items():
        assert tally.n - starts[name] == per, (name, tally.n - starts[name], per)
        tally.n = starts[name] + per * turns
        tally.turn = None


def hybrid_step(nc, x_prompt, x_sample, st_C, st_n, st_m, st_S, c_lat, c_ctx, norm_gain, ada_w, ada_b,
                ml_w_in, ml_b_gate, ml_norm, ml_w_out, ret_w_in, ret_decay, ret_norm, ret_w_out,
                ffn_w_up, ffn_conv, ffn_conv_b, ffn_w_down, k_common, k_ml, k_ret,
                y_prompt, y_sample, new_C, new_n, new_m, new_S, x_saved_dram):
    with ExitStack() as ctx:
        def sb(name, shape, stack=ctx, dt=F32):
            return stack.enter_context(nc.sbuf_tensor(name, shape, dt))

        def sem(name):
            return ctx.enter_context(nc.semaphore(name))

        xT = sb("xT", [P, KT, TOK])
        uT = sb("uT", [P, KT, TOK])
        common = sb("common", [P, 3 * P])
        cols = sb("cols", [P, COLS])
        silu_c = sb("silu_c", [P, KT, 2])
        mod = sb("mod", [P, DEPTH, 48, 2])
        pre_a = sb("pre_a", [P, 2, KT, 2])
        post_a = sb("post_a", [P, 2, KT, 2])
        sq = sb("sq", [P, 2, TOK])
        sqsum = sb("sqsum", [P, TOK])
        tok_rstd = sb("tok_rstd", [P, CH])
        diag = sb("diag", [P, CH, P])
        ada_mem = sb("ada_mem", [P, SLOTS, 256])
        ada_rows = ada_mem[0:2, :, :]
        dcy = sb("dcy", [P, 6, 16])
        eps = sb("eps", [P, 1])
        wait_here = sb("wait_here", [P, 1])
        ident, mean_w, ones = common[:, 0:P], common[:, P:P + 1], common[:, 2 * P:3 * P]

        u_high = sb("u_high", [P, KT, TOK], dt=F32R)
        u_low = sb("u_low", [P, KT, TOK], dt=F32R)
        w_high = [sb(f"w_high{s}", [P, UNIT], dt=F32R) for s in range(2)]
        ring, ring_low = [], []
        mixer = ExitStack()
        for pair, stack in (((0, 1), ctx), ((2, 3), mixer)):
            with ExitStack() as place:
                ring += [sb(f"ring{s}", [P, UNIT], place) for s in pair]
            ring_low += [sb(f"ring_low{s}", [P, UNIT], stack, F32R) for s in pair]

        def mb(name, shape):
            return sb(name, shape, mixer)

        qk, gt = uT[:, 0:4, :], uT[:, 4:8, :]
        hT = mb("hT", [P, 2 * B_HEADS, TOK])
        xflat = xT[:, :, :].rearrange("p k t -> p (k t)")
        vt_n, kz_n, qz_n = CH * 2 * (DV + 1), CH * DK, (CH - 1) * P
        vt = xflat[:, 0:vt_n].rearrange("p (c h v) -> p c h v", c=CH, h=2)
        kzf, kzb = (xflat[:, vt_n + d * kz_n:vt_n + (d + 1) * kz_n].rearrange("p (c k) -> p c k", k=DK) for d in range(2))
        qz_at = vt_n + 2 * kz_n
        qzf, qzb = (xflat[:, qz_at + d * qz_n:qz_at + (d + 1) * qz_n].rearrange("p (c l) -> p c l", l=P) for d in range(2))
        hn = sq[:, :, :].rearrange("p a t -> p (a t)").rearrange("p (c v) -> p c v", v=DV)
        stats = mb("stats", [P, CH, 6])
        mv = mb("mv", [P, CH, 2])
        hstd = mb("hstd", [P, CH])
        kz, qz = [kzf, kzb], [qzf, qzb]

        ml_mem = ExitStack()
        mlc = hT[:, 8:10, :].rearrange("p a t -> p (a t)")
        wg = hT[:, 10:12, :].rearrange("p a t -> p (a t)")[:, 0:KT * 128].rearrange("p (k b r) -> p k b r", k=KT, b=2)
        rone, rt = hT[0:64, 12, :], hT[0:64, 13, :]
        winter = hT[:, 10:12, :].rearrange("p a t -> p (a t)")[:, 0:2 * (CH - 1) * P].rearrange(
            "p (d c l) -> p d c l", d=2, l=P)
        Cout = hT[:, 12, 0:2 * (DV + 1)].rearrange("p (d v) -> p d v", d=2)
        W = hT[:, 14:16, :].rearrange("p d (c l) -> p d c l", l=P)
        rA = rt
        gbias = sb("gbias", [64, 2], ml_mem)
        m0col = sb("m0col", [64, 1], ml_mem)
        ri = sb("ri", [64, TOK], ml_mem)
        rf = sb("rf", [64, TOK], ml_mem)
        rM = sb("rM", [64, TOK + 1], ml_mem)
        bcol = sb("bcol", [P, CH, 64], ml_mem)
        eqcol = sb("eqcol", [P, CH, 64], ml_mem)
        bound = sb("bound", [P, 2, 4, CH], ml_mem)
        wsdec = sb("wsdec", [P, 2, 2, CH], ml_mem)
        Cst = sb("Cst", [P, 2, 4, DV + 1], ml_mem)
        dn = sb("dn", [P, 2], ml_mem)
        ml_mem.close()

        ret_mem = ExitStack()
        rope = hT[:, 14:16, :].rearrange("p a t -> p (a t)")[:, 0:2 * SAMPLE]
        Dm = ada_mem[:, :, :].rearrange("p s m -> p (s m)").rearrange("p (h l) -> p h l", l=P)
        Pm = diag
        Sout = sqsum[:, 0:2 * DV].rearrange("p (d v) -> p d v", d=2)
        zcol = sb("zcol", [P, 2, B_HEADS], ret_mem)
        cdcol = sb("cdcol", [P, 2, B_HEADS], ret_mem)
        XI = sb("XI", [P, 2, B_HEADS, P], ret_mem)
        Sst = sb("Sst", [P, 2, 4, DV], ret_mem)
        swapped = Sst[:, :, :, :].rearrange("p d s v -> p (d s v)").rearrange("p (q t) -> p q t", t=SAMPLE)
        ret_mem.close()
        mixer.close()

        ffn_mem = ExitStack()
        act_high = sb("act_high", [P, HALVES[0], TOK], ffn_mem, F32R)
        w_low = [sb(f"w_low{s}", [P, UNIT], ffn_mem, F32R) for s in range(2)]
        act_low = sb("act_low", [P, HALVES[0], TOK], ffn_mem, F32R)
        conv = sq
        ffn_mem.close()

        io_mem = ExitStack()
        for s in range(2, SLOTS):
            sb(f"ring_hole{s}", [P, UNIT], io_mem)
        rows = sb("rows", [P, 5, P], io_mem)
        xin = sb("xin", [P, CH, D_MODEL], io_mem)
        io_mem.close()
        krt = hT[:, 0, :]

        PJ = ctx.enter_context(nc.psum_tensor("PJ", [P, 2, 2, 512], F32))
        AT = ctx.enter_context(nc.psum_tensor("AT", [P, 4, 512], F32))
        ATf = AT[:, :, :].rearrange("p b n -> p (b n)")

        def chunks(bank):
            return ATf[:, bank * 512:bank * 512 + TOK].rearrange("p (c l) -> p c l", l=P)

        mean_sq = ATf[:, 1536 + 256:1536 + 256 + CH]
        rstd = ATf[:, 1024:1024 + TOK]

        ring_full = [sem(f"ring_full{s}") for s in range(SLOTS)]
        made = [sem(f"made{s}") for s in range(SLOTS)]
        turned = sem("turned")
        pj_free = [sem("pj_free0"), sem("pj_free1")]
        const_in, rows_in, x_in, rows_zero = sem("const_in"), sem("rows_in"), sem("x_in"), sem("rows_zero")
        h_split, l_split = [sem("h_split0"), sem("h_split1")], [sem("l_split0"), sem("l_split1")]
        uh_ready, ul_ready, acth_ready, ada_row = sem("uh_ready"), sem("ul_ready"), sem("acth_ready"), sem("ada_row")
        prod_ready, ada_done, mod_ready = sem("prod_ready"), sem("ada_done"), sem("mod_ready")
        diag_ready, rstd_full = sem("diag_ready"), sem("rstd_full")
        out_by_vector = sem("out_by_vector")
        silu_ready, out_by_scalar = sem("silu_ready"), sem("out_by_scalar")
        sq_ready, sq_added, stat_full = sem("sq_ready"), sem("sq_added"), sem("stat_full")
        std_ready, sum_zero = sem("std_ready"), sem("sum_zero")
        scaled_ready, u_ready, y_scaled, x_added = sem("scaled_ready"), sem("u_ready"), sem("y_scaled"), sem("x_added")
        conv_begun, gelu_ready, act_ready = sem("conv_begun"), sem("gelu_ready"), sem("act_ready")
        rope_ready, swap_in = sem("rope_ready"), sem("swap_in")
        score_full, p_ready, kz_ready, qz_ready = sem("score_full"), sem("p_ready"), sem("kz_ready"), sem("qz_ready")
        state_in, ds_full, st_ready, state_out = sem("state_in"), sem("ds_full"), sem("st_ready"), sem("state_out")
        ret_state_in = sem("ret_state_in")
        o_full, o_free, var_ready, hstd_ready = sem("o_full"), sem("o_free"), sem("var_ready"), sem("hstd_ready")
        hn_ready, ht_full, h_ready = sem("hn_ready"), sem("ht_full"), sem("h_ready")
        ml_in, ml_zero, rowf_ready, rowe_ready, rowb_ready = (sem("ml_in"), sem("ml_zero"), sem("rowf_ready"),
                                                              sem("rowe_ready"), sem("rowb_ready"))
        rowT_full, bc_full, arg_ready, exp_ready, bcol_ready = (sem("rowT_full"), sem("bc_full"), sem("arg_ready"),
                                                                sem("exp_ready"), sem("bcol_ready"))
        ret_in, ret_arg, ret_exp = sem("ret_in"), sem("ret_arg"), sem("ret_exp")
        out_staged, out_done, m_out = sem("out_staged"), sem("out_done"), sem("m_out")
        x_saved, x_back = sem("x_saved"), sem("x_back")
        dve_own, act_own = sem("dve_own"), sem("act_own")

        GROUPS = [A_HEADS // 2, B_HEADS // 2]
        HK = [A_HEADS * DK, B_HEADS * DK]
        HV = [A_HEADS * DV, B_HEADS * DV]
        w_in = [ml_w_in, ret_w_in]
        w_out = [ml_w_out, ret_w_out]
        OUT_TILES = [2, 1]
        OUT_UNITS = [2, 4]
        EVACS_BEFORE_ML = 4
        EVACS_BEFORE_RET = EVACS_BEFORE_ML + 9 * GROUPS[0] + KT // 2 + FT + KT
        ADA_FIRST, ADA_START = (0, 0, (0, 1, 2, 3), 1), (0, 4, (0, 1, 2, 3), 1)
        ADA_NORM, ADA_ROWS = (0, 8, (0, 1, 2, 3), 2), (0, 16, (2, 3), 4)
        ADA_LATER = {(0, 1): ((1, 0, (2, 3), 2), (1, 4, (2, 3), 2)), (1, 0): ((1, 8, (2, 3), 2), (1, 12, (2, 3), 2)),
                     (1, 1): ((1, 16, (2, 3), 2), (1, 20, (2, 3), 2))}
        FFN = (("up", HALVES[0] // 2, 0), ("down", KT // 2, 0), ("up", HALVES[1] // 2, HALVES[0]),
               ("down", KT // 2, HALVES[0]))
        OUT_BY_SCALAR = 3
        out_bank = [PJ[:, 0, 0, :], PJ[:, 0, 1, :], PJ[:, 1, 0, :], PJ[:, 1, 1, :], AT[:, 0, :]]
        block = ctx.enter_context(nc.Block())

        @block.sync
        def _(sp):
            uses = [Tally() for _ in range(SLOTS)]

            def load(slot, src, k, width, outputs):
                if uses[slot].turn is not None or uses[slot].n > 0:
                    sp.wait_ge(made[slot], uses[slot].now())
                dst = ring[slot][:, 0:k * width].rearrange("p (k m) -> p k m", k=k)
                sp.dma_start(dst, src.rearrange("(k p) m -> p k m", p=P)).then_inc(ring_full[slot], 16)
                uses[slot].add(outputs)

            def per(*outputs):
                return {f"s{s}": (uses[s], n) for s, n in enumerate(outputs)}

            splits = [Tally(), Tally()]

            def load_ffn(kind, layer, slot, n, first, up, down):
                if kind == "up":
                    dst = ring[slot][:, :].rearrange("p (b k m) -> p b k m", k=KT, b=2)
                    for b in range(2):
                        sp.dma_start(dst[:, b, :, :], up[:, ds(n * P + (first * P + b * D_FF), P)].rearrange(
                            "(k p) m -> p k m", p=P)).then_inc(ring_full[slot], 16)
                else:
                    half = HALVES[int(first > 0)] // 2
                    dst = ring[slot][:, 0:2 * half * P].rearrange("p (b k m) -> p b k m", k=half, b=2)
                    for b in range(2):
                        lo = (first + b * half) * P
                        sp.dma_start(dst[:, b, :, :], down[lo:lo + half * P, ds(n * P, P)].rearrange(
                            "(k p) m -> p k m", p=P)).then_inc(ring_full[slot], 16)

            def load_ada(part):
                layer, first, slots, turns = part
                n = len(slots)
                with loop(sp, turns, **per(*[int(s in slots) for s in range(SLOTS)])) as i:
                    for j, s in enumerate(slots):
                        load(s, ada_w[layer, :, ds((i * n + (first + j)) * 256, 256)], KT, 256, 1)

            sp.wait_ge(rows_zero, 1)
            sp.dma_start(rows[0:96, 1, :], ada_b.rearrange("l (t m) -> (l t) m", m=P)).then_inc(rows_in, 16)
            cr = ffn_conv.rearrange("l w (t m) -> (l w t) m", m=P)
            sp.dma_start(rows[:, 2, :], cr[0:P, :]).then_inc(rows_in, 16)
            sp.dma_start(rows[:, 3, :], cr[P:2 * P, :]).then_inc(rows_in, 16)
            sp.dma_start(rows[0:8, 4, :], cr[2 * P:264, :]).then_inc(rows_in, 16)
            sp.dma_start(rows[8:96, 4, :], ffn_conv_b.rearrange("l (t m) -> (l t) m", m=P)).then_inc(rows_in, 16)
            for j in range(SLOTS):
                load(j, ada_w[0, :, j * 256:(j + 1) * 256], KT, 256, 1)
            sp.dma_start(xin[:, 0, :], x_prompt[0]).then_inc(x_in, 16)
            sp.dma_start(xin[:, 1:CH, :], x_sample[0].rearrange("(c p) d -> p c d", p=P)).then_inc(x_in, 16)
            load_ada(ADA_START)
            load_ada(ADA_NORM)
            for layer in range(DEPTH):
                hk, hv, w = HK[layer], HV[layer], w_in[layer]

                def load_qk(g):
                    load(0, w[0, :, ds(g * 256, 256)], KT, 256, 2)
                    load(1, w[0, :, ds(g * 256 + hk, 256)], KT, 256, 2)

                def load_v_gates(g):
                    load(2, w[0, :, ds(g * 512 + 2 * hk, 256)], KT, 256, CH)
                    load(3, w[0, :, ds(g * 512 + (2 * hk + 256), 256)], KT, 256, CH)
                    load(0, w[0, :, ds(g * 512 + (2 * hk + hv), 256)], KT, 256, 2)
                    load(1, w[0, :, ds(g * 512 + (2 * hk + hv + 256), 256)], KT, 256, 2)

                load_qk(0)
                for part in [ADA_ROWS] if layer == 0 else ADA_LATER[1, 0]:
                    load_ada(part)
                with loop(sp, GROUPS[layer] - 1, **per(4, 4, CH, CH)) as g:
                    load_v_gates(g)
                    load_qk(g + 1)
                load_v_gates(GROUPS[layer] - 1)
                for s in range(2):
                    splits[s].add(3 * GROUPS[layer])
                n, tiles = OUT_UNITS[layer], OUT_TILES[layer]
                with loop(sp, 2, **per(*[tiles * int(s < n) for s in range(4)])) as i:
                    for j in range(n):
                        load(j, w_out[layer][0, :, ds((i * n + j) * (tiles * P), tiles * P)], hv // P, tiles * P, tiles)
                up, down = ffn_w_up[layer], ffn_w_down[layer]
                for kind, turns, first in FFN:
                    start = kind == "up" and first == 0
                    if start:
                        for s in range(2):
                            sp.wait_ge(made[s], uses[s].now())
                            load_ffn(kind, layer, s, s, first, up, down)
                        for part in ADA_LATER[layer, 1]:
                            load_ada(part)
                    with loop(sp, turns - start, sp0=(splits[0], 1), sp1=(splits[1], 1)) as i:
                        for s in range(2):
                            sp.wait_ge(l_split[s], splits[s].add())
                            load_ffn(kind, layer, s, i * 2 + (s + 2 * start), first, up, down)
                for s in range(2):
                    splits[s].add()
                    uses[s].add(HALVES[0] + HALVES[1] + KT)
                    sp.wait_ge(made[s], uses[s].now())

            for half in range(2):
                for c in range(CH):
                    if half == 1 and c >= OUT_BY_SCALAR:
                        sp.wait_ge(out_by_vector, c + 1 - OUT_BY_SCALAR)
                    else:
                        sp.wait_ge(out_by_scalar, half * CH + c + 1)
                    cut = slice(half * 4 * P, (half + 1) * 4 * P)
                    sp.dma_start(y_prompt[0][:, cut] if c == 0 else y_sample[0, (c - 1) * P:c * P, cut], xin[:, c, cut]
                                 ).then_inc(out_done, 16)
            sp.wait_ge(out_done, 16 * 2 * CH)
            sp.wait_ge(state_out, 16 * (4 * A_HEADS + 2 * B_HEADS))
            sp.wait_ge(m_out, 32)

        @block.gpsimd
        def _(pool):
            sqn, stn, hd = Tally(), Tally(), Tally()

            def norm_sums(turns, per):
                pool.wait_ge(stat_full, stn.now())
                pool.memset(sqsum[:, :], 0.0).then_inc(sum_zero, 1)
                stn.add()
                pool.wait_ge(sum_zero, stn.now())
                if per is None:
                    for k in range(turns):
                        step_sum(k)
                else:
                    with loop(pool, turns, sq=(sqn, per)) as _:
                        for k in range(per):
                            step_sum(k)

            def step_sum(k):
                pool.wait_ge(sq_ready, sqn.add())
                pool.wait_ge(sq_added, sqn.now(1))
                pool.tensor_tensor(sqsum[:, :], sqsum[:, :], sq[:, k % 2, :], ALU.add).then_inc(sq_added, 1)

            pool.memset(rows[:, :, :], 0.0).then_inc(rows_zero, 1)
            with nc.allow_non_contiguous_dma(reason="sixteen decay exponents to every partition"):
                pool.dma_start(dcy[:, 0, :], ret_decay.rearrange("a d h -> a (d h)").to_broadcast(
                    [P, 16])).then_inc(ret_in, 16)

            def save_x():
                pool.wait_ge(u_ready, (2 * layer + 1) * KT)
                pool.dma_start(x_saved_dram, xT[:, :, :]).then_inc(x_saved, 16)
                pool.wait_ge(x_saved, 16 * (layer + 1))
                pool.memset(vt[:, :, :, DV:DV + 1], 1.0).then_inc(ml_zero, 1)

            for layer in range(DEPTH):
                if layer == 0:
                    pool.wait_ge(turned, CH + 1)
                    pool.memset(wg[:, :, :, :], 0.0).then_inc(ml_zero, 1)
                    pool.memset(gbias[:, :], 0.0).then_inc(ml_zero, 1)
                    pool.memset(m0col[:, :], 0.0).then_inc(ml_zero, 1)
                    pool.memset(rone[:, :], 1.0).then_inc(ml_zero, 1)
                    pool.wait_ge(ml_zero, 4)
                    with nc.allow_non_contiguous_dma(reason="a few gate columns and biases"):
                        pool.dma_start(mlc[:, :], k_ml).then_inc(ml_in, 16)
                        gw = ml_w_in[0, :, 2 * HK[0] + 2 * HV[0]:].rearrange("(k p) m -> p k m", p=P)
                        for d in range(2):
                            for kind in range(2):
                                s = (2 * d + kind) * A_HEADS
                                pool.dma_start(wg[:, :, kind, 32 * d:32 * d + A_HEADS],
                                               gw[:, :, s:s + A_HEADS]).then_inc(ml_in, 16)
                                pool.dma_start(gbias[32 * d:32 * d + A_HEADS, kind:kind + 1],
                                               ml_b_gate[0, 2 * d + kind, :].unsqueeze(1)).then_inc(ml_in, 16)
                            pool.dma_start(m0col[32 * d:32 * d + A_HEADS, :],
                                           st_m[0, 0, d, :].unsqueeze(1)).then_inc(ml_in, 16)
                    norm_sums(KT, None)
                    save_x()

                    def ml_head(h):
                        hd.add()
                        if h > 0:
                            pool.wait_ge(hn_ready, hd.now(1))
                        for d in range(2):
                            pool.dma_start(Cst[:, d, 0, 0:DV], st_C[0, 0, d, h]).then_inc(state_in, 16)
                            with nc.allow_non_contiguous_dma(reason="normaliser state, one number a partition"):
                                pool.dma_start(Cst[:, d, 0, DV:DV + 1],
                                               st_n[0, 0, d, h, :].unsqueeze(1)).then_inc(state_in, 16)
                        pool.wait_ge(exp_ready, h + 1)
                        for d in range(2):
                            pool.tensor_tensor(qz[d][:, :, :].rearrange("p c l -> p (c l)"), qk[:, h % 2, PROMPT:TOK],
                                               winter[:, d, :, :].rearrange("p c l -> p (c l)"),
                                               ALU.mult).then_inc(qz_ready, 1)

                    pool.wait_ge(rowb_ready, 2)
                    with nc.allow_non_contiguous_dma(reason="one number a partition"):
                        for d in range(2):
                            pool.dma_start(new_m[0, 0, d, :].unsqueeze(1), m0col[32 * d:32 * d + A_HEADS, :]
                                           ).then_inc(m_out, 16)
                    for h in range(A_HEADS):
                        ml_head(h)
                else:
                    pool.dma_start(krt, k_ret[:, 0:TOK]).then_inc(ret_in, 16)
                    pool.dma_start(rope[:, :], k_ret[:, TOK:TOK + 2 * SAMPLE]).then_inc(ret_in, 16)
                    norm_sums(KT, None)
                    save_x()
                    pool.wait_ge(ret_exp, 3)
                    ropn = Tally()
                    with loop(pool, GROUPS[1], ropn=(ropn, 1), hd=(hd, 2)) as g:
                        pool.wait_ge(rope_ready, ropn.add())
                        for hh in range(2):
                            pool.wait_ge(hn_ready, hd.add() - 1)
                            for d in range(2):
                                pool.tensor_tensor(
                                    qz[d][:, :, :], qk[:, hh, PROMPT:TOK].rearrange("p (c l) -> p c l", l=P),
                                    XI[:, d, ds(g * 2 + hh, 1), :].to_broadcast([P, CH - 1, P]),
                                    ALU.mult).then_inc(qz_ready, 1)
                if layer == 1:
                    pool.wait_ge(state_out, 64 * A_HEADS + 32 * B_HEADS)
                norm_sums(2, 4)
                norm_sums(KT, None)
                norm_sums(KT // 2, 2)

        @block.scalar
        def _(a):
            pjn, sqn, stn, scn, xan = Tally(), Tally(), Tally(), Tally(), Tally()
            free, actn, own = [Tally(), Tally()], Tally(), Tally()
            gaten, hd, turnn, prodn = Tally(), Tally(), Tally(), Tally()
            outs = [Tally() for _ in range(SLOTS)]
            landed = [Tally() for _ in range(SLOTS)]
            adan = Tally()

            def link(ins):
                ins.then_inc(act_own, 1)
                a.wait_ge(act_own, own.add())

            def norm_std():
                a.wait_ge(stat_full, stn.add())
                a.activation(tok_rstd[:, :], mean_sq, ACT.Sqrt, bias=eps[:, 0:1]).then_inc(std_ready, 1)

            def square(src, k):
                if sqn.turn is not None or sqn.n >= 2:
                    a.wait_ge(sq_added, sqn.now(1))
                sqn.add()
                a.activation(sq[:, k % 2, :], src, ACT.Square).then_inc(sq_ready, 1)

            def high_weights(s):
                a.wait_ge(ring_full[s], landed[s].add(2) * 16)
                a.wait_ge(made[s], outs[s].now())
                a.activation(w_high[s][:, :], ring[s][:, :], ACT.Copy).then_inc(h_split[s], 1)

            def high_unit(s, before):
                a.wait_ge(ring_full[s], landed[s].add() * 16)
                a.wait_ge(made[before], outs[before].now())
                a.activation(w_high[s % 2][:, :], ring[s][:, :], ACT.Copy).then_inc(h_split[s % 2], 1)

            def ada_row_out(part, n):
                j = n % len(part[2])
                a.wait_ge(made[part[2][j]], outs[part[2][j]].add())
                if n >= len(part[2]):
                    a.wait_ge(ada_done, adan.n + n // len(part[2]))
                a.activation(ada_rows[:, j, :], PJ[0:2, j // 2, j % 2, 0:256], ACT.Copy).then_inc(ada_row, 1)
                if n == len(part[2]) * part[3] - 1:
                    adan.add(part[3])

            def prenorm(which, sub, during_squares, during_scaling):
                first_units, units = (len(part[2]) * part[3] for part in (during_squares, during_scaling))
                for k in range(KT):
                    if which > 0:
                        a.wait_ge(x_added, xan.add())
                    square(xT[:, k, :], k)
                    if (k + 1) % (KT // first_units) == 0:
                        ada_row_out(during_squares, k // (KT // first_units))
                norm_std()
                for k in range(KT):
                    if k and k % (KT // units) == 0:
                        ada_row_out(during_scaling, k // (KT // units) - 1)
                    a.wait_ge(scaled_ready, scn.add())
                    for grp, (lo, hi) in enumerate(((0, PROMPT), (PROMPT, TOK))):
                        ins = a.activation(uT[:, k, lo:hi], uT[:, k, lo:hi], ACT.Identity,
                                           bias=mod[:, which // 2, sub * 24 + k, grp:grp + 1])
                    ins.then_inc(u_ready, 1)
                    a.wait_ge(u_ready, which * KT + k + 1)
                    a.activation(u_high[:, k, :], uT[:, k, :], ACT.Copy).then_inc(uh_ready, 1)
                    if k < 2 and sub == 1:
                        high_weights(k)
                    elif k < 2 and which == 2:
                        high_unit(k, k)
                ada_row_out(during_scaling, units - 1)

            def pj(slot):
                a.wait_ge(made[slot], outs[slot].add())
                pjn.add()
                free[(pjn.n - 1) % 2].add()
                return (pjn.n - 1) % 2

            def pj_turned():
                a.wait_ge(turned, turnn.add())
                pjn.add()
                free[(pjn.n - 1) % 2].add()
                return (pjn.n - 1) % 2

            def per(*outputs):
                return {f"o{s}": (outs[s], n) for s, n in enumerate(outputs)}

            def y_squares(turns, per):
                with loop(a, turns, sq=(sqn, per), f0=(free[0], per // 2), f1=(free[1], per // 2)) as i:
                    for k in range(per):
                        s = (pjn.n + k) % 2
                        a.wait_ge(pj_free[s], free[s].add())
                        square(uT[:, ds(i * per + k, 1), :].rearrange("p a t -> p (a t)"), k)
                pjn.add(turns * per)
                norm_std()

            a.dma_start(common[:, :], k_common).then_inc(const_in, 16)
            a.wait_ge(rows_zero, 1)
            a.dma_start(rows[0:64, 0, :], norm_gain.rearrange("l w (t m) -> (l w t) m", m=P)).then_inc(rows_in, 16)
            a.dma_start(rows[64:72, 0, :], c_ctx.rearrange("(t m) -> t m", m=P)).then_inc(rows_in, 16)
            a.dma_start(rows[72:80, 0, :], c_lat.rearrange("b (t m) -> (b t) m", m=P)).then_inc(rows_in, 16)
            a.dma_start(rows[80:88, 0, :], ml_norm.rearrange("a h (t m) -> (a h t) m", m=P)).then_inc(rows_in, 16)
            a.dma_start(rows[88:104, 0, :], ret_norm.rearrange("a h (t m) -> (a h t) m", m=P)).then_inc(rows_in, 16)

            a.wait_ge(pj_free[0], 1)
            pjn.add(CH + 1)
            turnn.add(CH + 1)
            for grp, col in ((0, COL_CCTX), (1, COL_C)):
                a.activation(silu_c[:, :, grp:grp + 1], cols[:, col:col + KT].unsqueeze(2), ACT.Silu).then_inc(silu_ready, 1)
            for n in range(SLOTS):
                ada_row_out(ADA_FIRST, n)
            a.wait_ge(pj_free[0], 3)
            a.wait_ge(pj_free[1], 3)
            free[0].n = free[1].n = 3

            for layer in range(DEPTH):
                if layer == 0:
                    prenorm(0, 0, ADA_START, ADA_NORM)
                else:
                    prenorm(2, 0, *ADA_LATER[1, 0])
                    for s in (2, 3):
                        landed[s].add(8)
                if layer == 0:
                    a.wait_ge(ml_in, 16 * 11)
                    s = pj_turned()
                    a.activation(ri[:, :].rearrange("p (b t) -> p b t", b=2), PJ[0:64, s, :, 0:HALF], ACT.Identity,
                                 bias=gbias[:, 0:1]).then_inc(pj_free[s], 1)
                    s = pj_turned()
                    a.activation(rf[:, :].rearrange("p (b t) -> p b t", b=2), PJ[0:64, s, :, 0:HALF], ACT.Identity,
                                 bias=gbias[:, 1:2]).then_inc(pj_free[s], 1)
                    for s in range(SLOTS):
                        landed[s].add((4, 4, 8, 8)[s])
                    for s in range(2):
                        high_unit(s, s)
                    a.wait_ge(ret_in, 16)
                    a.activation(dcy[:, 1, :], dcy[:, 0, :], ACT.Exp, scale=-math.log(2.0)).then_inc(ret_exp, 1)
                    a.wait_ge(rowf_ready, 1)
                    link(a.activation(rt[:, :], rt[:, :], ACT.Exp, scale=-1.0))
                    a.activation(rt[:, :], rt[:, :], ACT.Ln, bias=1.0).then_inc(rowe_ready, 1)
                    a.wait_ge(ret_arg, 1)
                    a.activation(dcy[:, 3, :], dcy[:, 2, :], ACT.Ln).then_inc(ret_exp, 1)
                    for n in range(8):
                        ada_row_out(ADA_ROWS, n)
                else:
                    a.wait_ge(ret_arg, 2)
                    link(a.activation(Dm[:, :, :].rearrange("p h l -> p (h l)"), Dm[:, :, :].rearrange("p h l -> p (h l)"), ACT.Exp))
                    a.activation(XI[:, :, :, :].rearrange("p d h l -> p (d h l)"),
                                 XI[:, :, :, :].rearrange("p d h l -> p (d h l)"), ACT.Exp)
                    a.activation(zcol[:, :, :].rearrange("p d h -> p (d h)"), zcol[:, :, :].rearrange("p d h -> p (d h)"), ACT.Exp)
                    a.activation(cdcol[:, :, :].rearrange("p d h -> p (d h)"), dcy[:, 5, :], ACT.Exp,
                                 scale=float(P)).then_inc(ret_exp, 1)
                    a.wait_ge(ret_exp, 3)

                def evac_qkv():
                    for t in range(4):
                        s = pj(t // 2)
                        a.activation(qk[:, t, :].rearrange("p (b t) -> p b t", b=2), PJ[:, s, :, 0:HALF], ACT.Copy,
                                     scale=1.0 if t < 2 else DK ** -0.5).then_inc(pj_free[s], 1)
                        if t == 1:
                            high_unit(2, 0)
                    if layer == 1:
                        a.wait_ge(pj_free[0], free[0].now())
                        a.wait_ge(pj_free[1], free[1].now())
                        for q in range(4):
                            a.dma_start(swapped[32 * q:32 * q + 32, :, :],
                                        qk[32 * (q ^ 1):32 * (q ^ 1) + 32, :, PROMPT:TOK]).then_inc(swap_in, 16)
                    high_unit(3, 1)
                    a.wait_ge(x_saved, 16 * (layer + 1))
                    for t in range(2 * CH):
                        s = pj(2 + t // CH)
                        a.activation(vt[:, t % CH, t // CH, 0:DV], PJ[:, s, 0, 0:DV], ACT.Copy).then_inc(pj_free[s], 1)
                        if t == CH - 1:
                            high_unit(0, 2)

                def evac_gate(t):
                    s = pj(t // 2)
                    if t == 0:
                        a.wait_ge(h_ready, gaten.now())
                        gaten.add(2)
                    a.activation(gt[:, t, :].rearrange("p (b t) -> p b t", b=2), PJ[:, s, :, 0:HALF],
                                 ACT.Sigmoid if layer == 0 else ACT.Silu).then_inc(pj_free[s], 1)

                def head_std():
                    hd.add()
                    a.wait_ge(var_ready, hd.now())
                    a.activation(hstd[:, :], mv[:, :, 1], ACT.Sqrt, bias=eps[:, 0:1]).then_inc(hstd_ready, 1)

                if layer == 0:
                    for g in range(GROUPS[0]):
                        evac_qkv()
                        if g == 0:
                            a.wait_ge(rowT_full, 1)
                            a.activation(eqcol[:, :, :].rearrange("p c r -> p (c r)"), AT[:, 1, 0:CH * 64], ACT.Exp
                                         ).then_inc(bcol_ready, 1)
                        for hh in range(2):
                            h = 2 * g + hh
                            a.wait_ge(arg_ready, h + 1)
                            a.activation(W[:, :, :, :].rearrange("p d c l -> p (d c l)"),
                                         W[:, :, :, :].rearrange("p d c l -> p (d c l)"), ACT.Exp)
                            for d in range(2):
                                bc = chunks(2 * d)
                                for c in range(1, CH):
                                    a.activation(winter[:, d, c - 1, :], bc[:, c, :], ACT.Exp,
                                                 bias=bound[:, d, 1, c:c + 1])
                            a.activation(wsdec[:, :, :, :], bound[:, :, 2:4, :], ACT.Exp).then_inc(exp_ready, 1)
                            evac_gate(3 * hh)
                            a.wait_ge(exp_ready, h + 1)
                            a.wait_ge(score_full, h + 1)
                            for d in range(2):
                                for c in range(CH):
                                    ins = a.activation(kz[d][:, c, :], chunks(2)[:, c, :], ACT.Copy,
                                                       scale=wsdec[:, d, 0, c:c + 1])
                            ins.then_inc(kz_ready, 1)
                            if hh == 0:
                                high_unit(1, 3)
                                evac_gate(1)
                            a.wait_ge(out_staged, h + 1)
                            for d in range(2):
                                a.dma_start(new_C[0, 0, d, h], Cout[:, d, 0:DV]).then_inc(state_out, 16)
                                with nc.allow_non_contiguous_dma(reason="one number a partition"):
                                    a.dma_start(new_n[0, 0, d, h, :].unsqueeze(1), Cout[:, d, DV:DV + 1]).then_inc(state_out, 16)
                            head_std()
                            if g + 1 < GROUPS[0]:
                                high_unit(hh, hh)
                            if hh == 0:
                                evac_gate(2)
                else:
                    scn_h, stg = Tally(), Tally()
                    scn_h.n, stg.n = A_HEADS, A_HEADS

                    def ret_group(g, last):
                        evac_qkv()
                        for hh in range(2):
                            a.wait_ge(score_full, scn_h.add())
                            for d in range(2):
                                a.dma_start(Sst[:, d, 0, :], st_S[0, 0, d, ds(g * 2 + hh, 1)].rearrange(
                                    "a k v -> (a k) v")).then_inc(ret_state_in, 16)
                            for d in range(2):
                                ins = a.activation(kz[d][:, :, :], chunks(2), ACT.Copy,
                                                   scale=zcol[:, d, ds(g * 2 + hh, 1)])
                            ins.then_inc(kz_ready, 1)
                            if hh == 0:
                                high_unit(1, 3)
                                evac_gate(0)
                                evac_gate(1)
                            else:
                                evac_gate(3)
                            a.wait_ge(out_staged, stg.add())
                            for d in range(2):
                                a.dma_start(new_S[0, 0, d, ds(g * 2 + hh, 1)].rearrange("a k v -> (a k) v"),
                                            Sout[:, d, :]).then_inc(state_out, 16)
                            head_std()
                            if not last:
                                high_unit(hh, hh)
                            if hh == 0:
                                evac_gate(2)

                    with loop(a, GROUPS[1] - 1, pjn=(pjn, 18), f0=(free[0], 9), f1=(free[1], 9), **per(4, 4, CH, CH),
                              gate=(gaten, 2), hd=(hd, 2), sc=(scn_h, 2), stg=(stg, 2),
                              **{f"l{s}": (landed[s], (2, 2, 1, 1)[s]) for s in range(SLOTS)}) as g:
                        ret_group(g, False)
                    ret_group(GROUPS[1] - 1, True)
                a.wait_ge(h_ready, A_HEADS + layer * B_HEADS)
                a.dma_start(xT[:, :, :], x_saved_dram).then_inc(x_back, 16)
                y_squares(2, 4)
                for s in range(OUT_UNITS[layer]):
                    outs[s].add(2 * OUT_TILES[layer])
                for s in range(OUT_UNITS[layer]):
                    landed[s].add(2)
                prenorm(2 * layer + 1, 1, *ADA_LATER[layer, 1])

                def up_pair(t, tile, s_in):
                    for b in range(2):
                        s = pj(s_in)
                        a.activation(conv[:, b, :].rearrange("p (b t) -> p b t", b=2), PJ[:, s, :, 0:HALF],
                                     ACT.Identity, scale=cols[:, ds(t + (COL_CONV + (layer * 3 + 1) * 2 * FT + b * FT), 1)],
                                     bias=cols[:, ds(t + (COL_CONVB + layer * 2 * FT + b * FT), 1)]).then_inc(conv_begun, 1)
                        if b == 0:
                            a.wait_ge(pj_free[s], free[s].now())
                            a.activation(conv[:, 0, :], conv[:, 0, :], ACT.Gelu_apprx_tanh).then_inc(gelu_ready, 1)
                        else:
                            high_weights(s_in)
                    a.wait_ge(prod_ready, prodn.add())
                    a.activation(act_high[:, ds(tile, 1), :].rearrange("p a t -> p (a t)"), conv[:, 1, :], ACT.Copy
                                 ).then_inc(acth_ready, 1)
                    a.wait_ge(act_ready, actn.add())

                def down_tile(m, s_in, k, half):
                    s = pjn.n % 2
                    pjn.add()
                    outs[s_in].add()
                    free[s].add()
                    if half:
                        a.wait_ge(pj_free[s], free[s].now())
                        square(uT[:, ds(m, 1), :].rearrange("p a t -> p (a t)"), k)

                for kind, turns, first in FFN:
                    out_per = 2 if kind == "up" else 1
                    tallies = dict(pjn=(pjn, 2 * out_per), f0=(free[0], out_per), f1=(free[1], out_per),
                                   o0=(outs[0], out_per), o1=(outs[1], out_per), l0=(landed[0], 2), l1=(landed[1], 2))
                    if kind == "up":
                        with loop(a, turns, **tallies, act=(actn, 2), prod=(prodn, 2)) as i:
                            for j in range(2):
                                up_pair(i * 2 + (first + j), i * 2 + j, j)
                    elif first == 0:
                        with loop(a, turns, **tallies) as i:
                            for j in range(2):
                                down_tile(i * 2 + j, j, j, 0)
                                high_weights(j)
                    else:
                        with loop(a, turns - 1, **tallies, sq=(sqn, 2)) as i:
                            for j in range(2):
                                down_tile(i * 2 + j, j, j, 1)
                                high_weights(j)
                        for j in range(2):
                            down_tile(KT - 2 + j, j, j, 1)
                norm_std()

            for half in range(2):
                for c in range(CH if half == 0 else OUT_BY_SCALAR):
                    a.wait_ge(turned, turnn.n + half * CH + c + 1)
                    a.activation(xin[:, c, half * 4 * P:(half + 1) * 4 * P], out_bank[c], ACT.Copy
                                 ).then_inc(out_by_scalar, 1)

        @block.vector
        def _(v):
            own, pjn, stn, yn = Tally(), Tally(), Tally(), Tally()
            free, cvn, gen, hd = [Tally(), Tally()], Tally(), Tally(), Tally()
            turnn = Tally()
            outs = [Tally() for _ in range(SLOTS)]

            def link(ins):
                ins.then_inc(dve_own, 1)
                v.wait_ge(dve_own, own.add())

            def pj(slot):
                v.wait_ge(made[slot], outs[slot].add())
                pjn.add()
                return (pjn.n - 1) % 2

            def pj_turned():
                v.wait_ge(turned, turnn.add())
                pjn.add()
                return (pjn.n - 1) % 2

            def per(*outputs):
                return {f"o{s}": (outs[s], n) for s, n in enumerate(outputs)}

            def norm_rstd():
                v.wait_ge(std_ready, stn.add())
                link(v.reciprocal(tok_rstd[:, :], tok_rstd[:, :]))
                v.tensor_tensor(diag[:, :, :], ident.unsqueeze(1).to_broadcast([P, CH, P]),
                                tok_rstd[:, :].unsqueeze(2).to_broadcast([P, CH, P]), ALU.mult).then_inc(diag_ready, 1)
                v.wait_ge(rstd_full, stn.now())

            highs = [Tally(), Tally()]

            def low_weights(s):
                v.wait_ge(h_split[s], highs[s].add())
                v.tensor_tensor(w_low[s][:, :], ring[s][:, :], w_high[s][:, :].bitcast(F32), ALU.subtract
                                ).then_inc(l_split[s], 1)

            def low_unit(s):
                v.wait_ge(h_split[s % 2], highs[s % 2].add())
                v.tensor_tensor(ring_low[s][:, :], ring[s][:, :], w_high[s % 2][:, :].bitcast(F32), ALU.subtract
                                ).then_inc(l_split[s % 2], 1)

            def split_input(which, weights):
                for k in range(KT):
                    v.wait_ge(uh_ready, which * KT + k + 1)
                    v.tensor_tensor(u_low[:, k, :], uT[:, k, :], u_high[:, k, :].bitcast(F32), ALU.subtract
                                    ).then_inc(ul_ready, 1)
                    if k < 2 and weights:
                        weights(k)

            def scale_tiles(src, factor, signal):
                for k in range(KT):
                    for grp, (lo, hi) in enumerate(((0, PROMPT), (PROMPT, TOK))):
                        ins = v.scalar_tensor_tensor(uT[:, k, lo:hi], src[:, k, lo:hi], factor[:, k, grp:grp + 1],
                                                     rstd[:, lo:hi], ALU.mult, ALU.mult)
                    ins.then_inc(signal, 1)
                    if signal is y_scaled and k:
                        add_residual(k - 1)
                if signal is y_scaled:
                    add_residual(KT - 1)

            def add_residual(k):
                v.wait_ge(y_scaled, yn.add())
                v.tensor_tensor(xT[:, k, :], xT[:, k, :], uT[:, k, :], ALU.add).then_inc(x_added, 1)

            def modulate(part, tiles):
                layer = part[0]
                v.wait_ge(ada_done, done_after[part])
                ab = COL_ADAB + layer * 48
                lo, hi = tiles
                ins = v.tensor_tensor(mod[:, layer, lo:hi, :], AT[:, 0, 2 * lo:2 * hi].rearrange("p (t g) -> p t g", g=2),
                                      cols[:, ab + lo:ab + hi].unsqueeze(2).to_broadcast([P, hi - lo, 2]), ALU.add)
                ins.then_inc(mod_ready, 1)
                v.wait_ge(mod_ready, modn.add())

            def gain(layer, w):
                at = COL_GAIN + (layer * 4 + w) * KT
                return cols[:, at:at + KT].unsqueeze(2).to_broadcast([P, KT, 2])

            def pre_factor(layer, sub):
                link(v.scalar_tensor_tensor(pre_a[:, sub, :, :], mod[:, layer, sub * 24 + 8:sub * 24 + 16, :], 1.0,
                                            gain(layer, 2 * sub), ALU.add, ALU.mult))

            def post_factor(layer, sub):
                link(v.tensor_tensor(post_a[:, sub, :, :], mod[:, layer, sub * 24 + 16:sub * 24 + 24, :],
                                     gain(layer, 2 * sub + 1), ALU.mult))

            modn = Tally()
            done_after, total = {}, 0
            for part in (ADA_FIRST, ADA_START, ADA_NORM, ADA_ROWS, *ADA_LATER[0, 1], *ADA_LATER[1, 0], *ADA_LATER[1, 1]):
                total += part[3]
                done_after[part] = total

            def y_copies(turns, slots, outputs):
                with loop(v, turns, pjn=(pjn, len(slots)), **per(*outputs)) as i:
                    for k, slot in enumerate(slots):
                        s = pj(slot)
                        v.tensor_copy(uT[:, ds(i * len(slots) + k, 1), :].rearrange("p a (b t) -> p (a b) t", b=2),
                                      PJ[:, s, :, 0:HALF]).then_inc(pj_free[s], 1)

            v.memset(eps[:, :], EPS)
            s = pj_turned()
            v.tensor_copy(cols[:, :], PJ[:, s, :, :].rearrange("p b n -> p (b n)")[:, 0:COLS]).then_inc(pj_free[s], 1)
            for c in range(CH):
                s = pj_turned()
                v.tensor_copy(xT[:, :, c * P:(c + 1) * P], PJ[:, s, :, :].rearrange("p b (k t) -> p (b k) t", t=P)
                              ).then_inc(pj_free[s], 1)

            for layer in range(DEPTH):
                if layer == 0:
                    for s in range(SLOTS):
                        outs[s].add((4, 4, 8, 8)[s])
                    modulate(ADA_START, (0, 16))
                else:
                    modulate(ADA_LATER[1, 0][0], (16, 24))
                pre_factor(layer, 0)
                norm_rstd()
                scale_tiles(xT, pre_a[:, 0], scaled_ready)
                split_input(2 * layer, low_unit if layer == 1 else None)
                if layer == 1:
                    modulate(ADA_LATER[1, 0][1], (24, 32))
                    post_factor(1, 0)
                if layer == 0:
                    pjn.add(2)
                    turnn.add(2)
                    v.wait_ge(pj_free[0], 4)
                    v.wait_ge(pj_free[1], 4)
                    v.scalar_tensor_tensor(rt[:, :], rf[:, :], -1.0, rf[:, :], ALU.mult, ALU.max).then_inc(rowf_ready, 1)
                    v.wait_ge(ret_exp, 1)
                    v.tensor_scalar(dcy[:, 2, :], dcy[:, 1, :], -1.0, 1.0, ALU.mult, ALU.add).then_inc(ret_arg, 1)
                    for s in range(2):
                        low_unit(s)
                    v.wait_ge(rowf_ready, 1)
                    v.wait_ge(rowe_ready, 1)
                    link(v.scalar_tensor_tensor(rf[:, :], rf[:, :], 0.0, rt[:, :], ALU.min, ALU.subtract))
                    dirs = ((0, slice(0, PROMPT), slice(PROMPT, TOK)),
                            (32, slice(PROMPT - 1, None, -1), slice(TOK - 1, PROMPT - 1, -1)))
                    for r, pr, sa in dirs:
                        for part in (pr, sa):
                            ins = v.tensor_tensor_scan(rA[r:r + 32, part], rone[r:r + 32, part], rf[r:r + 32, part],
                                                       0.0, ALU.mult, ALU.add)
                    link(ins)
                    link(v.tensor_tensor(ri[:, :], ri[:, :], rA[:, :], ALU.subtract))
                    for r, pr, sa in dirs:
                        for part, first in ((pr, 0.0), (sa, m0col[r:r + 32, 0:1])):
                            v.tensor_tensor_scan(rM[r:r + 32, part], ri[r:r + 32, part], ri[r:r + 32, part],
                                                 first, ALU.max, ALU.max)
                    link(v.tensor_copy(rM[:, TOK:TOK + 1], m0col[:, :]))
                    v.scalar_tensor_tensor(rf[:, :], rM[:, 0:TOK], -1.0, rA[:, :], ALU.mult, ALU.subtract
                                           ).then_inc(rowb_ready, 1)
                    v.wait_ge(rowb_ready, 1)
                    for r in (0, 32):
                        ins = v.tensor_scalar(m0col[r:r + 4, :], rf[r:r + 4, PROMPT - 1:PROMPT] if r == 0 else rf[r:r + 4, 0:1],
                                              -1.0, None, ALU.mult)
                    ins.then_inc(rowb_ready, 1)
                    v.wait_ge(ret_arg, 1)
                    link(v.tensor_scalar(dcy[:, 4, :], dcy[:, 2, :], -1.0, 1.0, ALU.mult, ALU.add))
                    link(v.tensor_scalar(dcy[:, 4, :], dcy[:, 4, :], 1e-30, None, ALU.add))
                    link(v.reciprocal(dcy[:, 4, :], dcy[:, 4, :]))
                    v.wait_ge(ret_exp, 2)
                    link(v.tensor_scalar(dcy[:, 3, :], dcy[:, 3, :], -1.0, 1e-30, ALU.mult, ALU.add))
                    link(v.tensor_tensor(dcy[:, 3, :], dcy[:, 3, :], dcy[:, 4, :], ALU.mult))
                    link(v.scalar_tensor_tensor(dcy[:, 5, :], dcy[:, 3, :], -1.0, dcy[:, 1, :], ALU.mult, ALU.mult))
                    modulate(ADA_ROWS, (16, 48))
                    pre_factor(0, 1)
                    post_factor(0, 0)
                    post_factor(0, 1)
                    for s in (2, 3, 0):
                        low_unit(s)
                    v.wait_ge(rowT_full, 1)
                    v.tensor_copy(bcol[:, :, :].rearrange("p c r -> p (c r)"), AT[:, 0, 0:CH * 64]).then_inc(bcol_ready, 1)
                    v.wait_ge(bcol_ready, 2)
                else:
                    B = B_HEADS
                    v.wait_ge(ret_in, 48)
                    kc = krt[:, 0:4 * P].rearrange("p (a l) -> p a l", a=4)
                    for h in range(B):
                        v.tensor_scalar(Dm[:, h, :], kc[:, 0, :], dcy[:, 5, h:h + 1], None, ALU.mult)
                        for d in range(2):
                            ins = v.tensor_scalar(XI[:, d, h, :], kc[:, 2 + d, :], dcy[:, 5, d * B + h:d * B + h + 1],
                                                  None, ALU.mult)
                    link(ins)
                    for h in range(B):
                        v.scalar_tensor_tensor(Dm[:, h, :], kc[:, 1, :], dcy[:, 5, B + h:B + h + 1], Dm[:, h, :],
                                               ALU.mult, ALU.add)
                    for d in range(2):
                        ins = v.tensor_scalar(zcol[:, d, :], dcy[:, 5, d * B:(d + 1) * B], krt[:, 4 * P + d:4 * P + d + 1],
                                              None, ALU.mult)
                    ins.then_inc(ret_arg, 1)
                    v.wait_ge(ret_exp, 3)
                    link(v.tensor_tensor(Dm[:, :, :], Dm[:, :, :], ident.unsqueeze(1).to_broadcast([P, B, P]), ALU.add))

                norm_col = [COL_MLN, COL_RETN][layer]

                def head_tail(tile, hh, col, gates, from_psum, split_next):
                    v.memset(wait_here[:, :], 0.0)
                    for c in range(CH):
                        ins = v.bn_aggr(mv[:, c, :], stats[:, c, :])
                    ins.then_inc(var_ready, 1)
                    v.wait_ge(hstd_ready, hd.now())
                    link(v.reciprocal(hstd[:, :], hstd[:, :]))
                    for c in range(CH):
                        src = ATf[:, c * DV:(c + 1) * DV] if from_psum else hn[:, c, :]
                        ins = v.tensor_scalar(hn[:, c, :], src, mv[:, c, 0:1], hstd[:, c:c + 1], ALU.subtract, ALU.mult)
                    ins.then_inc(hn_ready, 1)
                    if split_next:
                        low_unit(hh)
                    for s in range(2):
                        v.wait_ge(pj_free[s], gates)
                    v.wait_ge(ht_full, hd.now())
                    for vh in range(2):
                        ins = v.scalar_tensor_tensor(
                            hT[:, tile + vh, :] if isinstance(tile, int) else
                            hT[:, ds(tile + vh, 1), :].rearrange("p a t -> p (a t)"),
                            ATf[:, vh * 1024:vh * 1024 + TOK],
                            cols[:, col + vh:col + vh + 1] if isinstance(col, int) else cols[:, ds(col + vh, 1)],
                            gt[:, 2 * hh + vh, :], ALU.mult, ALU.mult)
                    ins.then_inc(h_ready, 1)

                if layer == 0:
                    for h in range(A_HEADS):
                        hh = h % 2
                        hd.add()
                        if hh == 0:
                            pjn.add(18)
                            for s in range(SLOTS):
                                outs[s].add((4, 4, CH, CH)[s])
                            if h > 0:
                                for s in (2, 3, 0):
                                    low_unit(s)
                        v.wait_ge(bc_full, h + 1)
                        for d in range(2):
                            r = 32 * d + h
                            bc = chunks(2 * d)
                            m0 = ATf[:, 1024 * d + TOK:1024 * d + TOK + 1]
                            for c in range(CH):
                                v.scalar_tensor_tensor(W[:, d, c, :], bc[:, c, :], bcol[:, c, r:r + 1],
                                                       mlc[:, d * P:(d + 1) * P], ALU.add, ALU.add)
                            edge = P - 1 if d == 0 else 0
                            v.tensor_copy(bound[:, d, 0, :], bc[:, :, edge])
                            if d == 0:
                                v.tensor_scalar(bound[:, d, 1, 2:CH], bc[:, 1:CH - 1, edge], -1.0, None, ALU.mult)
                                v.tensor_scalar(bound[:, d, 1, 1:2], m0, -1.0, None, ALU.mult)
                                ins = v.memset(bound[:, d, 1, 0:1], 0.0)
                            else:
                                v.tensor_scalar(bound[:, d, 1, 1:CH - 1], bc[:, 2:CH, edge], -1.0, None, ALU.mult)
                                v.tensor_scalar(bound[:, d, 1, CH - 1:CH], m0, -1.0, None, ALU.mult)
                                ins = v.memset(bound[:, d, 1, 0:1], 0.0)
                        link(ins)
                        for d in range(2):
                            r = 32 * d + h
                            v.tensor_tensor(bound[:, d, 2, :], bcol[:, :, r], bound[:, d, 0, :], ALU.add)
                            ins = v.tensor_tensor(bound[:, d, 3, :], bound[:, d, 0, :], bound[:, d, 1, :], ALU.add)
                        ins.then_inc(arg_ready, 1)
                        v.wait_ge(exp_ready, h + 1)
                        v.wait_ge(score_full, h + 1)
                        for d in range(2):
                            ins = v.tensor_tensor(W[:, d, :, :], W[:, d, :, :], chunks(0), ALU.mult)
                        ins.then_inc(p_ready, 1)
                        v.wait_ge(state_in, 64 * (h + 1))
                        if h > 0:
                            v.wait_ge(state_out, 64 * h)
                        for d in range(2):
                            v.wait_ge(ds_full, 2 * h + d + 1)
                            ins = v.tensor_copy(Cout[:, d, :], AT[:, 0, 0:DV + 1])
                            if d == 1:
                                ins.then_inc(out_staged, 1)
                            for n in range(1, 4):
                                c = n if d == 0 else CH - n
                                ins = (v.scalar_tensor_tensor(Cst[:, d, n, :], Cst[:, d, n - 1, :],
                                                            wsdec[:, d, 1, c:c + 1], AT[:, n, 0:DV + 1],
                                                            ALU.mult, ALU.add))
                                if n < 3:
                                    link(ins)
                            ins.then_inc(st_ready, 1)
                        if hh == 0:
                            low_unit(1)
                        for c in range(CH):
                            b = 2 * (c % 2)
                            v.wait_ge(o_full, CH * h + c + 1)
                            den = AT[:, b:b + 2, DV]
                            link(v.scalar_tensor_tensor(dn[:, :], den, -1.0, eqcol[:, c, h:h + 33:32], ALU.mult, ALU.max))
                            link(v.tensor_tensor(dn[:, :], den, dn[:, :], ALU.max))
                            link(v.reciprocal(dn[:, :], dn[:, :]))
                            link(v.tensor_scalar(hn[:, c, :], AT[:, b, 0:DV], dn[:, 0:1], None, ALU.mult))
                            v.scalar_tensor_tensor(hn[:, c, :], AT[:, b + 1, 0:DV], dn[:, 1:2], hn[:, c, :],
                                                   ALU.mult, ALU.add).then_inc(o_free, 1)
                            v.wait_ge(o_free, CH * h + c + 1)
                            ins = v.bn_stats(stats[:, c, :], hn[:, c, :])
                        link(ins)
                        head_tail(2 * h, hh, norm_col + 2 * h, EVACS_BEFORE_ML + 9 * (h // 2) + 8 + hh, False,
                                  h < A_HEADS - 2)
                else:
                    scnt, dcnt, ocnt, gcount, swn = (Tally() for _ in range(5))
                    scnt.n = A_HEADS
                    dcnt.n = 2 * A_HEADS
                    ocnt.n = CH * A_HEADS
                    gcount.n = EVACS_BEFORE_RET
                    sin_n, sout_n = Tally(), Tally()
                    sout_n.n = 64 * A_HEADS

                    def ret_group(g, last):
                        for s in (2, 3):
                            low_unit(s)
                        v.wait_ge(swap_in, swn.add(64))
                        cos = rope[:, 0:SAMPLE].unsqueeze(1).to_broadcast([P, 4, SAMPLE])
                        sin = rope[:, SAMPLE:].unsqueeze(1).to_broadcast([P, 4, SAMPLE])
                        v.tensor_tensor(swapped[:, :, :], swapped[:, :, :], sin, ALU.mult)
                        link(v.tensor_tensor(qk[:, :, PROMPT:TOK], qk[:, :, PROMPT:TOK], cos, ALU.mult))
                        v.tensor_tensor(qk[:, :, PROMPT:TOK], qk[:, :, PROMPT:TOK], swapped[:, :, :],
                                        ALU.add).then_inc(rope_ready, 1)
                        low_unit(0)
                        for hh in range(2):
                            head = g * 2 + hh
                            hd.add()
                            v.wait_ge(score_full, scnt.add())
                            v.tensor_tensor(Pm[:, :, :], chunks(0), Dm[:, ds(head, 1), :].to_broadcast([P, CH, P]),
                                            ALU.mult).then_inc(p_ready, 1)
                            v.wait_ge(ds_full, dcnt.add())
                            v.wait_ge(ret_state_in, sin_n.add(32))
                            v.wait_ge(state_out, sout_n.now())
                            sout_n.add(32)
                            for d in range(2):
                                ins = v.tensor_copy(Sout[:, d, :], ATf[:, d * 1024:d * 1024 + DV])
                            ins.then_inc(out_staged, 1)
                            for n in range(1, 4):
                                for d in range(2):
                                    at = d * 1024 + n * DV
                                    ins = v.scalar_tensor_tensor(Sst[:, d, n, :], Sst[:, d, n - 1, :],
                                                                 cdcol[:, d, ds(head, 1)],
                                                                 ATf[:, at:at + DV], ALU.mult, ALU.add)
                                if n < 3:
                                    link(ins)
                            ins.then_inc(st_ready, 1)
                            if hh == 0:
                                low_unit(1)
                            v.wait_ge(o_full, ocnt.add())
                            for c in range(CH):
                                ins = v.bn_stats(stats[:, c, :], ATf[:, c * DV:(c + 1) * DV])
                            link(ins)
                            gcount.add(8 if hh == 0 else 1)
                            head_tail(g * 4 + 2 * hh, hh, g * 4 + (norm_col + 2 * hh), gcount.now(), True, not last)

                    with loop(v, GROUPS[1] - 1, own=(own, 9), hd=(hd, 2), sc=(scnt, 2), dc=(dcnt, 2), oc=(ocnt, 2),
                              gc=(gcount, 9), sw=(swn, 64), si=(sin_n, 64), so=(sout_n, 64), h0=(highs[0], 3),
                              h1=(highs[1], 3)) as g:
                        ret_group(g, False)
                    ret_group(GROUPS[1] - 1, True)
                    pjn.add(18 * GROUPS[1])
                    for s in range(SLOTS):
                        outs[s].add(GROUPS[1] * (4, 4, CH, CH)[s])
                if layer == 0:
                    y_copies(2, [0, 0, 1, 1], (2, 2, 0, 0))
                else:
                    y_copies(2, [0, 1, 2, 3], (1, 1, 1, 1))
                norm_rstd()
                v.wait_ge(x_back, 16 * (layer + 1))
                scale_tiles(uT, post_a[:, 0], y_scaled)
                modulate(ADA_LATER[layer, 1][0], ((0, 8), (32, 40))[layer])
                if layer == 1:
                    pre_factor(1, 1)
                norm_rstd()
                scale_tiles(xT, pre_a[:, 1], scaled_ready)
                split_input(2 * layer + 1, low_weights)
                modulate(ADA_LATER[layer, 1][1], ((8, 16), (40, 48))[layer])
                if layer == 1:
                    post_factor(1, 1)

                def taps(t, b):
                    s = pjn.n % 2
                    pjn.add()
                    v.wait_ge(conv_begun, cvn.add())
                    pieces = ((0, 0, 1, PROMPT), (0, PROMPT, (HALF - PROMPT) // GRID_W, GRID_W),
                              (1, 0, HALF // GRID_W, GRID_W))
                    for tap in (0, 2):
                        scalar = cols[:, ds(t + (COL_CONV + (layer * 3 + tap) * 2 * FT + b * FT), 1)]
                        for bank, lo, n, w in pieces:
                            z = PJ[:, s, bank, lo:lo + n * w].rearrange("p (r w) -> p r w", w=w)
                            o = conv[:, b, bank * HALF + lo:bank * HALF + lo + n * w].rearrange("p (r w) -> p r w", w=w)
                            o, z = (o[:, :, 1:w], z[:, :, 0:w - 1]) if tap == 0 else (o[:, :, 0:w - 1], z[:, :, 1:w])
                            ins = v.scalar_tensor_tensor(o, z, scalar, o, ALU.mult, ALU.add)
                        if tap == 0:
                            link(ins)
                    ins.then_inc(pj_free[s], 1)
                    free[s].add()
                    return s

                def up_pair(t, tile, slot):
                    taps(t, 0)
                    s = taps(t, 1)
                    v.wait_ge(pj_free[s], free[s].now())
                    v.wait_ge(gelu_ready, gen.add())
                    v.tensor_tensor(conv[:, 1, :], conv[:, 0, :], conv[:, 1, :], ALU.mult).then_inc(prod_ready, 1)
                    low_weights(slot)
                    v.wait_ge(acth_ready, gen.now())
                    at = ds(tile, 1)
                    v.tensor_tensor(act_low[:, at, :], conv[:, 1:2, :], act_high[:, at, :].bitcast(F32), ALU.subtract
                                    ).then_inc(act_ready, 1)

                def down_tile(m, slot, half):
                    s = pj(slot)
                    y = uT[:, ds(m, 1), :].rearrange("p a (b t) -> p (a b) t", b=2)
                    if half == 0:
                        v.tensor_copy(y, PJ[:, s, :, 0:HALF]).then_inc(pj_free[s], 1)
                    else:
                        v.tensor_tensor(y, PJ[:, s, :, 0:HALF], y, ALU.add).then_inc(pj_free[s], 1)

                free[0].n = free[1].n = pjn.n // 2
                assert pjn.n % 2 == 0
                v.wait_ge(state_out, 64 * A_HEADS + layer * 32 * B_HEADS)
                for kind, turns, first in FFN:
                    if kind == "up":
                        for s in range(2):
                            outs[s].add(2 * turns)
                        with loop(v, turns, own=(own, 4), pjn=(pjn, 4), cv=(cvn, 4), ge=(gen, 2), f0=(free[0], 2),
                                  f1=(free[1], 2), h0=(highs[0], 1), h1=(highs[1], 1)) as i:
                            for j in range(2):
                                up_pair(i * 2 + (first + j), i * 2 + j, j)
                    else:
                        last = first > 0
                        with loop(v, turns - last, pjn=(pjn, 2), o0=(outs[0], 1), o1=(outs[1], 1), h0=(highs[0], 1),
                                  h1=(highs[1], 1)) as i:
                            for j in range(2):
                                down_tile(i * 2 + j, j, last)
                                low_weights(j)
                        if last:
                            for j in range(2):
                                down_tile(KT - 2 + j, j, last)
                        for s in range(2):
                            free[s].n = pjn.n // 2
                norm_rstd()
                scale_tiles(uT, post_a[:, 1], y_scaled)
                if layer == 0:
                    for s in (2, 3):
                        outs[s].add(8)

            for c in range(OUT_BY_SCALAR, CH):
                v.wait_ge(turned, turnn.n + CH + c + 1)
                v.tensor_copy(xin[:, c, 4 * P:], out_bank[c]).then_inc(out_by_vector, 1)

        @block.tensor
        def _(pe):
            full = [Tally() for _ in range(SLOTS)]
            pjn, free = Tally(), [Tally(), Tally()]
            stn, hrn, rown, splits = Tally(), Tally(), Tally(), [Tally(), Tally()]
            scn, stc, qzn, hnn, ron = (Tally() for _ in range(5))

            def per(*uses):
                return {f"s{s}": (full[s], n) for s, n in enumerate(uses)}

            def unit(slot, dmas=1):
                full[slot].add(dmas)
                pe.wait_ge(ring_full[slot], full[slot].now() * 16)

            def emptied():
                for s in range(2):
                    pe.wait_ge(pj_free[s], free[s].now())

            def pj_slot():
                s = pjn.n % 2
                pjn.add()
                pe.wait_ge(pj_free[s], free[s].now())
                free[s].add()
                return s

            def norm_stat():
                pe.wait_ge(sq_added, 8 * stn.now() + 8)
                stn.add()
                for c in range(CH):
                    ins = pe.matmul(mean_sq[:, c:c + 1], sqsum[:, c * P:(c + 1) * P], mean_w, start=True, stop=True)
                ins.then_inc(stat_full, 1)

            def norm_rstd():
                pe.wait_ge(diag_ready, stn.now())
                d = diag[:, :, :].rearrange("p c t -> p (c t)")
                pe.matmul(rstd[:, 0:512], ones, d[:, 0:512], start=True, stop=True)
                pe.matmul(rstd[:, 512:TOK], ones, d[:, 512:TOK], start=True, stop=True).then_inc(rstd_full, 1)

            pe.wait_ge(const_in, 16)
            pe.wait_ge(rows_in, 160)
            s = pj_slot()
            for n in range(5):
                ins = pe.transpose(PJ[:, s, n // 4, (n % 4) * P:(n % 4 + 1) * P], rows[:, n, :], ident)
            ins.then_inc(turned, 1)

            def ada(part):
                layer, first, slots, turns = part
                n = len(slots)
                with loop(pe, turns, **per(*[int(s in slots) for s in range(SLOTS)]), row=(rown, n)) as i:
                    for j, slot in enumerate(slots):
                        unit(slot)
                        w = ring[slot][:, :].rearrange("p (k m) -> p k m", k=KT)
                        for k in range(KT):
                            ins = pe.matmul(PJ[0:2, j // 2, j % 2, 0:256], silu_c[:, k, :], w[:, k, :],
                                            start=(k == 0), stop=(k == KT - 1))
                        ins.then_inc(made[slot], 1)
                    pe.wait_ge(ada_row, rown.add(n))
                    for m in range(2 * n):
                        ins = pe.matmul(AT[:, 0, ds(i * (4 * n) + (4 * first + 2 * m), 2)],
                                        ada_rows[:, m // 2, (m % 2) * P:(m % 2 + 1) * P],
                                        ident[0:2, 0:2], start=True, stop=True)
                    ins.then_inc(ada_done, 1)

            def project_split(weights_high, weights_low, kts, at, step, high, low, s, source_ready=None):
                for k in range(kts):
                    if source_ready:
                        split, before = source_ready
                        pe.wait_ge(split, before + k + 1)
                    for n, (w, x) in enumerate(((weights_high, high), (weights_high, low), (weights_low, high))):
                        for b in range(2):
                            ins = pe.matmul(PJ[:, s, b, 0:HALF], w[:, at + k * step:at + k * step + P],
                                            x[:, k, b * HALF:(b + 1) * HALF],
                                            start=(k == 0 and n == 0), stop=(k == kts - 1 and n == 2))
                return ins

            def ada_later(part):
                pe.wait_ge(mod_ready, modn.add())
                ada(part)

            pe.wait_ge(silu_ready, 2)
            emptied()
            ada(ADA_FIRST)
            pe.wait_ge(x_in, 32)
            for c in range(CH):
                s = pj_slot()
                for k in range(KT):
                    ins = pe.transpose(PJ[:, s, k // 4, (k % 4) * P:(k % 4 + 1) * P], xin[:, c, k * P:(k + 1) * P], ident)
                ins.then_inc(turned, 1)

            modn = Tally()
            modn.n = 1
            for layer in range(DEPTH):
                if layer == 0:
                    emptied()
                    ada(ADA_START)
                if layer == 1:
                    ada_later(ADA_LATER[1, 0][0])
                norm_stat()
                norm_rstd()
                if layer == 0:
                    pe.wait_ge(mod_ready, 1)
                    ada(ADA_NORM)
                else:
                    ada_later(ADA_LATER[1, 0][1])
                if layer == 0:
                    pe.wait_ge(u_ready, KT)
                    pe.wait_ge(ml_in, 16 * 11)
                    for kind in range(2):
                        s = pj_slot()
                        for k in range(KT):
                            for b in range(2):
                                ins = pe.matmul(PJ[0:64, s, b, 0:HALF], wg[:, k, kind, :],
                                                uT[:, k, b * HALF:(b + 1) * HALF], start=(k == 0), stop=(k == KT - 1))
                        ins.then_inc(turned, 1)
                    emptied()
                    ada(ADA_ROWS)

                def turn_gate_rows():
                    pe.wait_ge(rowb_ready, 1)
                    pe.wait_ge(mod_ready, 2)
                    for n, row in enumerate((ri, rf)):
                        for c in range(CH):
                            ins = pe.transpose(AT[:, n, c * 64:(c + 1) * 64], row[:, c * P:(c + 1) * P], ident[0:64, 0:64])
                    ins.then_inc(rowT_full, 1)
                    pe.wait_ge(bcol_ready, 2)

                def split_unit(slot):
                    full[slot].add()
                    pe.wait_ge(l_split[slot % 2], splits[slot % 2].add())

                def project_unit(slot, m, source_ready=None):
                    s = pj_slot()
                    project_split(w_high[slot % 2], ring_low[slot], KT, m * P, 256, u_high, u_low, s,
                                  source_ready).then_inc(made[slot], 1)

                def gate(t):
                    if t % 2 == 0:
                        split_unit(t // 2)
                    project_unit(t // 2, t % 2)

                def q_tile(m, source_ready=None):
                    if m == 0:
                        split_unit(0)
                    project_unit(0, m, source_ready)

                def kv():
                    split_unit(1)
                    for m in range(2):
                        project_unit(1, m)
                    for hh in range(2):
                        split_unit(2 + hh)
                        for c in range(CH):
                            s = pj_slot()
                            for k in range(KT):
                                for n, (x, w) in enumerate(((u_high, w_high[hh]), (u_high, ring_low[2 + hh]),
                                                            (u_low, w_high[hh]))):
                                    ins = pe.matmul(PJ[:, s, 0, 0:DV], x[:, k, c * P:(c + 1) * P],
                                                    w[:, k * DV:(k + 1) * DV], start=(k == 0 and n == 0),
                                                    stop=(k == KT - 1 and n == 2))
                            ins.then_inc(made[2 + hh], 1)

                def scores(hh):
                    for c in range(CH):
                        pe.matmul(chunks(0)[:, c, :], qk[:, 2 + hh, c * P:(c + 1) * P], qk[:, hh, c * P:(c + 1) * P],
                                  start=True, stop=True)
                    for c in range(CH):
                        ins = pe.transpose(chunks(2)[:, c, :], qk[:, 2 + hh, c * P:(c + 1) * P], ident)
                    ins.then_inc(score_full, 1)

                def turn_back():
                    pe.wait_ge(hn_ready, hnn.add())
                    for vh in range(2):
                        for c in range(CH):
                            ins = pe.transpose(chunks(2 * vh)[:, c, :], hn[:, c, vh * P:(vh + 1) * P], ident)
                    ins.then_inc(ht_full, 1)

                out_units, out_tiles, out_kts = OUT_UNITS[layer], OUT_TILES[layer], HV[layer] // P
                out_slots = {}

                def out_product(j, m, k, s):
                    for b in range(2):
                        at = (k * out_tiles + m) * P
                        ins = pe.matmul(PJ[:, s, b, 0:HALF], ring[j][:, at:at + P], hT[:, k, b * HALF:(b + 1) * HALF],
                                        start=(k == 0), stop=(k == out_kts - 1))
                    return ins

                def out_ahead(*products):
                    for m, ks in products:
                        if m not in out_slots:
                            if m == 0:
                                unit(0)
                            out_slots[m] = pj_slot()
                        for k in ks:
                            out_product(0, m, k, out_slots[m])

                q_tile(0, (ul_ready, 2 * layer * KT))
                q_tile(1)
                if layer == 0:
                    for g in range(GROUPS[0]):
                        last = g == GROUPS[0] - 1
                        kv()
                        if g == 0:
                            turn_gate_rows()
                        for hh in range(2):
                            h = 2 * g + hh
                            pe.wait_ge(h_ready, h)
                            for d in range(2):
                                sel = mlc[0:64, (2 + 4 * d + h) * P:(3 + 4 * d + h) * P]
                                pe.matmul(ATf[:, 1024 * d:1024 * d + 512], sel, rM[:, 0:512], start=True, stop=True)
                                ins = pe.matmul(ATf[:, 1024 * d + 512:1024 * d + TOK + 1], sel, rM[:, 512:TOK + 1],
                                                start=True, stop=True)
                            ins.then_inc(bc_full, 1)
                            gate(3 * hh)
                            pe.wait_ge(exp_ready, h + 1)
                            scores(hh)
                            if hh == 0:
                                gate(1)
                            elif not last:
                                q_tile(0)
                            else:
                                out_ahead((0, (0, 1, 2)))
                            pe.wait_ge(p_ready, h + 1)
                            pe.wait_ge(kz_ready, h + 1)
                            pe.wait_ge(ml_zero, 5)
                            for d in range(2):
                                if d == 1 and hh == 1 and last:
                                    out_ahead((0, (3, 4)))
                                pe.wait_ge(st_ready, 2 * h + d)
                                for n in range(4):
                                    c = n if d == 0 or n == 0 else CH - n
                                    ins = pe.matmul(AT[:, n, 0:DV + 1], kz[d][:, c, :], vt[:, c, hh, :], start=True, stop=True)
                                ins.then_inc(ds_full, 1)
                            if hh == 1 and last:
                                out_ahead((0, (5,)), (1, (0,)))
                            pe.wait_ge(st_ready, 2 * h + 2)
                            pe.wait_ge(qz_ready, 2 * h + 2)
                            for c in range(CH):
                                if c >= 2:
                                    pe.wait_ge(o_free, CH * h + c - 1)
                                for d in range(2):
                                    o = AT[:, 2 * (c % 2) + d, 0:DV + 1]
                                    ins = pe.matmul(o, W[:, d, c, :], vt[:, c, hh, :], start=True, stop=(c == 0))
                                    if c:
                                        ins = pe.matmul(o, qz[d][:, c - 1, :], Cst[:, d, c - 1 if d == 0 else CH - 1 - c, :],
                                                        start=False, stop=True)
                                ins.then_inc(o_full, 1)
                            if hh == 0:
                                gate(2)
                            elif not last:
                                q_tile(1)
                            else:
                                out_ahead((1, (1, 2, 3, 4, 5)))
                            turn_back()
                else:
                    hrn.n = scn.n = A_HEADS
                    stc.n, qzn.n = 2 * A_HEADS, 2 * A_HEADS
                    pe.wait_ge(ml_zero, 6)

                    def ret_group(last):
                        kv()
                        pe.wait_ge(rope_ready, ron.add())
                        for hh in range(2):
                            pe.wait_ge(h_ready, hrn.now())
                            hrn.add()
                            scores(hh)
                            gate(0 if hh == 0 else 3)
                            pe.wait_ge(p_ready, scn.add())
                            pe.wait_ge(kz_ready, scn.now())
                            for d in range(2):
                                for n in range(4):
                                    c = n if d == 0 or n == 0 else CH - n
                                    at = d * 1024 + n * DV
                                    ins = pe.matmul(ATf[:, at:at + DV], kz[d][:, c, :], vt[:, c, hh, 0:DV],
                                                    start=True, stop=True)
                            ins.then_inc(ds_full, 1)
                            if hh == 0:
                                gate(1)
                            elif not last:
                                q_tile(0)
                            else:
                                out_ahead((0, range(4)))
                            pe.wait_ge(st_ready, stc.add())
                            pe.wait_ge(qz_ready, qzn.add(2))
                            for c in range(CH):
                                o = ATf[:, c * DV:(c + 1) * DV]
                                ins = pe.matmul(o, Pm[:, c, :], vt[:, c, hh, 0:DV], start=True, stop=(c == 0))
                                if c:
                                    for d in range(2):
                                        ins = pe.matmul(o, qz[d][:, c - 1, :], Sst[:, d, c - 1 if d == 0 else CH - 1 - c, :],
                                                        start=False, stop=(d == 1))
                            ins.then_inc(o_full, 1)
                            if hh == 0:
                                gate(2)
                            elif not last:
                                q_tile(1)
                            else:
                                out_ahead((0, range(4, 10)))
                            turn_back()

                    with loop(pe, GROUPS[1] - 1, pjn=(pjn, 18), f0=(free[0], 9), f1=(free[1], 9), h=(hrn, 2), sc=(scn, 2),
                              st=(stc, 2), qz=(qzn, 4), hn=(hnn, 2), ro=(ron, 1), sp0=(splits[0], 3), sp1=(splits[1], 3),
                              **per(2, 2, 1, 1)):
                        ret_group(False)
                    ret_group(True)
                    out_ahead((0, range(10, 14)))
                pe.wait_ge(h_ready, [A_HEADS, A_HEADS + B_HEADS][layer])

                for turn in range(2):
                    for j in range(out_units):
                        first = turn == 0 and j == 0
                        if not first:
                            unit(j)
                        for m in range(out_tiles):
                            s = out_slots[m] if first else pj_slot()
                            for k in range(out_kts - 2 if first else 0, out_kts):
                                ins = out_product(j, m, k, s)
                            ins.then_inc(made[j], 1)
                norm_stat()
                norm_rstd()
                ada_later(ADA_LATER[layer, 1][0])
                norm_stat()
                norm_rstd()
                ada_later(ADA_LATER[layer, 1][1])

                for kind, turns, first in FFN:
                    out_per = 2 if kind == "up" else 1

                    def ffn_turn(source_ready=None):
                        for j in range(2):
                            pe.wait_ge(l_split[j], splits[j].add())
                            for b in range(out_per):
                                s = pj_slot()
                                if kind == "up":
                                    ins = project_split(w_high[j], w_low[j], KT, b * KT * P, P, u_high, u_low, s, source_ready)
                                else:
                                    ins = project_split(w_high[j], w_low[j], HALVES[int(first > 0)], 0, P, act_high, act_low, s,
                                                        source_ready)
                                source_ready = None
                                ins.then_inc(made[j], 1)

                    if kind == "down":
                        ffn_turn((act_ready, FT * layer + first))
                    elif first == 0:
                        ffn_turn((ul_ready, KT * (2 * layer + 1)))
                    with loop(pe, turns - (kind == "down" or first == 0), pjn=(pjn, 2 * out_per), f0=(free[0], out_per),
                              f1=(free[1], out_per), sp0=(splits[0], 1), sp1=(splits[1], 1)):
                        ffn_turn()
                for s in range(2):
                    full[s].add(2 * (FT + KT * 2) // 2)
                norm_stat()
                norm_rstd()

            emptied()
            for k in range(KT):
                pe.wait_ge(x_added, 3 * KT + k + 1)
                for c in range(CH):
                    if k == KT // 2:
                        pe.wait_ge(out_by_scalar, c + 1)
                    ins = pe.transpose(out_bank[c][:, (k % 4) * P:(k % 4 + 1) * P], xT[:, k, c * P:(c + 1) * P], ident)
                    if k % 4 == 3:
                        ins.then_inc(turned, 1)


_INS = ['x_prompt', 'x_sample', 'state_mlstm_C', 'state_mlstm_n', 'state_mlstm_m', 'state_ret_S', 'c', 'c_ctx',
        'norm_gain', 'ada_w', 'ada_b', 'ml_w_in', 'ml_b_gate', 'ml_norm', 'ml_w_out', 'ret_w_in', 'ret_decay',
        'ret_norm', 'ret_w_out', 'ffn_w_up', 'ffn_conv', 'ffn_conv_b', 'ffn_w_down']
_OUTS = [(1, PROMPT, D_MODEL), (1, SAMPLE, D_MODEL), (1, 1, 2, A_HEADS, DK, DV), (1, 1, 2, A_HEADS, DK),
         (1, 1, 2, A_HEADS), (1, 1, 2, B_HEADS, DK, DV)]


def shape_constants():
    one = np.arange(P)
    common = np.concatenate([np.eye(P), np.full((P, P), 1.0 / D_MODEL), np.ones((P, P))], axis=1)
    s, l = one[:, None], one[None, :]
    ml = np.zeros((P, 10 * P))
    ml[:, 0:P] = np.where(s <= l, 0.0, MASKED)
    ml[:, P:2 * P] = np.where(s >= l, 0.0, MASKED)
    for d in range(2):
        for h in range(A_HEADS):
            at = (2 + 4 * d + h) * P
            ml[32 * d + h, at:at + P] = -1.0
    ret = np.zeros((P, TOK + 2 * SAMPLE))
    ret[:, 0:P] = np.maximum(l - s, 0)
    ret[:, P:2 * P] = np.maximum(s - l, 0)
    ret[:, 2 * P:3 * P] = l + 1
    ret[:, 3 * P:4 * P] = P - l
    ret[:, 4 * P] = P - 1 - one
    ret[:, 4 * P + 1] = one
    quarter = DK // 4
    inv = (10000.0 ** (-np.arange(quarter, dtype=np.float32) / quarter)).astype(np.float32)
    t = np.arange(SAMPLE)
    for half, pos in enumerate((t // GRID_W, t % GRID_W)):
        ang = (pos.astype(np.float32)[None, :] * inv[:, None]).astype(np.float32).astype(np.float64)
        for part, sign in enumerate((-1.0, 1.0)):
            r = half * 2 * quarter + part * quarter
            ret[r:r + quarter, TOK:TOK + SAMPLE] = np.cos(ang)
            ret[r:r + quarter, TOK + SAMPLE:] = sign * np.sin(ang)
    return {n: a.astype(np.float32) for n, a in (("common", common), ("ml", ml), ("ret", ret))}


def kernel(**inputs):
    import concourse.bacc as bacc
    from concourse.bass_utils import run_bass_kernel_spmd

    nc = bacc.Bacc("TRN2", target_bir_lowering=False, num_devices=1)
    given = {name: np.ascontiguousarray(inputs[name]) for name in _INS}
    arrays, args = {}, []
    for name, a in {**given, **{"k_" + n: a for n, a in shape_constants().items()}}.items():
        arrays[f"in_{name}"] = a
        args.append(nc.dram_tensor(f"in_{name}", a.shape, mybir.dt.from_np(a.dtype), kind="ExternalInput").ap())
    for i, shape in enumerate(_OUTS):
        args.append(nc.dram_tensor(f"out_{i}", shape, F32, kind="ExternalOutput").ap())
    args.append(nc.dram_tensor("x_saved_dram", (P, KT, TOK), F32, kind="Internal").ap())
    hybrid_step(nc, *args)
    r = run_bass_kernel_spmd(nc, [arrays], core_ids=[0])
    return tuple(r.results[0][f"out_{i}"] for i in range(len(_OUTS)))
```
